# Optimizing a Trainium2 kernel written in Bass

```python
import jax
import jax.numpy as jnp
from jax import lax
import numpy as np

D_MODEL = 1024
BATCH = 1
SEQ = 1024
DEPTH = 1
DEC_BATCH = 1
DEC_SEQ = 64
PAST_LEN = 128

CHUNK = 64
EPS = 1e-6
A_HEADS = 8
A_HEAD_DIM = 64
A_WIDTH = A_HEADS * A_HEAD_DIM
BAND_CHUNKS = 8
BAND_PAST = BAND_CHUNKS * CHUNK
BAND_LEN = BAND_PAST + CHUNK
REL_CLIP = 128
MASK_VALUE = -1e30
R_HEADS = 4
R_KEY_DIM = 128
R_VAL_DIM = 128
R_QK_WIDTH = R_HEADS * R_KEY_DIM
R_V_WIDTH = R_HEADS * R_VAL_DIM
ROPE_BASE = 10000.0
P_HEADS = 8
P_KEYS = 128
P_EXPERTS = P_KEYS * P_KEYS
P_QUERY_DIM = 256
P_HALF = P_QUERY_DIM // 2
P_TOPK = 16
P_TOKEN_BLOCK = 128
IN_SIZES = (A_WIDTH, A_WIDTH, A_WIDTH, R_QK_WIDTH, R_QK_WIDTH, R_V_WIDTH, R_V_WIDTH, D_MODEL, D_MODEL)
IN_WIDTH = sum(IN_SIZES)

kernel_name = "streaming_band_attn_retention_peer"

def rms_norm(x, g):
    xf = x.astype(jnp.float32)
    y = xf * lax.rsqrt(jnp.mean(xf * xf, axis=-1, keepdims=True) + EPS)
    return (y * g.astype(jnp.float32)).astype(x.dtype)

def rotary(x, pos):
    half = x.shape[-1] // 2
    inv = ROPE_BASE ** (-jnp.arange(half, dtype=jnp.float32) / half)
    ang = pos.astype(jnp.float32)[:, None] * inv[None, :]
    cos = jnp.cos(ang)[None, :, None, :]
    sin = jnp.sin(ang)[None, :, None, :]
    xf = x.astype(jnp.float32)
    x1, x2 = xf[..., :half], xf[..., half:]
    return jnp.concatenate([x1 * cos - x2 * sin, x1 * sin + x2 * cos], axis=-1).astype(x.dtype)

def mixer_inputs(h, pos, w_in, q_norm_g, k_norm_g):
    B, T, _ = h.shape
    z = h @ w_in
    offs = [int(o) for o in np.cumsum(IN_SIZES)[:-1]]
    qa, ka, va, qr, kr, vr, gr, gate_a, gate_r = jnp.split(z, offs, axis=-1)
    qa = rms_norm(qa.reshape(B, T, A_HEADS, A_HEAD_DIM), q_norm_g)
    ka = rms_norm(ka.reshape(B, T, A_HEADS, A_HEAD_DIM), k_norm_g)
    va = va.reshape(B, T, A_HEADS, A_HEAD_DIM)
    qr = rotary(qr.reshape(B, T, R_HEADS, R_KEY_DIM), pos)
    kr = rotary(kr.reshape(B, T, R_HEADS, R_KEY_DIM), pos) * (R_KEY_DIM ** -0.5)
    vr = vr.reshape(B, T, R_HEADS, R_VAL_DIM)
    return qa, ka, va, qr, kr, vr, gr, gate_a, gate_r

def band_attention(q, k, v, qpos, kpos, kvalid, rel_bias):
    s = jnp.einsum('bqhd,bkhd->bhqk', q, k).astype(jnp.float32) * (A_HEAD_DIM ** -0.5)
    rel = jnp.clip(qpos[:, None] - kpos[None, :], -REL_CLIP, REL_CLIP) + REL_CLIP
    s = s + rel_bias.astype(jnp.float32)[:, rel]
    s = jnp.where(kvalid[None, None, None, :], s, MASK_VALUE)
    p = jax.nn.softmax(s, axis=-1).astype(v.dtype)
    return jnp.einsum('bhqk,bkhd->bqhd', p, v)

def attention_prompt(q, k, v, rel_bias):
    B, S, H, Dh = q.shape
    nc = S // CHUNK
    kp = jnp.pad(k, ((0, 0), (BAND_PAST, 0), (0, 0), (0, 0)))
    vp = jnp.pad(v, ((0, 0), (BAND_PAST, 0), (0, 0), (0, 0)))
    qc = q.reshape(B, nc, CHUNK, H, Dh).swapaxes(0, 1)
    local_q = jnp.arange(CHUNK)
    local_k = jnp.arange(BAND_LEN) - BAND_PAST

    def one_chunk(args):
        c, qb = args
        start = c * CHUNK
        kb = lax.dynamic_slice_in_dim(kp, start, BAND_LEN, axis=1)
        vb = lax.dynamic_slice_in_dim(vp, start, BAND_LEN, axis=1)
        kvalid = (start + local_k) >= 0
        return band_attention(qb, kb, vb, local_q, local_k, kvalid, rel_bias)

    out = lax.map(one_chunk, (jnp.arange(nc), qc))
    return out.swapaxes(0, 1).reshape(B, S, H, Dh)

def retention_block(q, k, v, state):
    L = q.shape[1]
    dt = q.dtype
    log_gamma = jnp.log1p(-(2.0 ** (-5.0 - jnp.arange(R_HEADS, dtype=jnp.float32))))
    idx = jnp.arange(L, dtype=jnp.float32)
    diff = idx[:, None] - idx[None, :]
    decay = jnp.where(diff >= 0, jnp.exp(log_gamma[:, None, None] * jnp.maximum(diff, 0.0)), 0.0)
    inner = jnp.einsum('blhd,bmhd->bhlm', q, k) * decay.astype(dt)[None]
    o = jnp.einsum('bhlm,bmhe->blhe', inner, v)
    q_decay = jnp.exp(log_gamma[None, :] * (idx[:, None] + 1.0)).astype(dt)
    o = o + jnp.einsum('blhd,bhde->blhe', q, state) * q_decay[None, :, :, None]
    k_decay = jnp.exp(log_gamma[None, :] * (L - 1.0 - idx)[:, None]).astype(dt)
    state_decay = jnp.exp(log_gamma * L).astype(dt)
    new_state = state * state_decay[None, :, None, None] + jnp.einsum('blhd,lh,blhe->bhde', k, k_decay, v)
    return o, new_state

def retention_prompt(q, k, v):
    B, S, H, dk = q.shape
    nc = S // CHUNK

    def to_chunks(a):
        return a.reshape(B, nc, CHUNK, H, a.shape[-1]).swapaxes(0, 1)

    s0 = jnp.zeros((B, H, dk, v.shape[-1]), q.dtype)

    def step(s, qkv):
        o, s_new = retention_block(qkv[0], qkv[1], qkv[2], s)
        return s_new, o

    s_fin, o = lax.scan(step, s0, (to_chunks(q), to_chunks(k), to_chunks(v)))
    return o.swapaxes(0, 1).reshape(B, S, H, v.shape[-1]), s_fin

def peer(h, w_query, sub_keys, expert_u, expert_v):
    n = h.shape[0]
    nb = -(-n // P_TOKEN_BLOCK)
    hp = jnp.pad(h, ((0, nb * P_TOKEN_BLOCK - n), (0, 0))).reshape(nb, P_TOKEN_BLOCK, D_MODEL)

    def one_block(hb):
        t = hb.shape[0]
        qry = (hb @ w_query).reshape(t, P_HEADS, 2, P_HALF)
        s = jnp.einsum('thcd,hckd->thck', qry, sub_keys).astype(jnp.float32)
        top_s, top_i = lax.top_k(s, P_TOPK)
        cand_s = (top_s[:, :, 0, :, None] + top_s[:, :, 1, None, :]).reshape(t, P_HEADS, P_TOPK * P_TOPK)
        cand_i = (top_i[:, :, 0, :, None] * P_KEYS + top_i[:, :, 1, None, :]).reshape(t, P_HEADS, P_TOPK * P_TOPK)
        best_s, best_pos = lax.top_k(cand_s, P_TOPK)
        expert = jnp.take_along_axis(cand_i, best_pos, axis=-1)
        gate = jax.nn.softmax(best_s, axis=-1)
        a = jnp.einsum('td,thkd->thk', hb, expert_u[expert]).astype(jnp.float32)
        act = (jax.nn.gelu(a, approximate=False) * gate).astype(hb.dtype)
        return jnp.einsum('thk,thkd->td', act, expert_v[expert])

    out = lax.map(one_block, hp)
    return out.reshape(nb * P_TOKEN_BLOCK, D_MODEL)[:n]

def layer_forward(x, pos, attend, retain, p):
    (mix_g, w_in, q_g, k_g, rel_b, r_g, w_ba, w_br, w_o, ffn_g, w_q, s_keys, e_u, e_v) = p
    B, T, _ = x.shape
    h = rms_norm(x, mix_g)
    qa, ka, va, qr, kr, vr, gr, gate_a, gate_r = mixer_inputs(h, pos, w_in, q_g, k_g)
    oa, k_new, v_new = attend(qa, ka, va, rel_b)
    orr, s_new = retain(qr, kr, vr)
    branch_a = oa.reshape(B, T, A_WIDTH) @ w_ba
    branch_r = (rms_norm(orr, r_g).reshape(B, T, R_V_WIDTH) * jax.nn.silu(gr)) @ w_br
    merged = jax.nn.sigmoid(gate_a) * branch_a + jax.nn.sigmoid(gate_r) * branch_r
    x = x + merged @ w_o
    h2 = rms_norm(x, ffn_g).reshape(B * T, D_MODEL)
    x = x + peer(h2, w_q, s_keys, e_u, e_v).reshape(B, T, D_MODEL)
    return x, k_new, v_new, s_new

def setup_inputs(seed: int = 0) -> dict:
    key = jax.random.key(seed)
    ks = jax.random.split(key, 20)
    f32 = jnp.float32

    def nrm(k, shape, scale):
        return jax.random.normal(k, shape, f32) * scale

    rows = min(BAND_PAST, PAST_LEN)
    return {
        "x_prompt": nrm(ks[0], (BATCH, SEQ, D_MODEL), 1.0),
        "x_sample": nrm(ks[1], (DEC_BATCH, DEC_SEQ, D_MODEL), 1.0),
        "cache_attn_k": nrm(ks[2], (DEPTH, DEC_BATCH, rows, A_HEADS, A_HEAD_DIM), 1.0),
        "cache_attn_v": nrm(ks[3], (DEPTH, DEC_BATCH, rows, A_HEADS, A_HEAD_DIM), 1.0),
        "state_retention": nrm(ks[4], (DEPTH, DEC_BATCH, R_HEADS, R_KEY_DIM, R_VAL_DIM), 0.5),
        "mix_norm_g": 1.0 + nrm(ks[5], (DEPTH, D_MODEL), 0.02),
        "w_in": nrm(ks[6], (DEPTH, D_MODEL, IN_WIDTH), D_MODEL ** -0.5),
        "attn_q_norm_g": 1.0 + nrm(ks[7], (DEPTH, A_HEAD_DIM), 0.02),
        "attn_k_norm_g": 1.0 + nrm(ks[8], (DEPTH, A_HEAD_DIM), 0.02),
        "attn_rel_bias": nrm(ks[9], (DEPTH, A_HEADS, 2 * REL_CLIP + 1), 0.1),
        "ret_out_norm_g": 1.0 + nrm(ks[10], (DEPTH, R_HEADS, R_VAL_DIM), 0.02),
        "w_branch_attn": nrm(ks[11], (DEPTH, A_WIDTH, D_MODEL), A_WIDTH ** -0.5),
        "w_branch_ret": nrm(ks[12], (DEPTH, R_V_WIDTH, D_MODEL), R_V_WIDTH ** -0.5),
        "w_out": nrm(ks[13], (DEPTH, D_MODEL, D_MODEL), D_MODEL ** -0.5),
        "ffn_norm_g": 1.0 + nrm(ks[14], (DEPTH, D_MODEL), 0.02),
        "peer_w_query": nrm(ks[15], (DEPTH, D_MODEL, P_HEADS * P_QUERY_DIM), D_MODEL ** -0.5),
        "peer_sub_keys": nrm(ks[16], (DEPTH, P_HEADS, 2, P_KEYS, P_HALF), P_HALF ** -0.5),
        "peer_expert_u": nrm(ks[17], (DEPTH, P_EXPERTS, D_MODEL), D_MODEL ** -0.5),
        "peer_expert_v": nrm(ks[18], (DEPTH, P_EXPERTS, D_MODEL), P_HEADS ** -0.5),
    }

def reference(x_prompt, x_sample, cache_attn_k, cache_attn_v, state_retention,
              mix_norm_g, w_in, attn_q_norm_g, attn_k_norm_g, attn_rel_bias, ret_out_norm_g,
              w_branch_attn, w_branch_ret, w_out, ffn_norm_g, peer_w_query, peer_sub_keys,
              peer_expert_u, peer_expert_v):
    S = x_prompt.shape[1]
    T = x_sample.shape[1]
    pos_p = jnp.arange(S)
    pos_s = PAST_LEN + jnp.arange(T)
    keep_p = min(BAND_PAST, S)
    y_p, y_s = x_prompt, x_sample
    kp_l, vp_l, sp_l, ks_l, vs_l, ss_l = [], [], [], [], [], []
    for l in range(DEPTH):
        p = (mix_norm_g[l], w_in[l], attn_q_norm_g[l], attn_k_norm_g[l], attn_rel_bias[l],
             ret_out_norm_g[l], w_branch_attn[l], w_branch_ret[l], w_out[l], ffn_norm_g[l],
             peer_w_query[l], peer_sub_keys[l], peer_expert_u[l], peer_expert_v[l])

        def attend_prompt(q, k, v, rel_b):
            o = attention_prompt(q, k, v, rel_b)
            return o, k[:, S - keep_p:], v[:, S - keep_p:]

        def retain_prompt(q, k, v):
            return retention_prompt(q, k, v)

        ck, cv, cs = cache_attn_k[l], cache_attn_v[l], state_retention[l]

        def attend_sample(q, k, v, rel_b, ck=ck, cv=cv):
            r = ck.shape[1]
            kk = jnp.concatenate([ck, k], axis=1)
            vv = jnp.concatenate([cv, v], axis=1)
            qpos = jnp.arange(T)
            kpos = jnp.concatenate([jnp.arange(r) - r, jnp.arange(T)])
            kvalid = jnp.ones((r + T,), dtype=bool)
            return band_attention(q, kk, vv, qpos, kpos, kvalid, rel_b), k, v

        def retain_sample(q, k, v, cs=cs):
            return retention_block(q, k, v, cs)

        y_p, kp, vp, sp = layer_forward(y_p, pos_p, attend_prompt, retain_prompt, p)
        y_s, kn, vn, sn = layer_forward(y_s, pos_s, attend_sample, retain_sample, p)
        kp_l.append(kp); vp_l.append(vp); sp_l.append(sp)
        ks_l.append(kn); vs_l.append(vn); ss_l.append(sn)
    return (y_p, y_s, jnp.stack(kp_l), jnp.stack(vp_l), jnp.stack(sp_l),
            jnp.stack(ks_l), jnp.stack(vs_l), jnp.stack(ss_l))


_drawn_inputs = setup_inputs


def setup_inputs(seed=0):
    import zlib

    import numpy as np

    out = dict(_drawn_inputs(seed))
    spreads = {}
    factors = {'attn_q_norm_g': 8.0,
     'attn_k_norm_g': 2.981,
     'attn_rel_bias': 3.928,
     'ret_out_norm_g': 3.522,
     'cache_attn_k': 8.0,
     'cache_attn_v': 8.0,
     'ffn_norm_g': 3.274}
    for name, (base, spread) in spreads.items():
        noise = np.random.default_rng([zlib.crc32(name.encode()), seed]).standard_normal(out[name].shape)
        drawn = base * np.exp(spread * noise) if base else spread * noise
        out[name] = jnp.asarray(drawn.astype(out[name].dtype))
    for name, factor in factors.items():
        out[name] = (out[name] * factor).astype(out[name].dtype)
    return out
```

```python
import math
from contextlib import ExitStack

import numpy as np

import concourse.bass as bass
from concourse import mybir

F32 = mybir.dt.float32
U32 = mybir.dt.uint32
ALU = mybir.AluOpType
ACT = mybir.ActivationFunctionType
AX = mybir.AxisListType

P = 128
D = 1024
KD = D // P
SEQ, DEC, PAST = 1024, 64, 128
NP = SEQ // P
NT = NP + 1
TOK = SEQ + DEC
TPAD = NT * P
EPS = 1e-6
AH, AD = 8, 64
AW = AH * AD
BAND = 512
BT = BAND // P
CLIP = 128
MASK = -1e30
RH, RD = 4, 128
RW = RH * RD
ZW = 3 * AW + 4 * RW + 2 * D
O_A, O_R, O_G = 0, 3 * AW, 3 * AW + 4 * RW
KSCALE = float(RD) ** -0.5
PH, PK, TOPK = 8, 128, 16
HC = 2 * PH
SLOTS = PH * TOPK
CAND = TOPK * TOPK
LOWEST = -3.0e38
CHUNK = 64


def at(start, size):
    return slice(start, start + size) if isinstance(start, int) else bass.ds(start, size)


def after(eng, sem, value):
    if not isinstance(value, int) or value > 0:
        eng.wait_ge(sem, value)


def across(row, parts=P):
    return bass.AP(row.tensor, row.offset, [[0, parts]] + [list(x) for x in row.ap])


class Stage:

    def __init__(self, nc, name):
        self.nc, self.name, self.ctx, self.sems = nc, name, ExitStack(), []

    def __enter__(self):
        self.ctx.__enter__()
        return self

    def __exit__(self, *e):
        self.ctx.__exit__(*e)
        self.nc.clear_and_free_semaphores(self.sems)
        self.nc.all_engine_barrier()

    def sb(self, name, shape, dt=F32):
        return self.ctx.enter_context(self.nc.sbuf_tensor(f"{self.name}_{name}", shape, dt))

    def pb(self, name, shape):
        return self.ctx.enter_context(self.nc.psum_tensor(f"{self.name}_{name}", shape, F32))

    def sem(self, name):
        self.sems.append(self.nc.alloc_semaphore(name=f"{self.name}_{name}"))
        return self.sems[-1]

    def block(self):
        return self.ctx.enter_context(self.nc.Block())


def project(nc, d):
    NB = ZW // 512
    with Stage(nc, "prj") as s:
        x = s.sb("x", [P, NT, D])
        sq = s.sb("sq", [P, D])
        gain = s.sb("gain", [P, D])
        ident = s.sb("ident", [P, P])
        half = s.sb("half", [P, NT])
        ms = s.sb("ms", [P, NT])
        rs = s.sb("rs", [P, NT])
        h = s.sb("h", [P, 3, D])
        hT = s.sb("hT", [P, KD, TPAD])
        w = s.sb("w", [P, 2, KD, 512])
        zo = s.sb("zo", [P, NT, 512])
        tp = s.pb("tp", [P, 3, 512])
        zp = s.pb("zp", [P, 5, 512])
        x_in, gain_in, ident_in = s.sem("x_in"), s.sem("gain_in"), s.sem("ident_in")
        w_in = [[s.sem(f"w_in{slot}_{k}") for k in range(0, KD, 2)] for slot in range(2)]
        half_set, squared, mean_ready, rs_ready = s.sem("half_set"), s.sem("squared"), s.sem("mean_ready"), s.sem("rs_ready")
        h_ready, turned, turned_out = s.sem("h_ready"), s.sem("turned"), s.sem("turned_out")
        z_ready, z_out = s.sem("z_ready"), s.sem("z_out")
        z_stored = [s.sem(f"z_stored{n}") for n in range(3)]
        TURNED0, TOUT0, Z0 = 6, 3, 2 * NT
        ZOUT0 = NT
        bank = lambda i: 4 if i == 8 else i % 4
        block = s.block()

        @block.sync
        def _(sp):
            sp.dma_start(ident[:, :], d["ident"]).then_inc(ident_in, 16)
            sp.dma_start(gain[:, :], across(d["mix_g"])).then_inc(gain_in, 16)
            sp.dma_start(x[:, :, :], d["x"].rearrange("(n p) c -> p n c", p=P)).then_inc(x_in, 16)
            w_v = d["w_in"].rearrange("(k p) n -> p k n", p=P)

            def load(b, slot):
                sp.wait_ge(z_ready, NT * b + Z0 - NT)
                for k in range(0, KD, 2):
                    sp.dma_start(w[:, slot, k:k + 2, :], w_v[:, k:k + 2, at(b * 512, 512)]
                                 ).then_inc(w_in[slot][k // 2], 16)

            with sp.Fori(0, NB // 2) as pair:
                load(2 * pair, 0)
                load(2 * pair + 1, 1)
            load(NB - 1, 0)

        @block.gpsimd
        def _(pool):
            nc.gpsimd.memset(half[:, :], -0.5).then_inc(half_set, 1)
            pool.wait_ge(half_set, 1)
            pool.wait_ge(mean_ready, 1)
            nc.gpsimd.tensor_tensor(rs[:, :], ms[:, :], half[:, :], ALU.pow).then_inc(rs_ready, 1)

        @block.scalar
        def _(act):
            act.wait_ge(x_in, 16)
            with act.Fori(0, NT) as i:
                nc.scalar.activation(sq[:, :], x[:, i, :], ACT.Square, accum_out=ms[:, at(i, 1)]).then_inc(squared, 1)
                act.wait_ge(squared, i + 1)
            act.sem_inc(turned_out, TOUT0)
            act.sem_inc(z_out, ZOUT0)
            for g in range(3):
                act.sem_inc(z_stored[g], 16)
            z_v = d["z"].rearrange("(n p) c -> p n c", p=P)
            with act.Fori(0, 3) as g:
                for u in range(6):
                    act.wait_ge(turned, 6 * g + TURNED0 + u + 1)
                    nc.scalar.copy(hT[:, 4 * (u % 2):4 * (u % 2) + 4, at((3 * g + u // 2) * P, P)],
                                   tp[:, u % 3, :].rearrange("p (k t) -> p k t", k=4)).then_inc(turned_out, 1)
            with act.Fori(0, NB) as b:
                for i in range(NT):
                    act.wait_ge(z_ready, NT * b + Z0 + i + 1)
                    act.wait_ge(z_stored[i // 3], 16 * b + 16)
                    nc.scalar.copy(zo[:, i, :], zp[:, bank(i), :]).then_inc(z_out, 1)
                    if i % 3 == 2:
                        act.wait_ge(z_out, NT * b + ZOUT0 + i + 1)
                        act.dma_start(z_v[:, i - 2:i + 1, at(b * 512, 512)],
                                      zo[:, i - 2:i + 1, :]).then_inc(z_stored[i // 3], 16)
            for g in range(3):
                act.wait_ge(z_stored[g], 16 * NB + 16)

        @block.vector
        def _(dve):
            dve.wait_ge(squared, NT)
            nc.vector.tensor_scalar(ms[:, :], ms[:, :], 1.0 / D, EPS, ALU.mult, ALU.add).then_inc(mean_ready, 1)
            dve.wait_ge(gain_in, 16)
            dve.wait_ge(rs_ready, 1)
            with dve.Fori(0, 3) as g:
                for u in range(3):
                    dve.wait_ge(turned, 6 * g + TURNED0 + 2 * u - 4)
                    nc.vector.scalar_tensor_tensor(out=h[:, u, :], in0=x[:, 3 * g + u, :], scalar=rs[:, at(3 * g + u, 1)],
                                                   in1=gain[:, :], op0=ALU.mult, op1=ALU.mult).then_inc(h_ready, 1)

        @block.tensor
        def _(pe):
            pe.sem_inc(turned, TURNED0)
            pe.sem_inc(z_ready, Z0)
            pe.wait_ge(ident_in, 16)
            with pe.Fori(0, 3) as g:
                for u in range(6):
                    pe.wait_ge(h_ready, 3 * g + u // 2 + 1)
                    pe.wait_ge(turned_out, 6 * g + u + 1)
                    for k in range(4):
                        last = nc.tensor.transpose(tp[:, u % 3, k * P:(k + 1) * P],
                                                   h[:, u // 2, (4 * (u % 2) + k) * P:(4 * (u % 2) + k + 1) * P], ident[:, :])
                    last.then_inc(turned, 1)
            pe.wait_ge(turned_out, 2 * NT + TOUT0)

            def multiply(b, pair, slot):
                for i in range(NT):
                    before = i + 4 - NT if i < 4 else i - 4 if i < 8 else -1
                    pe.wait_ge(z_out, NT * b + ZOUT0 + before + 1)
                    for k in range(KD):
                        if i == 0 and k % 2 == 0:
                            pe.wait_ge(w_in[slot][k // 2], 16 * pair + 16)
                        last = nc.tensor.matmul(zp[:, bank(i), :], hT[:, k, i * P:(i + 1) * P],
                                                w[:, slot, k, :], start=(k == 0), stop=(k == KD - 1))
                    last.then_inc(z_ready, 1)

            with pe.Fori(0, NB // 2) as pair:
                multiply(2 * pair, pair, 0)
                multiply(2 * pair + 1, pair, 1)
            multiply(NB - 1, NB // 2, 0)


def gammas():
    return [1.0 - 2.0 ** (-5.0 - h) for h in range(RH)]


def mix(nc, d):
    with Stage(nc, "mix") as s:
        w_a = s.sb("w_a", [P, AW // P, D])
        w_r = s.sb("w_r", [P, RW // P, D])
        w_o = s.sb("w_o", [P, KD, D])
        ident = s.sb("ident", [P, P])
        bias8 = s.sb("bias8", [P, AH, (BT + 1) * P])
        keysT = s.sb("keysT", [P, AH // 2, NP * P])
        vals = s.sb("vals", [P, NP, AW])
        qpad = s.sb("qpad", [P, AH, P])
        za = s.sb("za", [P, 3 * AW])
        zr = s.sb("zr", [P, 4 * RW])
        zg = s.sb("zg", [P, 2 * D])
        x = s.sb("x", [P, D])
        cs = s.sb("cs", [P, 2, RD // 2])
        sq = s.sb("sq", [P, 2 * AW])
        qk = s.sb("qk", [P, 2 * AW])
        g_qk = s.sb("g_qk", [P, 2, AD])
        g_r = s.sb("g_r", [P, RW])
        g_f = s.sb("g_f", [P, D])
        part = s.sb("part", [P, 2, 2 * RH, RD // 2])
        rot = s.sb("rot", [P, 2 * RH, RD])
        rqT = s.sb("rqT", [P, RH, P])
        rqdT = s.sb("rqdT", [P, RH, P])
        rkT = s.sb("rkT", [P, RH, P])
        inner = s.sb("inner", [P, RH, P])
        decay = s.sb("decay", [P, RH, P])
        q_dec = s.sb("q_dec", [P, RH, P])
        k_dec = s.sb("k_dec", [P, 2, RH])
        state = s.sb("state", [P, 2, RH, RD])
        ro = s.sb("ro", [P, RW])
        r_gate = s.sb("r_gate", [P, RW])
        sc = s.sb("sc", [P, 2, (BT + 1) * P])
        pT = s.sb("pT", [P, 2, BT + 1, P])
        oa = s.sb("oa", [P, AW])
        tT = s.sb("tT", [P, KD, P])
        half = s.sb("half", [P, 16])
        qk_ms, qk_rs = s.sb("qk_ms", [P, 16]), s.sb("qk_rs", [P, 16])
        r_ms, r_rs = s.sb("r_ms", [P, RH]), s.sb("r_rs", [P, RH])
        f_ms, f_rs = s.sb("f_ms", [P, 1]), s.sb("f_rs", [P, 1])
        neg_max, den, rden = s.sb("neg_max", [P, AH]), s.sb("den", [P, AH]), s.sb("rden", [P, AH])
        S = s.pb("S", [P, 2, 1024])
        T = s.pb("T", [P, 2, 512])
        OM = s.pb("OM", [P, 2, 512])
        O, M = OM[:, 0, :], OM[:, 1, :]
        heads4 = lambda ap: ap.rearrange("p (h e) -> p h e", h=RH)

        BW = (BT + 1) * P
        mark = s.sb("mark", [P, AH])
        flip = s.sb("flip", [P, P])
        bias_rev = w_o[:, :, :].rearrange("p k n -> p (k n)")[:, 0:AH * BW].rearrange("p (h n) -> p h n", h=AH)
        names = """ident_in bias_turned w_in bias_in const_in cache_in za_in zr_in zg_in x_in state_in
            bias_set zeros_set halves_set
            qk_squared qk_summed qk_mean qk_rs_ready qk_scaled qk_ready v_ready
            q_turned k_turned q_padded keys_ready cache_turned
            rot_part rotated rq_turned rk_turned rq_ready rqd_ready rk_ready k_decayed
            inner_ready inner_scaled ret_ready ret_out update_ready state_ready
            r_squared r_summed r_mean r_rs_ready r_scaled r_exp r_plus r_silu r_gained r_ready
            scores_ready softmax_in p_ready p_turned p_out o_ready den_ready oa_ready
            oa_turned r_turned oa_out r_out gate_exp gate_plus gates_ready
            branch_ready gated merged m_turned m_out proj_ready x2_ready
            f_squared f_mean f_rs_ready h2_ready h2_turned h2_out
            k_stored v_stored x2_stored h2_stored state_stored""".split()
        (ident_in, bias_turned, w_in, bias_in, const_in, cache_in, za_in, zr_in, zg_in, x_in, state_in,
         bias_set, zeros_set, halves_set,
         qk_squared, qk_summed, qk_mean, qk_rs_ready, qk_scaled, qk_ready, v_ready,
         q_turned, k_turned, q_padded, keys_ready, cache_turned,
         rot_part, rotated, rq_turned, rk_turned, rq_ready, rqd_ready, rk_ready, k_decayed,
         inner_ready, inner_scaled, ret_ready, ret_out, update_ready, state_ready,
         r_squared, r_summed, r_mean, r_rs_ready, r_scaled, r_exp, r_plus, r_silu, r_gained, r_ready,
         scores_ready, softmax_in, p_ready, p_turned, p_out, o_ready, den_ready, oa_ready,
         oa_turned, r_turned, oa_out, r_out, gate_exp, gate_plus, gates_ready,
         branch_ready, gated, merged, m_turned, m_out, proj_ready, x2_ready,
         f_squared, f_mean, f_rs_ready, h2_ready, h2_turned, h2_out,
         k_stored, v_stored, x2_stored, h2_stored, state_stored) = [s.sem(n) for n in names]
        block = s.block()

        def tiles(eng, body):
            for i in range(BT):
                body(i, i)
            with eng.Fori(BT, NP) as i:
                body(i, BT)
            body(NP, 1)

        @block.sync
        def _(sp):
            sp.sem_inc(k_stored, 16)
            sp.dma_start(ident[:, :], d["ident"]).then_inc(ident_in, 16)
            sp.dma_start(flip[:, :], d["flip"]).then_inc(ident_in, 16)
            rel = d["rel"]
            sp.dma_start(bias_rev, bass.AP(rel.tensor, rel.offset, [[1, P], [rel.shape[1], AH], [1, BW]])).then_inc(bias_in, 16)
            for out, src in ((g_qk[:, 0, :], across(d["q_g"])), (g_qk[:, 1, :], across(d["k_g"])),
                             (g_r[:, :], across(d["r_g"])), (g_f[:, :], across(d["f_g"])),
                             (decay[:, :, :], d["decay"]), (q_dec[:, :, :], d["q_dec"]), (k_dec[:, :, :], d["k_dec"])):
                sp.dma_start(out, src).then_inc(const_in, 16)
            sp.dma_start(state[:, 1, :, :], d["state"].rearrange("h d e -> d h e")).then_inc(state_in, 16)

            def body(i, past):
                row = i * P if isinstance(i, int) else sp.snap((i - BT) * P)
                after(sp, qk_scaled, i)
                after(sp, v_ready, i)
                after(sp, qk_squared, i)
                sp.dma_start(za[:, :], d["z"][at(i * P, P), O_A:O_R]).then_inc(za_in, 16)
                after(sp, rotated, i)
                after(sp, update_ready, i)
                after(sp, r_ready, i)
                sp.dma_start(zr[:, :], d["z"][at(i * P, P), O_R:O_G]).then_inc(zr_in, 16)
                sp.dma_start(cs[:, :, :], d["cs"][at(i * P, P), :, :]).then_inc(zr_in, 16)
                after(sp, h2_turned, 2 * i)
                after(sp, merged, i)
                sp.dma_start(zg[:, :], d["z"][at(i * P, P), O_G:ZW]).then_inc(zg_in, 16)
                after(sp, x2_stored, 16 * i)
                after(sp, f_squared, i)
                after(sp, h2_ready, i)
                sp.dma_start(x[:, :], d["x"][at(i * P, P), :]).then_inc(x_in, 16)
                if isinstance(i, int) and i == 0:
                        for k in range(2):
                            sp.dma_start(w_a[:, 2 * k:2 * k + 2, :], d["w_a"].rearrange("(k p) n -> p k n", p=P)[:, 2 * k:2 * k + 2, :]).then_inc(w_in, 16)
                            sp.dma_start(w_r[:, 2 * k:2 * k + 2, :], d["w_r"].rearrange("(k p) n -> p k n", p=P)[:, 2 * k:2 * k + 2, :]).then_inc(w_in, 16)
                        sp.wait_ge(bias_set, AH)
                        sp.dma_start(w_o[:, :, :], d["w_o"].rearrange("(k p) n -> p k n", p=P)).then_inc(w_in, 16)
                if not isinstance(i, int) or i == NP:
                    kd, vd, n = ((d["nks"], d["nvs"], DEC) if isinstance(i, int) else
                                 (d["nkp"][at(row, P), :], d["nvp"][at(row, P), :], P))
                    slot = 1 if isinstance(i, int) else i
                    sp.wait_ge(qk_ready, i + 1)
                    sp.dma_start(kd, qk[0:n, AW:2 * AW]).then_inc(k_stored, 16)
                    sp.wait_ge(v_ready, i + 1)
                    sp.dma_start(vd, vals[0:n, slot, :]).then_inc(v_stored, 16)

            for i in range(BT):
                body(i, i)
            with sp.Fori(BT, NP) as i:
                body(i, BT)
            sp.wait_ge(o_ready, AH * NP)
            sp.wait_ge(k_turned, NP)
            sp.wait_ge(k_stored, 16 * (NP - BT) + 16)
            sp.dma_start(qk[:, AW:2 * AW], d["ck"]).then_inc(cache_in, 16)
            sp.dma_start(vals[:, 0, :], d["cv"]).then_inc(cache_in, 16)
            body(NP, 1)
            sp.wait_ge(state_ready, RH * NP)
            sp.dma_start(d["nsp"].rearrange("h d e -> d h e"), state[:, 0, :, :]).then_inc(state_stored, 16)
            sp.wait_ge(state_ready, RH * NT)
            sp.dma_start(d["nss"].rearrange("h d e -> d h e"), state[:, 1, :, :]).then_inc(state_stored, 16)
            sp.wait_ge(state_stored, 32)
            sp.wait_ge(k_stored, 16 * (NP - BT + 1) + 16)
            sp.wait_ge(v_stored, 16 * (NP - BT + 1))

        @block.gpsimd
        def _(pool):
            nc.gpsimd.memset(half[:, :], -0.5).then_inc(halves_set, 1)
            pool.wait_ge(halves_set, 1)
            nc.gpsimd.memset(qpad[:, :, :], 0.0).then_inc(zeros_set, 1)
            nc.gpsimd.memset(state[:, 0, :, :], 0.0).then_inc(zeros_set, 1)
            pool.wait_ge(const_in, 7 * 16)

            def body(i, past):
                sample = isinstance(i, int) and i == NP
                slot = 1 if sample else i
                pool.wait_ge(za_in, 16 * i + 16)
                after(pool, f_squared, i)
                nc.gpsimd.tensor_tensor(sq[:, :], za[:, 0:2 * AW], za[:, 0:2 * AW], ALU.mult).then_inc(qk_squared, 1)
                nc.gpsimd.tensor_copy(vals[:, slot, :], za[:, 2 * AW:3 * AW]).then_inc(v_ready, 1)
                pool.wait_ge(zr_in, 32 * i + 32)
                after(pool, rq_turned, i)
                after(pool, update_ready, i)
                zqk = zr[:, 0:2 * RW].rearrange("p (h c e) -> p h c e", h=2 * RH, c=2)
                x1, x2_ = zqk[:, :, 0, :], zqk[:, :, 1, :]
                cos = cs[:, 0:1, :].broadcast_to([P, 2 * RH, RD // 2])
                sin = cs[:, 1:2, :].broadcast_to([P, 2 * RH, RD // 2])
                for n, (a, ta, b, tb, op, out) in enumerate(((x1, cos, x2_, sin, ALU.subtract, rot[:, :, 0:RD // 2]),
                                                             (x1, sin, x2_, cos, ALU.add, rot[:, :, RD // 2:RD]))):
                    nc.gpsimd.tensor_tensor(part[:, 0, :, :], a, ta, ALU.mult).then_inc(rot_part, 1)
                    nc.gpsimd.tensor_tensor(part[:, 1, :, :], b, tb, ALU.mult).then_inc(rot_part, 1)
                    pool.wait_ge(rot_part, 5 * i + 3 * n + 2)
                    nc.gpsimd.tensor_tensor(out, part[:, 0, :, :], part[:, 1, :, :], op).then_inc(
                        rot_part if n == 0 else rotated, 1)
                    if n == 0:
                        pool.wait_ge(rot_part, 5 * i + 3)
                pool.wait_ge(qk_mean, i + 1)
                nc.gpsimd.tensor_tensor(qk_rs[:, :], qk_ms[:, :], half[:, :], ALU.pow).then_inc(qk_rs_ready, 1)
                pool.wait_ge(rotated, i + 1)
                pool.wait_ge(rk_turned, i + 1)
                kdec = k_dec[:, 1 if sample else 0, :].rearrange("p (h o) -> p h o", o=1).broadcast_to([P, RH, RD])
                nc.gpsimd.tensor_tensor(rot[:, RH:, :], rot[:, RH:, :], kdec, ALU.mult).then_inc(k_decayed, 1)
                pool.wait_ge(ret_out, i + 1)
                pool.wait_ge(qk_summed, i + 1)
                nc.gpsimd.tensor_tensor(sq[:, 0:RW], ro[:, :], ro[:, :], ALU.mult).then_inc(r_squared, 1)
                pool.wait_ge(r_mean, i + 1)
                nc.gpsimd.tensor_tensor(r_rs[:, :], r_ms[:, :], half[:, 0:RH], ALU.pow).then_inc(r_rs_ready, 1)
                pool.wait_ge(f_mean, i + 1)
                nc.gpsimd.tensor_tensor(f_rs[:, :], f_ms[:, :], half[:, 0:1], ALU.pow).then_inc(f_rs_ready, 1)

            tiles(pool, body)

        @block.scalar
        def _(act):
            def body(i, past):
                sample = isinstance(i, int) and i == NP
                slot = 1 if sample else i
                if sample:
                    act.wait_ge(cache_turned, 1)
                    nc.scalar.copy(keysT[:, :, 0:P], T[:, 1, :].rearrange("p (k t) -> p k t", k=4)).then_inc(keys_ready, 1)
                act.wait_ge(zr_in, 32 * i + 32)
                after(act, r_ready, i)
                nc.scalar.activation(r_gate[:, :], zr[:, 3 * RW:4 * RW], ACT.Exp, scale=-1.0).then_inc(r_exp, 1)
                act.wait_ge(q_turned, i + 1)
                act.wait_ge(zeros_set, 2)
                for odd in range(2):
                    rows = slice(64 * odd, 64 * odd + 64)
                    nc.scalar.copy(qpad[rows, odd:AH:2, :],
                                   T[rows, 0, :].rearrange("p (k t) -> p k t", k=4)).then_inc(q_padded, 1)
                act.wait_ge(k_turned, i + 1)
                nc.scalar.copy(keysT[:, :, at(slot * P, P)],
                               T[:, 1, :].rearrange("p (k t) -> p k t", k=4)).then_inc(keys_ready, 1)
                act.wait_ge(rq_turned, i + 1)
                nc.scalar.copy(rqT[:, :, :], heads4(O)).then_inc(rq_ready, 1)
                act.wait_ge(rk_turned, i + 1)
                nc.scalar.activation(rkT[:, :, :], heads4(M), ACT.Copy, scale=KSCALE).then_inc(rk_ready, 1)
                act.wait_ge(zg_in, 16 * i + 16)
                nc.scalar.activation(zg[:, :], zg[:, :], ACT.Exp, scale=-1.0).then_inc(gate_exp, 1)
                act.wait_ge(ret_ready, i + 1)
                after(act, r_turned, i)
                nc.scalar.copy(ro[:, :], O).then_inc(ret_out, 1)
                for h in range(AH):
                    W = (past + 1) * P if not sample else P + DEC
                    act.wait_ge(softmax_in, AH * i + h + 1)
                    nc.scalar.activation(sc[:, h % 2, 0:W], sc[:, h % 2, 0:W], ACT.Exp, scale=-1.0,
                                         bias=neg_max[:, h:h + 1], accum_out=den[:, h:h + 1]).then_inc(p_ready, 1)
                    act.wait_ge(p_turned, AH * i + h + 1)
                    after(act, o_ready, AH * i + h - 1)
                    if sample:
                        nc.scalar.copy(pT[:, h % 2, 0, :], T[:, 0, 0:P])
                        nc.scalar.copy(pT[0:DEC, h % 2, 1, :], T[0:DEC, 0, P:2 * P]).then_inc(p_out, 1)
                    else:
                        nc.scalar.copy(pT[:, h % 2, 0:past + 1, :].rearrange("p k t -> p (k t)"),
                                       T[:, :, :].rearrange("p b n -> p (b n)")[:, 0:W]).then_inc(p_out, 1)
                act.wait_ge(r_turned, i + 1)
                after(act, h2_stored, 16 * i)
                nc.scalar.copy(tT[:, 4:8, :], T[:, 0, :].rearrange("p (k t) -> p k t", k=4)).then_inc(r_out, 1)
                act.wait_ge(oa_turned, i + 1)
                nc.scalar.copy(tT[:, 0:4, :], T[:, 1, :].rearrange("p (k t) -> p k t", k=4)).then_inc(oa_out, 1)
                for b in range(2):
                    act.wait_ge(m_turned, 2 * i + b + 1)
                    nc.scalar.copy(tT[:, 4 * b:4 * b + 4, :], T[:, b, :].rearrange("p (k t) -> p k t", k=4)).then_inc(m_out, 1)
                act.wait_ge(x2_ready, i + 1)
                act.dma_start(d["x2"][at(i * P, P), :], x[:, :]).then_inc(x2_stored, 16)
                for b in range(2):
                    act.wait_ge(h2_turned, 2 * i + b + 1)
                    nc.scalar.copy(tT[:, 4 * b:4 * b + 4, :], T[:, b, :].rearrange("p (k t) -> p k t", k=4)).then_inc(h2_out, 1)
                act.wait_ge(h2_out, 2 * i + 2)
                act.dma_start(d["h2T"].rearrange("(k p) t -> p k t", p=P)[:, :, at(i * P, P)], tT[:, :, :]).then_inc(h2_stored, 16)

            tiles(act, body)
            act.wait_ge(x2_stored, 16 * NT)
            act.wait_ge(h2_stored, 16 * NT)

        @block.vector
        def _(dve):
            V = nc.vector
            for h in range(AH):
                dve.wait_ge(bias_turned, h + 1)
                V.tensor_scalar(bias8[:, h, :], S[:, h % 2, 0:BW], float(AD) ** 0.5, None, ALU.mult).then_inc(bias_set, 1)
            dve.wait_ge(bias_set, AH)
            V.memset(bias8[0:64, :, BAND + CHUNK:BAND + P], 8 * MASK).then_inc(bias_set, 1)
            V.memset(bias8[64:128, :, 0:CHUNK], 8 * MASK).then_inc(bias_set, 1)
            dve.wait_ge(bias_set, AH + 2)
            dve.wait_ge(const_in, 7 * 16)
            dve.wait_ge(state_in, 16)
            dve.wait_ge(zeros_set, 2)

            def body(i, past):
                sample = isinstance(i, int) and i == NP
                st = 1 if sample else 0
                W = (past + 1) * P if not sample else P + DEC
                b0 = (BT - past) * P
                dve.wait_ge(qk_squared, i + 1)
                V.tensor_reduce(qk_ms[:, :], sq[:, :].rearrange("p (h e) -> p h e", e=AD), AX.X, ALU.add).then_inc(qk_summed, 1)
                dve.wait_ge(qk_summed, i + 1)
                V.tensor_scalar(qk_ms[:, :], qk_ms[:, :], 1.0 / AD, EPS, ALU.mult, ALU.add).then_inc(qk_mean, 1)
                dve.wait_ge(qk_rs_ready, i + 1)
                if sample:
                    dve.wait_ge(cache_turned, 1)
                if not isinstance(i, int) or sample:
                    dve.wait_ge(k_stored, 16 * (i - BT) + 16)
                after(dve, k_turned, i)
                V.tensor_tensor(qk[:, :].rearrange("p (h e) -> p h e", e=AD), za[:, 0:2 * AW].rearrange("p (h e) -> p h e", e=AD),
                                qk_rs[:, :].rearrange("p (h o) -> p h o", o=1).broadcast_to([P, 2 * AH, AD]), ALU.mult
                                ).then_inc(qk_scaled, 1)
                dve.wait_ge(qk_scaled, i + 1)
                qk4 = qk[:, :].rearrange("p (c h e) -> p c h e", c=2, e=AD)
                gq = g_qk[:, :, :].rearrange("p c (o e) -> p c o e", o=1).broadcast_to([P, 2, AH, AD])
                V.tensor_tensor(qk4, qk4, gq, ALU.mult).then_inc(qk_ready, 1)
                dve.wait_ge(rq_ready, i + 1)
                V.tensor_tensor(rqdT[:, :, :], rqT[:, :, :], q_dec[:, :, :], ALU.mult).then_inc(rqd_ready, 1)
                dve.wait_ge(inner_ready, i + 1)
                V.tensor_tensor(inner[:, :, :], heads4(M), decay[:, :, :], ALU.mult).then_inc(inner_scaled, 1)
                dve.wait_ge(update_ready, i + 1)
                for h in range(RH):
                    g_l = gammas()[h] ** (DEC if sample else P)
                    V.scalar_tensor_tensor(out=state[:, st, h, :], in0=state[:, st, h, :], scalar=g_l,
                                           in1=M[:, h * RD:(h + 1) * RD], op0=ALU.mult, op1=ALU.add).then_inc(state_ready, 1)

                def softmax_head(h):
                    dve.wait_ge(scores_ready, AH * i + h + 1)
                    after(dve, p_turned, AH * i + h - 1)
                    V.memset(mark[:, h:h + 1], 0.0)
                    V.tensor_tensor_reduce(out=sc[:, h % 2, 0:W], in0=S[:, h % 2, 0:W], in1=bias8[:, h, b0:b0 + W],
                                           scale=-float(AD) ** -0.5, scalar=-LOWEST, op0=ALU.add, op1=ALU.min,
                                           accum_out=neg_max[:, h:h + 1]).then_inc(softmax_in, 1)

                softmax_head(0)
                softmax_head(1)
                dve.wait_ge(r_squared, i + 1)
                V.tensor_reduce(r_ms[:, :], heads4(sq[:, 0:RW]), AX.X, ALU.add).then_inc(r_summed, 1)
                dve.wait_ge(r_summed, i + 1)
                V.tensor_scalar(r_ms[:, :], r_ms[:, :], 1.0 / RD, EPS, ALU.mult, ALU.add).then_inc(r_mean, 1)
                softmax_head(2)
                dve.wait_ge(r_exp, i + 1)
                V.tensor_scalar(r_gate[:, :], r_gate[:, :], 1.0, None, ALU.add).then_inc(r_plus, 1)
                softmax_head(3)
                dve.wait_ge(r_plus, 2 * i + 1)
                V.reciprocal(r_gate[:, :], r_gate[:, :]).then_inc(r_plus, 1)
                dve.wait_ge(r_plus, 2 * i + 2)
                V.tensor_tensor(r_gate[:, :], r_gate[:, :], zr[:, 3 * RW:4 * RW], ALU.mult).then_inc(r_silu, 1)
                softmax_head(4)
                dve.wait_ge(r_rs_ready, i + 1)
                dve.wait_ge(ret_out, i + 1)
                V.tensor_tensor(heads4(ro[:, :]), heads4(ro[:, :]),
                                r_rs[:, :].rearrange("p (h o) -> p h o", o=1).broadcast_to([P, RH, RD]), ALU.mult).then_inc(r_scaled, 1)
                dve.wait_ge(r_scaled, i + 1)
                V.tensor_tensor(ro[:, :], ro[:, :], g_r[:, :], ALU.mult).then_inc(r_gained, 1)
                softmax_head(5)
                dve.wait_ge(r_gained, i + 1)
                dve.wait_ge(r_silu, i + 1)
                V.tensor_tensor(ro[:, :], ro[:, :], r_gate[:, :], ALU.mult).then_inc(r_ready, 1)
                dve.wait_ge(gate_exp, i + 1)
                V.tensor_scalar(zg[:, :], zg[:, :], 1.0, None, ALU.add).then_inc(gate_plus, 1)
                softmax_head(6)
                softmax_head(7)
                dve.wait_ge(gate_plus, i + 1)
                V.reciprocal(zg[:, :], zg[:, :]).then_inc(gates_ready, 1)
                dve.wait_ge(p_ready, AH * i + AH)
                V.reciprocal(rden[:, :], den[:, :]).then_inc(den_ready, 1)
                dve.wait_ge(den_ready, i + 1)
                dve.wait_ge(o_ready, AH * i + AH)
                after(dve, oa_turned, i)
                V.tensor_tensor(oa[:, :].rearrange("p (h e) -> p h e", e=AD), M.rearrange("p (h e) -> p h e", e=AD),
                                rden[:, :].rearrange("p (h o) -> p h o", o=1).broadcast_to([P, AH, AD]), ALU.mult
                                ).then_inc(oa_ready, 1)
                dve.wait_ge(gates_ready, i + 1)
                for c in range(2):
                    dve.wait_ge(branch_ready, 2 * i + c + 1)
                    V.tensor_tensor(zg[:, c * D:(c + 1) * D], zg[:, c * D:(c + 1) * D], S[:, c, :], ALU.mult).then_inc(gated, 1)
                dve.wait_ge(gated, 2 * i + 2)
                V.tensor_tensor(zg[:, 0:D], zg[:, 0:D], zg[:, D:2 * D], ALU.add).then_inc(merged, 1)
                dve.wait_ge(proj_ready, i + 1)
                dve.wait_ge(x_in, 16 * i + 16)
                V.tensor_tensor(x[:, :], x[:, :], OM[:, :, :].rearrange("p b n -> p (b n)"), ALU.add).then_inc(x2_ready, 1)
                dve.wait_ge(x2_ready, i + 1)
                dve.wait_ge(r_summed, i + 1)
                V.tensor_tensor_reduce(out=sq[:, :], in0=x[:, :], in1=x[:, :], scale=1.0, scalar=0.0, op0=ALU.mult, op1=ALU.add,
                                       accum_out=f_ms[:, 0:1]).then_inc(f_squared, 1)
                dve.wait_ge(f_squared, i + 1)
                V.tensor_scalar(f_ms[:, :], f_ms[:, :], 1.0 / D, EPS, ALU.mult, ALU.add).then_inc(f_mean, 1)
                dve.wait_ge(f_rs_ready, i + 1)
                dve.wait_ge(m_turned, 2 * i + 2)
                V.scalar_tensor_tensor(out=zg[:, 0:D], in0=x[:, :], scalar=f_rs[:, 0:1], in1=g_f[:, :],
                                       op0=ALU.mult, op1=ALU.mult).then_inc(h2_ready, 1)

            tiles(dve, body)

        @block.tensor
        def _(pe):
            def mm(out, a, b, start=True, stop=True):
                return nc.tensor.matmul(out, a, b, start=start, stop=stop)

            def turn(out_bank, src, n=4, width=P):
                for k in range(n):
                    last = nc.tensor.transpose(out_bank[:, k * P:(k + 1) * P], src(k), ident[:, :])
                return last

            pe.wait_ge(ident_in, 32)
            pe.wait_ge(bias_in, 16)
            for h in range(AH):
                after(pe, bias_set, h - 1)
                mm(S[:, h % 2, 0:512], flip[:, :], bias_rev[:, h, 0:512])
                mm(S[:, h % 2, 512:BW], flip[:, :], bias_rev[:, h, 512:BW]).then_inc(bias_turned, 1)

            def body(i, past):
                sample = isinstance(i, int) and i == NP
                st = 1 if sample else 0
                first = 0 if sample or isinstance(i, int) else (i - BT) * P
                after(pe, h2_out, 2 * i)
                if sample:
                    pe.wait_ge(cache_in, 32)
                    turn(T[:, 1, :], lambda k: qk[:, AW + k * P:AW + (k + 1) * P]).then_inc(cache_turned, 1)
                    pe.wait_ge(keys_ready, NP + 1)
                pe.wait_ge(qk_ready, i + 1)
                turn(T[:, 0, :], lambda k: qk[:, k * P:(k + 1) * P]).then_inc(q_turned, 1)
                turn(T[:, 1, :], lambda k: qk[:, AW + k * P:AW + (k + 1) * P]).then_inc(k_turned, 1)
                after(pe, x2_ready, i)
                pe.wait_ge(rotated, i + 1)
                turn(O, lambda k: rot[:, k, :]).then_inc(rq_turned, 1)
                turn(M, lambda k: rot[:, RH + k, :]).then_inc(rk_turned, 1)
                pe.wait_ge(rq_ready, i + 1)
                pe.wait_ge(rk_ready, i + 1)
                for h in range(RH):
                    last = mm(M[:, h * P:(h + 1) * P], rkT[:, h, :], rqT[:, h, :])
                last.then_inc(inner_ready, 1)
                pe.wait_ge(inner_scaled, i + 1)
                pe.wait_ge(rqd_ready, i + 1)
                after(pe, state_ready, RH * i)
                for h in range(RH):
                    v = zr[:, 2 * RW + h * RD:2 * RW + (h + 1) * RD]
                    mm(O[:, h * RD:(h + 1) * RD], inner[:, h, :], v, stop=False)
                    last = mm(O[:, h * RD:(h + 1) * RD], rqdT[:, h, :], state[:, st, h, :], start=False)
                last.then_inc(ret_ready, 1)
                pe.wait_ge(k_decayed, i + 1)
                for h in range(RH):
                    last = mm(M[:, h * RD:(h + 1) * RD], rot[:, RH + h, :], zr[:, 2 * RW + h * RD:2 * RW + (h + 1) * RD])
                last.then_inc(update_ready, 1)

                def scores(h):
                    W = (past + 1) * P if not sample else P + DEC
                    after(pe, softmax_in, AH * i + h - 1)
                    if h < 2:
                        after(pe, gated, 2 * i)
                        pe.wait_ge(bias_set, AH)
                    last = mm(S[:, h % 2, 0:min(W, 512)], qpad[:, h, :], keysT[:, h // 2, at(first, min(W, 512))])
                    if W > 512:
                        last = mm(S[:, h % 2, 512:W], qpad[:, h, :], keysT[:, h // 2, at(first + 512, W - 512)])
                    last.then_inc(scores_ready, 1)

                def values(h):
                    pe.wait_ge(p_ready, AH * i + h + 1)
                    after(pe, p_out, AH * i + h)
                    n = past + 1
                    for k in range(n):
                        w_ = DEC if sample and k == 1 else P
                        last = nc.tensor.transpose(T[0:w_, k // 4, (k % 4) * P:(k % 4 + 1) * P],
                                                   sc[:, h % 2, k * P:k * P + w_], ident[:, :])
                    last.then_inc(p_turned, 1)
                    pe.wait_ge(p_out, AH * i + h + 1)
                    if h == 0:
                        pe.wait_ge(state_ready, RH * i + RH)
                        pe.wait_ge(v_ready, i + 1)
                    for k in range(n):
                        w_ = DEC if sample and k == 1 else P
                        vt = k if sample or isinstance(i, int) else i - BT + k
                        last = mm(M[:, h * AD:(h + 1) * AD], pT[0:w_, h % 2, k, :], vals[0:w_, vt, h * AD:(h + 1) * AD],
                                  start=(k == 0), stop=(k == n - 1))
                    last.then_inc(o_ready, 1)

                pe.wait_ge(q_padded, 2 * i + 2)
                pe.wait_ge(keys_ready, i + 1 + (1 if sample else 0))
                scores(0)
                scores(1)
                for h in range(AH):
                    values(h)
                    if h + 2 < AH:
                        scores(h + 2)
                pe.wait_ge(r_ready, i + 1)
                turn(T[:, 0, :], lambda k: ro[:, k * P:(k + 1) * P]).then_inc(r_turned, 1)
                pe.wait_ge(oa_ready, i + 1)
                turn(T[:, 1, :], lambda k: oa[:, k * P:(k + 1) * P]).then_inc(oa_turned, 1)
                if isinstance(i, int) and i == 0:
                    pe.wait_ge(w_in, 5 * 16)
                pe.wait_ge(oa_out, i + 1)
                pe.wait_ge(softmax_in, AH * i + AH)
                for c in range(2):
                    if c == 1:
                        pe.wait_ge(r_out, i + 1)
                    for n in range(2):
                        for k in range(4):
                            last = mm(S[:, c, n * 512:(n + 1) * 512], tT[:, 4 * c + k, :],
                                      (w_a, w_r)[c][:, k, n * 512:(n + 1) * 512], start=(k == 0), stop=(k == 3))
                    last.then_inc(branch_ready, 1)
                pe.wait_ge(merged, i + 1)
                for b in range(2):
                    turn(T[:, b, :], lambda k: zg[:, (4 * b + k) * P:(4 * b + k + 1) * P]).then_inc(m_turned, 1)
                pe.wait_ge(m_out, 2 * i + 2)
                pe.wait_ge(ret_out, i + 1)
                for n in range(2):
                    for k in range(KD):
                        last = mm(OM[:, n, :], tT[:, k, :], w_o[:, k, n * 512:(n + 1) * 512], start=(k == 0), stop=(k == KD - 1))
                last.then_inc(proj_ready, 1)
                pe.wait_ge(h2_ready, i + 1)
                for b in range(2):
                    turn(T[:, b, :], lambda k: zg[:, (4 * b + k) * P:(4 * b + k + 1) * P]).then_inc(h2_turned, 1)

            tiles(pe, body)


def route(nc, d):
    G, GT = 3, 3
    GW = GT * P
    PARTS = (range(0, 5), range(5, 10), range(10, HC))
    with Stage(nc, "rt") as s:
        wq = s.sb("wq", [P, KD, 2 * PH * PK])
        keys = s.sb("keys", [P, HC, PK])
        h2T = s.sb("h2T", [P, 2, KD, GW])
        qT = s.sb("qT", [P, 2, HC, GW])
        sc = s.sb("sc", [P, GT, HC, PK])
        ident = s.sb("ident", [P, P])
        iota16 = s.sb("iota16", [P, TOPK])
        tv = s.sb("tv", [P, PH, 2, TOPK])
        ti = s.sb("ti", [P, PH, 2, TOPK], U32)
        tf = s.sb("tf", [P, PH, 2, TOPK])
        cand = s.sb("cand", [P, PH, TOPK, TOPK])
        bv = s.sb("bv", [P, PH, TOPK])
        bi = s.sb("bi", [P, PH, TOPK], U32)
        ab = s.sb("ab", [P, 2, SLOTS], U32)
        abf = s.sb("abf", [P, 2, SLOTS])
        hit = s.sb("hit", [P, 2, SLOTS, TOPK])
        out = s.sb("out", [P, 3, SLOTS])
        den = s.sb("den", [P, 2, PH])
        outT = s.sb("outT", [P, 3, P])
        mark = s.sb("mark", [P, 1])
        qp = s.pb("qp", [P, 3, 512])
        sp_ = s.pb("sp", [P, 4, 512])
        tp = s.pb("tp", [P, 512])
        names = """const_in w_in h2_in0 h2_in1 iota_set q_ready q_out s_ready s_out
            top8 found8 cut8 top16 found16 keyed cand_ready best8 bfound8 bcut8 best16 bfound16
            split ab_ready hit_ready picked shifted expd summed recip out_ready out_turned outT_ready stored""".split()
        (const_in, w_in, h2_in0, h2_in1, iota_set, q_ready, q_out, s_ready, s_out,
         top8, found8, cut8, top16, found16, keyed, cand_ready, best8, bfound8, bcut8, best16, bfound16,
         split, ab_ready, hit_ready, picked, shifted, expd, summed, recip, out_ready, out_turned, outT_ready, stored
         ) = [s.sem(n) for n in names]
        h2_in = (h2_in0, h2_in1)
        block = s.block()

        @block.sync
        def _(sp):
            sp.dma_start(ident[:, :], d["ident"]).then_inc(const_in, 16)
            h2_v = d["h2T"].rearrange("(k p) t -> p k t", p=P)
            for g in range(G):
                after(sp, q_ready, HC * (g - 1))
                sp.dma_start(h2T[:, g % 2, :, :], h2_v[:, :, g * GW:(g + 1) * GW]).then_inc(h2_in[g % 2], 16)
                if g == 0:
                    w_v = d["w_q"].rearrange("(k p) n -> p k n", p=P)
                    for c in range(4):
                        sp.dma_start(wq[:, :, c * 512:(c + 1) * 512], w_v[:, :, c * 512:(c + 1) * 512]).then_inc(w_in, 16)
                        sp.wait_ge(w_in, 16 * c + 16)
                    sp.dma_start(keys[:, :, :], d["keys"]).then_inc(const_in, 16)

        @block.gpsimd
        def _(pool):
            nc.gpsimd.iota(iota16[:, :], [[1, TOPK]], base=0, channel_multiplier=0,
                           allow_small_or_imprecise_dtypes=True).then_inc(iota_set, 1)
            pool.wait_ge(iota_set, 1)
            with pool.Fori(0, NT) as t:
                for c in range(2):
                    pool.wait_ge(hit_ready, 2 * t + c + 1)
                    h4 = hit[:, c, :, :].rearrange("p (h k) a -> p h k a", h=PH)
                    keyv = tf[:, :, c, :].rearrange("p h (o a) -> p h o a", o=1).broadcast_to([P, PH, TOPK, TOPK])
                    nc.gpsimd.tensor_tensor(h4, h4, keyv, ALU.mult).then_inc(picked, 1)

        @block.scalar
        def _(act):
            act.sem_inc(stored, 16)

            def queries_out(g, part):
                for hc in part:
                    act.wait_ge(q_ready, HC * g + hc + 1)
                    nc.scalar.copy(qT[:, g % 2, hc, :], qp[:, hc % 3, 0:GW]).then_inc(q_out, 1)

            def softmax_and_store(t):
                act.wait_ge(shifted, t + 1)
                nc.scalar.activation(bv[:, :, :], bv[:, :, :], ACT.Exp).then_inc(expd, 1)
                act.wait_ge(out_turned, t + 2)
                act.wait_ge(stored, 16 * t + 16)
                nc.scalar.copy(outT[:, :, :], tp[:, 0:3 * P].rearrange("p (c t) -> p c t", c=3)).then_inc(outT_ready, 1)
                act.wait_ge(outT_ready, t + 1)
                act.dma_start(d["route"][:, :, t * P:(t + 1) * P], outT[:, :, :]).then_inc(stored, 16)

            queries_out(0, range(HC))
            for t in range(NT):
                for b in range(4):
                    act.wait_ge(s_ready, 4 * t + b + 1)
                    act.wait_ge(found16, HC * t + HC)
                    nc.scalar.copy(sc[:, t % GT, 4 * b:4 * b + 4, :].rearrange("p h k -> p (h k)"), sp_[:, b, :]).then_inc(s_out, 1)
                if t:
                    softmax_and_store(t - 1)
                if t // GT + 1 < G:
                    queries_out(t // GT + 1, PARTS[t % GT])
            softmax_and_store(NT - 1)
            act.wait_ge(stored, 16 * NT + 16)

        @block.vector
        def _(dve):
            V = nc.vector
            dve.sem_inc(found16, GT * HC)
            dve.wait_ge(iota_set, 1)

            def take_wait():
                V.memset(mark[:, :], 0.0)

            def tile(t, u):
                dve.wait_ge(s_out, 4 * t + 4)
                take_wait()
                for h in range(HC):
                    V.max(tv[:, h // 2, h % 2, 0:8], sc[:, u, h, :]).then_inc(top8, 1)
                dve.wait_ge(top8, HC * t + HC)
                take_wait()
                for h in range(HC):
                    V.max_index(ti[:, h // 2, h % 2, 0:8], tv[:, h // 2, h % 2, 0:8], sc[:, u, h, :]).then_inc(found8, 1)
                dve.wait_ge(found8, HC * t + HC)
                take_wait()
                for h in range(HC):
                    V.match_replace(sc[:, u, h, :], tv[:, h // 2, h % 2, 0:8], sc[:, u, h, :], LOWEST).then_inc(cut8, 1)
                dve.wait_ge(cut8, HC * t + HC)
                take_wait()
                for h in range(HC):
                    V.max(tv[:, h // 2, h % 2, 8:16], sc[:, u, h, :]).then_inc(top16, 1)
                dve.wait_ge(top16, HC * t + HC)
                take_wait()
                for h in range(HC):
                    V.max_index(ti[:, h // 2, h % 2, 8:16], tv[:, h // 2, h % 2, 8:16], sc[:, u, h, :]).then_inc(found16, 1)
                V.tensor_tensor(cand[:, :, :, :],
                                tv[:, :, 0, :].rearrange("p h (a o) -> p h a o", o=1).broadcast_to([P, PH, TOPK, TOPK]),
                                tv[:, :, 1, :].rearrange("p h (o b) -> p h o b", o=1).broadcast_to([P, PH, TOPK, TOPK]),
                                ALU.add).then_inc(cand_ready, 1)
                dve.wait_ge(found16, HC * t + HC + GT * HC)
                V.tensor_copy(tf[:, :, :, :], ti[:, :, :, :]).then_inc(keyed, 1)
                dve.wait_ge(cand_ready, t + 1)
                take_wait()
                flat = lambda h: cand[:, h, :, :].rearrange("p a b -> p (a b)")
                for h in range(PH):
                    V.max(bv[:, h, 0:8], flat(h)).then_inc(best8, 1)
                dve.wait_ge(best8, PH * t + PH)
                take_wait()
                for h in range(PH):
                    V.max_index(bi[:, h, 0:8], bv[:, h, 0:8], flat(h)).then_inc(bfound8, 1)
                dve.wait_ge(bfound8, PH * t + PH)
                take_wait()
                for h in range(PH):
                    V.match_replace(flat(h), bv[:, h, 0:8], flat(h), LOWEST).then_inc(bcut8, 1)
                dve.wait_ge(bcut8, PH * t + PH)
                take_wait()
                for h in range(PH):
                    V.max(bv[:, h, 8:16], flat(h)).then_inc(best16, 1)
                dve.wait_ge(best16, PH * t + PH)
                take_wait()
                for h in range(PH):
                    V.max_index(bi[:, h, 8:16], bv[:, h, 8:16], flat(h)).then_inc(bfound16, 1)
                dve.wait_ge(bfound16, PH * t + PH)
                V.tensor_tensor(cand[:, :, 0, :], bv[:, :, :], bv[:, :, 0:1].broadcast_to([P, PH, TOPK]),
                                ALU.subtract).then_inc(split, 1)
                bi2 = bi[:, :, :].rearrange("p h k -> p (h k)")
                V.tensor_single_scalar(ab[:, 0, :], bi2, 4, ALU.logical_shift_right).then_inc(split, 1)
                V.tensor_single_scalar(ab[:, 1, :], bi2, 15, ALU.bitwise_and).then_inc(split, 1)
                dve.wait_ge(split, 3 * t + 3)
                V.tensor_copy(bv[:, :, :], cand[:, :, 0, :]).then_inc(shifted, 1)
                V.tensor_copy(abf[:, :, :], ab[:, :, :]).then_inc(ab_ready, 1)
                dve.wait_ge(ab_ready, t + 1)
                for c in range(2):
                    V.tensor_tensor(hit[:, c, :, :], abf[:, c, :].rearrange("p (s o) -> p s o", o=1).broadcast_to([P, SLOTS, TOPK]),
                                    iota16[:, :].rearrange("p (o a) -> p o a", o=1).broadcast_to([P, SLOTS, TOPK]),
                                    ALU.is_equal).then_inc(hit_ready, 1)
                dve.wait_ge(expd, t + 1)
                V.tensor_reduce(den[:, 0, :], bv[:, :, :], AX.X, ALU.add).then_inc(summed, 1)
                dve.wait_ge(summed, t + 1)
                V.reciprocal(den[:, 1, :], den[:, 0, :]).then_inc(recip, 1)
                dve.wait_ge(recip, t + 1)
                dve.wait_ge(out_turned, t + 1)
                V.tensor_tensor(out[:, 2, :].rearrange("p (h k) -> p h k", h=PH), bv[:, :, :],
                                den[:, 1, :].rearrange("p (h o) -> p h o", o=1).broadcast_to([P, PH, TOPK]), ALU.mult).then_inc(out_ready, 1)
                for c in range(2):
                    dve.wait_ge(picked, 2 * t + c + 1)
                    V.tensor_reduce(out[:, c, :], hit[:, c, :, :], AX.X, ALU.add).then_inc(out_ready, 1)

            with dve.Fori(0, G) as g:
                for u in range(GT):
                    tile(GT * g + u, u)

        @block.tensor
        def _(pe):
            pe.sem_inc(out_turned, 1)
            pe.wait_ge(const_in, 32)

            def queries(g, part):
                for hc in part:
                    if hc == 0:
                        pe.wait_ge(h2_in[g % 2], 16 * (g // 2) + 16)
                    if g == 0 and hc % 4 == 0:
                        pe.wait_ge(w_in, 4 * hc + 16)
                    after(pe, q_out, HC * g + hc - (2 if hc else 0))
                    for k in range(KD):
                        last = nc.tensor.matmul(qp[:, hc % 3, 0:GW], wq[:, k, hc * PK:(hc + 1) * PK], h2T[:, g % 2, k, :],
                                                start=(k == 0), stop=(k == KD - 1))
                    last.then_inc(q_ready, 1)

            def scores(t, u):
                for hc in range(HC):
                    if u == 0:
                        pe.wait_ge(q_out, HC * (t // GT) + hc + 1)
                    if hc % 4 == 0:
                        after(pe, s_out, 4 * t + hc // 4 - 3)
                    last = nc.tensor.matmul(sp_[:, hc // 4, (hc % 4) * PK:(hc % 4 + 1) * PK], qT[:, t // GT % 2, hc, u * P:(u + 1) * P],
                                            keys[:, hc, :], start=True, stop=True)
                    if hc % 4 == 3:
                        last.then_inc(s_ready, 1)

            def turn(t):
                pe.wait_ge(out_ready, 3 * t + 3)
                after(pe, outT_ready, t)
                for c in range(3):
                    last = nc.tensor.transpose(tp[:, c * P:(c + 1) * P], out[:, c, :], ident[:, :])
                last.then_inc(out_turned, 1)

            queries(0, range(HC))
            for t in range(NT):
                scores(t, t % GT)
                if t:
                    turn(t - 1)
                if t // GT + 1 < G:
                    queries(t // GT + 1, PARTS[t % GT])
            turn(NT - 1)


def spread(nc, d):
    B = 4
    S4 = 4
    with Stage(nc, "spr") as s:
        rt = s.sb("rt", [P, 3, TPAD])
        iota = s.sb("iota", [P, P])
        rows = s.sb("rows", [P, S4, B, P])
        cols = s.sb("cols", [P, S4, B, P])
        g = s.sb("g", [P, 2, PK, P])
        gp = s.pb("gp", [P, S4, B * P])
        rt_in, iota_set = s.sem("rt_in"), s.sem("iota_set")
        hot_ready, spread_ready, g_out = s.sem("hot_ready"), s.sem("spread_ready"), s.sem("g_out")
        g_stored = [s.sem("g_stored0"), s.sem("g_stored1")]
        FREE = S4
        steps = P // (B * S4)
        block = s.block()

        def tiles(eng, body):
            with eng.Fori(0, NP // 2) as pair:
                body(2 * pair, 0, pair, P)
                body(2 * pair + 1, 1, pair, P)
            body(NP, 0, NP // 2, DEC)

        @block.sync
        def _(sp):
            sp.dma_start(rt[:, :, :], d["route"]).then_inc(rt_in, 16)
            sp.sem_inc(g_stored[0], 16)
            sp.sem_inc(g_stored[1], 16)

            def body(t, slot, pair, n):
                sp.wait_ge(g_out, t * (P // B) + n // B + FREE)
                sp.dma_start(d["gates"].rearrange("j i t -> i j t")[:, :, at(t * P, n)],
                             g[:, slot, :, 0:n]).then_inc(g_stored[slot], 16)

            tiles(sp, body)
            sp.wait_ge(g_stored[0], 16 * (NP // 2 + 1) + 16)
            sp.wait_ge(g_stored[1], 16 * (NP // 2) + 16)

        @block.gpsimd
        def _(pool):
            nc.gpsimd.iota(iota[:, :], [[1, P]], base=0, channel_multiplier=0,
                           allow_small_or_imprecise_dtypes=True).then_inc(iota_set, 1)

        @block.vector
        def _(dve):
            dve.wait_ge(iota_set, 1)
            dve.wait_ge(rt_in, 16)

            def body(t, slot, pair, n):
                with dve.Fori(0, n // (B * S4)) as m:
                    for q in range(S4):
                        dve.wait_ge(spread_ready, t * (P // B) + m * S4 + q + 1)
                        for b in range(B):
                            tok = t * P + m * (B * S4) + q * B + b
                            nc.vector.tensor_scalar(rows[:, q, b, :], iota[:, :], rt[:, 0, at(tok, 1)], None, ALU.is_equal)
                            last = nc.vector.tensor_scalar(cols[:, q, b, :], iota[:, :], rt[:, 1, at(tok, 1)], rt[:, 2, at(tok, 1)],
                                                           ALU.is_equal, ALU.mult)
                        last.then_inc(hot_ready, 1)

            tiles(dve, body)

        @block.tensor
        def _(pe):
            pe.sem_inc(spread_ready, FREE)

            def body(t, slot, pair, n):
                with pe.Fori(0, n // (B * S4)) as m:
                    for q in range(S4):
                        pe.wait_ge(hot_ready, t * (P // B) + m * S4 + q + 1)
                        pe.wait_ge(g_out, t * (P // B) + m * S4 + q + 1)
                        for b in range(B):
                            last = nc.tensor.matmul(gp[:, q, b * P:(b + 1) * P], rows[:, q, b, :], cols[:, q, b, :],
                                                    start=True, stop=True)
                        last.then_inc(spread_ready, 1)

            tiles(pe, body)

        @block.scalar
        def _(act):
            act.sem_inc(g_out, FREE)

            def body(t, slot, pair, n):
                act.wait_ge(g_stored[slot], 16 * pair + 16)
                with act.Fori(0, n // (B * S4)) as m:
                    for q in range(S4):
                        act.wait_ge(spread_ready, t * (P // B) + m * S4 + q + 1 + FREE)
                        nc.scalar.copy(g[:, slot, :, at(m * (B * S4) + q * B, B)],
                                       gp[:, q, :].rearrange("p (t j) -> p j t", t=B)).then_inc(g_out, 1)

            tiles(act, body)


NJ = 4
NSB = PK // NJ
TG = [(0, 384), (384, 384), (768, 320)]


def experts(nc, d):
    NU, NV = NJ * len(TG), KD * len(TG)
    with Stage(nc, "exp") as s:
        h2T = s.sb("h2T", [P, KD, TOK])
        acc = s.sb("acc", [P, KD, TOK])
        u = s.sb("u", [P, 2, KD, NJ, P])
        v = s.sb("v", [P, 2, NJ, D])
        gt = s.sb("gt", [P, NJ, TOK])
        ge = s.sb("ge", [P, 4, 384])
        am = s.sb("am", [P, 2, NJ, TOK])
        up = s.pb("up", [P, 4, 512])
        vp = s.pb("vp", [P, 4, 512])
        y = s.sb("y", [P, 2, D])
        ident = s.sb("ident", [P, P])
        h2_in, zeroed, ident_in = s.sem("h2_in"), s.sem("zeroed"), s.sem("ident_in")
        x2_in, y_stored = [s.sem("x2_in0"), s.sem("x2_in1")], [s.sem("y_stored0"), s.sem("y_stored1")]
        y_turned, y_ready = s.sem("y_turned"), s.sem("y_ready")
        u_in = [s.sem("u_in0"), s.sem("u_in1")]
        v_in = [s.sem("v_in0"), s.sem("v_in1")]
        g_in = [s.sem(f"g_in{j}") for j in range(NJ)]
        up_ready, gelu_ready, act_ready = s.sem("up_ready"), s.sem("gelu_ready"), s.sem("act_ready")
        down_ready, added = s.sem("down_ready"), s.sem("added")
        U0, V0, F0 = 2 * NU, 2 * NV, 4
        block = s.block()

        @block.sync
        def _(sp):
            sp.sem_inc(act_ready, U0)
            sp.dma_start(ident[:, :], d["ident"]).then_inc(ident_in, 16)
            sp.dma_start(h2T[:, :, :], d["h2T"].rearrange("(k p) t -> p k t", p=P)[:, :, 0:TOK]).then_inc(h2_in, 16)

            def load(b, slot):
                sp.wait_ge(up_ready, NU * b + U0 - NU)
                sp.dma_start(u[:, slot, :, :, :], d["u"][at(b, 1), :, :, :, :].rearrange("o p k j i -> p (o k) j i")
                             ).then_inc(u_in[slot], 16)
                sp.wait_ge(down_ready, NV * b + V0 - NV)
                sp.dma_start(v[:, slot, :, :], d["v"].rearrange("(i n j) e -> n i j e", i=PK, j=NJ)[at(b, 1), :, :, :]
                             .rearrange("o i j e -> i (o j) e")).then_inc(v_in[slot], 16)
                for j in range(NJ):
                    sp.wait_ge(act_ready, NU * (b - 1) + U0 + 3 * j + 3)
                    sp.dma_start(gt[:, j, :], d["gates"][at(b * NJ + j, 1), :, :].rearrange("o i t -> i (o t)")
                                 ).then_inc(g_in[j], 16)

            with sp.Fori(0, NSB // 2) as pair:
                load(2 * pair, 0)
                load(2 * pair + 1, 1)
            for t in range(NT + 2):
                if t >= 2:
                    r, n = t - 2, min(P, TOK - (t - 2) * P)
                    sp.wait_ge(y_ready, 2 * r + 2)
                    sp.dma_start(d["yp"][r * P:r * P + n, :] if r < NP else d["ys"][:, :], y[0:n, r % 2, :]
                                 ).then_inc(y_stored[r % 2], 16)
                if t < NT:
                    n = min(P, TOK - t * P)
                    after(sp, y_stored[t % 2], 16 * (t // 2))
                    sp.dma_start(y[0:n, t % 2, :], d["x2"][t * P:t * P + n, :]).then_inc(x2_in[t % 2], 16)
            sp.wait_ge(y_stored[0], 16 * (NT - NT // 2))
            sp.wait_ge(y_stored[1], 16 * (NT // 2))

        @block.scalar
        def _(act):
            act.sem_inc(gelu_ready, F0)
            with act.Fori(0, NSB) as b:
                for n in range(NU):
                    w = TG[n % 3][1]
                    act.wait_ge(up_ready, NU * b + U0 + n + 1)
                    act.wait_ge(act_ready, NU * b + U0 + n + 1 - 4)
                    nc.scalar.activation(ge[:, n % 4, 0:w], up[:, n % 4, 0:w], ACT.Gelu).then_inc(gelu_ready, 1)

        @block.vector
        def _(dve):
            V = nc.vector
            V.memset(acc[:, :, :], 0.0).then_inc(zeroed, 1)
            dve.sem_inc(added, F0)
            dve.wait_ge(zeroed, 1)

            def gate(b, slot):
                dve.wait_ge(down_ready, NV * b + V0 - NV)
                for n in range(NU):
                    t0, w = TG[n % 3]
                    if n % 3 == 0:
                        dve.wait_ge(g_in[n // 3], 16 * b + 16)
                    dve.wait_ge(gelu_ready, NU * b + F0 + n + 1)
                    V.tensor_tensor(am[:, slot, n // 3, t0:t0 + w], ge[:, n % 4, 0:w], gt[:, n // 3, t0:t0 + w],
                                    ALU.mult).then_inc(act_ready, 1)

            def add(b):
                for n in range(NV):
                    t0, w = TG[n % 3]
                    dve.wait_ge(down_ready, NV * b + V0 + n + 1)
                    V.tensor_tensor(acc[:, n // 3, t0:t0 + w], acc[:, n // 3, t0:t0 + w], vp[:, n % 4, 0:w],
                                    ALU.add).then_inc(added, 1)

            gate(0, 0)
            with dve.Fori(0, NSB // 2 - 1) as pair:
                for o in range(2):
                    gate(2 * pair + 1 + o, (1 + o) % 2)
                    add(2 * pair + o)
            gate(NSB - 1, 1)
            add(NSB - 2)
            add(NSB - 1)
            for t in range(NT):
                n = min(P, TOK - t * P)
                dve.wait_ge(x2_in[t % 2], 16 * (t // 2) + 16)
                for c in range(2):
                    dve.wait_ge(y_turned, 2 * t + c + 1)
                    V.tensor_tensor(y[0:n, t % 2, c * 512:(c + 1) * 512], y[0:n, t % 2, c * 512:(c + 1) * 512],
                                    vp[0:n, 2 * (t % 2) + c, :], ALU.add).then_inc(y_ready, 1)

        @block.tensor
        def _(pe):
            pe.sem_inc(up_ready, U0)
            pe.sem_inc(down_ready, V0)
            pe.wait_ge(h2_in, 16)

            def up_block(b, slot, half):
                pe.wait_ge(u_in[slot], 16 * half + 16)
                for n in range(NU):
                    t0, w = TG[n % 3]
                    pe.wait_ge(gelu_ready, NU * b + n + 1)
                    for k in range(KD):
                        last = nc.tensor.matmul(up[:, n % 4, 0:w], u[:, slot, k, n // 3, :], h2T[:, k, t0:t0 + w],
                                                start=(k == 0), stop=(k == KD - 1))
                    last.then_inc(up_ready, 1)

            def down_block(b, slot, half):
                pe.wait_ge(v_in[slot], 16 * half + 16)
                pe.wait_ge(act_ready, NU * b + U0 + NU)
                for n in range(NV):
                    t0, w = TG[n % 3]
                    pe.wait_ge(added, NV * b + n + 1)
                    for j in range(NJ):
                        last = nc.tensor.matmul(vp[:, n % 4, 0:w], v[:, slot, j, (n // 3) * P:(n // 3 + 1) * P],
                                                am[:, slot, j, t0:t0 + w], start=(j == 0), stop=(j == NJ - 1))
                    last.then_inc(down_ready, 1)

            up_block(0, 0, 0)
            with pe.Fori(0, NSB // 2 - 1) as pair:
                up_block(2 * pair + 1, 1, pair)
                down_block(2 * pair, 0, pair)
                up_block(2 * pair + 2, 0, pair + 1)
                down_block(2 * pair + 1, 1, pair)
            up_block(NSB - 1, 1, NSB // 2 - 1)
            down_block(NSB - 2, 0, NSB // 2 - 1)
            down_block(NSB - 1, 1, NSB // 2 - 1)
            pe.wait_ge(ident_in, 16)
            pe.wait_ge(added, NV * NSB + F0)
            for t in range(NT):
                n = min(P, TOK - t * P)
                after(pe, y_ready, 2 * (t - 2) + 2)
                for c in range(2):
                    for k in range(4):
                        last = nc.tensor.transpose(vp[0:n, 2 * (t % 2) + c, k * P:(k + 1) * P],
                                                   acc[:, 4 * c + k, t * P:t * P + n], ident[:, :])
                    last.then_inc(y_turned, 1)


def consts():
    f = np.float32
    half = RD // 2
    pos = np.concatenate([np.arange(SEQ), PAST + np.arange(DEC), np.zeros(TPAD - TOK)]).astype(f)
    inv = f(10000.0) ** (-np.arange(half, dtype=f) / f(half))
    ang = pos[:, None] * inv[None, :]
    g = np.array([1.0 - 2.0 ** (-5.0 - h) for h in range(RH)])
    m, l = np.arange(P)[:, None], np.arange(P)[None, :]
    decay = np.where((l >= m)[:, None, :], g[None, :, None] ** np.maximum(l - m, 0)[:, None, :], 0.0)
    q_dec = np.broadcast_to(g[None, :, None] ** (np.arange(P) + 1.0)[None, None, :], (P, RH, P))
    j = np.arange(P)[:, None]
    k_dec = np.stack([g ** (P - 1.0 - j) * KSCALE,
                      np.where(j < DEC, g ** np.maximum(DEC - 1.0 - j, 0), 0.0) * KSCALE], axis=1)
    return {"ident": np.eye(P, dtype=f), "flip": np.eye(P, dtype=f)[::-1], "cs": np.stack([np.cos(ang), np.sin(ang)], axis=1),
            "decay": decay.astype(f), "q_dec": q_dec.astype(f), "k_dec": k_dec.astype(f)}


def layout(a):
    rel = np.pad(a["attn_rel_bias"][0], ((0, 0), (BAND + P - 1 - CLIP, BAND + P - 1 - CLIP)), mode="edge")[:, ::-1]
    rel = rel[:, :P - 1 + BAND + P]
    u = a["peer_expert_u"][0].reshape(PK, PK // NJ, NJ, KD, P)
    return {
        "x": np.concatenate([a["x_prompt"][0], a["x_sample"][0], np.zeros((TPAD - TOK, D), np.float32)]),
        "ck": a["cache_attn_k"][0, 0].reshape(P, AW), "cv": a["cache_attn_v"][0, 0].reshape(P, AW),
        "state": a["state_retention"][0, 0], "mix_g": a["mix_norm_g"][0], "w_in": a["w_in"][0],
        "q_g": a["attn_q_norm_g"][0], "k_g": a["attn_k_norm_g"][0], "rel": rel,
        "r_g": a["ret_out_norm_g"][0].reshape(RW), "w_a": a["w_branch_attn"][0], "w_r": a["w_branch_ret"][0],
        "w_o": a["w_out"][0], "f_g": a["ffn_norm_g"][0], "w_q": a["peer_w_query"][0],
        "keys": a["peer_sub_keys"][0].reshape(HC, PK, P).transpose(2, 0, 1),
        "u": u.transpose(1, 4, 3, 2, 0),
        "v": a["peer_expert_v"][0],
    }


def program(nc, d):
    for name, shape in (("z", (TPAD, ZW)), ("x2", (TPAD, D)), ("h2T", (D, TPAD)), ("route", (P, 3, TPAD)),
                        ("gates", (PK, PK, TOK))):
        d[name] = nc.dram_tensor(f"scratch_{name}", shape, F32, kind="Internal").ap()
    project(nc, d)
    mix(nc, d)
    route(nc, d)
    spread(nc, d)
    experts(nc, d)


OUTPUTS = {"yp": ((SEQ, D), (1, SEQ, D)), "ys": ((DEC, D), (1, DEC, D)),
           "nkp": ((BAND, AW), (1, 1, BAND, AH, AD)), "nvp": ((BAND, AW), (1, 1, BAND, AH, AD)),
           "nsp": ((RH, RD, RD), (1, 1, RH, RD, RD)),
           "nks": ((DEC, AW), (1, 1, DEC, AH, AD)), "nvs": ((DEC, AW), (1, 1, DEC, AH, AD)),
           "nss": ((RH, RD, RD), (1, 1, RH, RD, RD))}


def kernel(**inputs):
    import concourse.bacc as bacc
    from concourse.bass_utils import run_bass_kernel_spmd

    nc = bacc.Bacc("TRN2", target_bir_lowering=False, num_devices=1)
    arrays, d = {}, {}
    for name, a in {**consts(), **layout({k: np.asarray(v) for k, v in inputs.items()})}.items():
        arrays[f"in_{name}"] = np.ascontiguousarray(a)
        d[name] = nc.dram_tensor(f"in_{name}", a.shape, mybir.dt.from_np(a.dtype), kind="ExternalInput").ap()
    for name, (shape, _) in OUTPUTS.items():
        d[name] = nc.dram_tensor(f"out_{name}", shape, F32, kind="ExternalOutput").ap()
    program(nc, d)
    r = run_bass_kernel_spmd(nc, [arrays], core_ids=[0])
    return tuple(r.results[0][f"out_{name}"].reshape(shape) for name, (_, shape) in OUTPUTS.items())
```

```python
import math
from contextlib import ExitStack

import numpy as np

import concourse.bass as bass
from concourse import mybir

F32 = mybir.dt.float32
U32 = mybir.dt.uint32
ALU = mybir.AluOpType
ACT = mybir.ActivationFunctionType
AX = mybir.AxisListType

P = 128
D = 1024
KD = D // P
SEQ, DEC, PAST = 1024, 64, 128
NP = SEQ // P
NT = NP + 1
TOK = SEQ + DEC
TPAD = NT * P
EPS = 1e-6
AH, AD = 8, 64
AW = AH * AD
BAND = 512
BT = BAND // P
CLIP = 128
MASK = -1e30
RH, RD = 4, 128
RW = RH * RD
ZW = 3 * AW + 4 * RW + 2 * D
O_A, O_R, O_G = 0, 3 * AW, 3 * AW + 4 * RW
KSCALE = float(RD) ** -0.5
PH, PK, TOPK = 8, 128, 16
HC = 2 * PH
SLOTS = PH * TOPK
CAND = TOPK * TOPK
LOWEST = -3.0e38
CHUNK = 64


def at(start, size):
    return slice(start, start + size) if isinstance(start, int) else bass.ds(start, size)


def after(eng, sem, value):
    if not isinstance(value, int) or value > 0:
        eng.wait_ge(sem, value)


def across(row, parts=P):
    return bass.AP(row.tensor, row.offset, [[0, parts]] + [list(x) for x in row.ap])


class Stage:

    def __init__(self, nc, name):
        self.nc, self.name, self.ctx, self.sems = nc, name, ExitStack(), []

    def __enter__(self):
        self.ctx.__enter__()
        return self

    def __exit__(self, *e):
        self.ctx.__exit__(*e)
        self.nc.clear_and_free_semaphores(self.sems)
        self.nc.all_engine_barrier()

    def sb(self, name, shape, dt=F32):
        return self.ctx.enter_context(self.nc.sbuf_tensor(f"{self.name}_{name}", shape, dt))

    def pb(self, name, shape):
        return self.ctx.enter_context(self.nc.psum_tensor(f"{self.name}_{name}", shape, F32))

    def sem(self, name):
        self.sems.append(self.nc.alloc_semaphore(name=f"{self.name}_{name}"))
        return self.sems[-1]

    def block(self):
        return self.ctx.enter_context(self.nc.Block())


def project(nc, d):
    NB = ZW // 512
    with Stage(nc, "prj") as s:
        x = s.sb("x", [P, NT, D])
        sq = s.sb("sq", [P, D])
        gain = s.sb("gain", [P, D])
        ident = s.sb("ident", [P, P])
        half = s.sb("half", [P, NT])
        ms = s.sb("ms", [P, NT])
        rs = s.sb("rs", [P, NT])
        h = s.sb("h", [P, 3, D])
        hT = s.sb("hT", [P, KD, TPAD])
        w = s.sb("w", [P, 2, KD, 512])
        zo = s.sb("zo", [P, NT, 512])
        tp = s.pb("tp", [P, 3, 512])
        zp = s.pb("zp", [P, 5, 512])
        x_in, gain_in, ident_in = s.sem("x_in"), s.sem("gain_in"), s.sem("ident_in")
        w_in = [[s.sem(f"w_in{slot}_{k}") for k in range(0, KD, 2)] for slot in range(2)]
        half_set, squared, mean_ready, rs_ready = s.sem("half_set"), s.sem("squared"), s.sem("mean_ready"), s.sem("rs_ready")
        h_ready, turned, turned_out = s.sem("h_ready"), s.sem("turned"), s.sem("turned_out")
        z_ready, z_out = s.sem("z_ready"), s.sem("z_out")
        z_stored = [s.sem(f"z_stored{n}") for n in range(3)]
        TURNED0, TOUT0, Z0 = 6, 3, 2 * NT
        ZOUT0 = NT
        bank = lambda i: 4 if i == 8 else i % 4
        block = s.block()

        @block.sync
        def _(sp):
            sp.dma_start(ident[:, :], d["ident"]).then_inc(ident_in, 16)
            sp.dma_start(gain[:, :], across(d["mix_g"])).then_inc(gain_in, 16)
            sp.dma_start(x[:, :, :], d["x"].rearrange("(n p) c -> p n c", p=P)).then_inc(x_in, 16)
            w_v = d["w_in"].rearrange("(k p) n -> p k n", p=P)

            def load(b, slot):
                sp.wait_ge(z_ready, NT * b + Z0 - NT)
                for k in range(0, KD, 2):
                    sp.dma_start(w[:, slot, k:k + 2, :], w_v[:, k:k + 2, at(b * 512, 512)]
                                 ).then_inc(w_in[slot][k // 2], 16)

            with sp.Fori(0, NB // 2) as pair:
                load(2 * pair, 0)
                load(2 * pair + 1, 1)
            load(NB - 1, 0)

        @block.gpsimd
        def _(pool):
            nc.gpsimd.memset(half[:, :], -0.5).then_inc(half_set, 1)
            pool.wait_ge(half_set, 1)
            pool.wait_ge(mean_ready, 1)
            nc.gpsimd.tensor_tensor(rs[:, :], ms[:, :], half[:, :], ALU.pow).then_inc(rs_ready, 1)

        @block.scalar
        def _(act):
            act.wait_ge(x_in, 16)
            with act.Fori(0, NT) as i:
                nc.scalar.activation(sq[:, :], x[:, i, :], ACT.Square, accum_out=ms[:, at(i, 1)]).then_inc(squared, 1)
                act.wait_ge(squared, i + 1)
            act.sem_inc(turned_out, TOUT0)
            act.sem_inc(z_out, ZOUT0)
            for g in range(3):
                act.sem_inc(z_stored[g], 16)
            z_v = d["z"].rearrange("(n p) c -> p n c", p=P)
            with act.Fori(0, 3) as g:
                for u in range(6):
                    act.wait_ge(turned, 6 * g + TURNED0 + u + 1)
                    nc.scalar.copy(hT[:, 4 * (u % 2):4 * (u % 2) + 4, at((3 * g + u // 2) * P, P)],
                                   tp[:, u % 3, :].rearrange("p (k t) -> p k t", k=4)).then_inc(turned_out, 1)
            with act.Fori(0, NB) as b:
                for i in range(NT):
                    act.wait_ge(z_ready, NT * b + Z0 + i + 1)
                    act.wait_ge(z_stored[i // 3], 16 * b + 16)
                    nc.scalar.copy(zo[:, i, :], zp[:, bank(i), :]).then_inc(z_out, 1)
                    if i % 3 == 2:
                        act.wait_ge(z_out, NT * b + ZOUT0 + i + 1)
                        act.dma_start(z_v[:, i - 2:i + 1, at(b * 512, 512)],
                                      zo[:, i - 2:i + 1, :]).then_inc(z_stored[i // 3], 16)
            for g in range(3):
                act.wait_ge(z_stored[g], 16 * NB + 16)

        @block.vector
        def _(dve):
            dve.wait_ge(squared, NT)
            nc.vector.tensor_scalar(ms[:, :], ms[:, :], 1.0 / D, EPS, ALU.mult, ALU.add).then_inc(mean_ready, 1)
            dve.wait_ge(gain_in, 16)
            dve.wait_ge(rs_ready, 1)
            with dve.Fori(0, 3) as g:
                for u in range(3):
                    dve.wait_ge(turned, 6 * g + TURNED0 + 2 * u - 4)
                    nc.vector.scalar_tensor_tensor(out=h[:, u, :], in0=x[:, 3 * g + u, :], scalar=rs[:, at(3 * g + u, 1)],
                                                   in1=gain[:, :], op0=ALU.mult, op1=ALU.mult).then_inc(h_ready, 1)

        @block.tensor
        def _(pe):
            pe.sem_inc(turned, TURNED0)
            pe.sem_inc(z_ready, Z0)
            pe.wait_ge(ident_in, 16)
            with pe.Fori(0, 3) as g:
                for u in range(6):
                    pe.wait_ge(h_ready, 3 * g + u // 2 + 1)
                    pe.wait_ge(turned_out, 6 * g + u + 1)
                    for k in range(4):
                        last = nc.tensor.transpose(tp[:, u % 3, k * P:(k + 1) * P],
                                                   h[:, u // 2, (4 * (u % 2) + k) * P:(4 * (u % 2) + k + 1) * P], ident[:, :])
                    last.then_inc(turned, 1)
            pe.wait_ge(turned_out, 2 * NT + TOUT0)

            def multiply(b, pair, slot):
                for i in range(NT):
                    before = i + 4 - NT if i < 4 else i - 4 if i < 8 else -1
                    pe.wait_ge(z_out, NT * b + ZOUT0 + before + 1)
                    for k in range(KD):
                        if i == 0 and k % 2 == 0:
                            pe.wait_ge(w_in[slot][k // 2], 16 * pair + 16)
                        last = nc.tensor.matmul(zp[:, bank(i), :], hT[:, k, i * P:(i + 1) * P],
                                                w[:, slot, k, :], start=(k == 0), stop=(k == KD - 1))
                    last.then_inc(z_ready, 1)

            with pe.Fori(0, NB // 2) as pair:
                multiply(2 * pair, pair, 0)
                multiply(2 * pair + 1, pair, 1)
            multiply(NB - 1, NB // 2, 0)


def gammas():
    return [1.0 - 2.0 ** (-5.0 - h) for h in range(RH)]


def mix(nc, d):
    with Stage(nc, "mix") as s:
        w_a = s.sb("w_a", [P, AW // P, D])
        w_r = s.sb("w_r", [P, RW // P, D])
        w_o = s.sb("w_o", [P, KD, D])
        ident = s.sb("ident", [P, P])
        bias8 = s.sb("bias8", [P, AH, (BT + 1) * P])
        keysT = s.sb("keysT", [P, AH // 2, NP * P])
        vals = s.sb("vals", [P, NP, AW])
        qpad = s.sb("qpad", [P, AH, P])
        za = s.sb("za", [P, 3 * AW])
        zr = s.sb("zr", [P, 4 * RW])
        zg = s.sb("zg", [P, 2 * D])
        x = s.sb("x", [P, D])
        cs = s.sb("cs", [P, 2, RD // 2])
        sq = s.sb("sq", [P, 2 * AW])
        qk = s.sb("qk", [P, 2 * AW])
        g_qk = s.sb("g_qk", [P, 2, AD])
        g_r = s.sb("g_r", [P, RW])
        g_f = s.sb("g_f", [P, D])
        part = s.sb("part", [P, 2, 2 * RH, RD // 2])
        rot = s.sb("rot", [P, 2 * RH, RD])
        rqT = s.sb("rqT", [P, RH, P])
        rqdT = s.sb("rqdT", [P, RH, P])
        rkT = s.sb("rkT", [P, RH, P])
        inner = s.sb("inner", [P, RH, P])
        decay = s.sb("decay", [P, RH, P])
        q_dec = s.sb("q_dec", [P, RH, P])
        k_dec = s.sb("k_dec", [P, 2, RH])
        state = s.sb("state", [P, 2, RH, RD])
        ro = s.sb("ro", [P, RW])
        r_gate = s.sb("r_gate", [P, RW])
        sc = s.sb("sc", [P, 2, (BT + 1) * P])
        pT = s.sb("pT", [P, 2, BT + 1, P])
        oa = s.sb("oa", [P, AW])
        tT = s.sb("tT", [P, KD, P])
        half = s.sb("half", [P, 16])
        qk_ms, qk_rs = s.sb("qk_ms", [P, 16]), s.sb("qk_rs", [P, 16])
        r_ms, r_rs = s.sb("r_ms", [P, RH]), s.sb("r_rs", [P, RH])
        f_ms, f_rs = s.sb("f_ms", [P, 1]), s.sb("f_rs", [P, 1])
        neg_max, den, rden = s.sb("neg_max", [P, AH]), s.sb("den", [P, AH]), s.sb("rden", [P, AH])
        S = s.pb("S", [P, 2, 1024])
        T = s.pb("T", [P, 2, 512])
        OM = s.pb("OM", [P, 2, 512])
        O, M = OM[:, 0, :], OM[:, 1, :]
        heads4 = lambda ap: ap.rearrange("p (h e) -> p h e", h=RH)

        BW = (BT + 1) * P
        mark = s.sb("mark", [P, AH])
        flip = s.sb("flip", [P, P])
        bias_rev = w_o[:, :, :].rearrange("p k n -> p (k n)")[:, 0:AH * BW].rearrange("p (h n) -> p h n", h=AH)
        names = """ident_in bias_turned w_in bias_in const_in cache_in za_in zr_in zg_in x_in state_in
            bias_set zeros_set halves_set
            qk_squared qk_summed qk_mean qk_rs_ready qk_scaled qk_ready v_ready
            q_turned k_turned q_padded keys_ready cache_turned
            rot_part rotated rq_turned rk_turned rq_ready rqd_ready rk_ready k_decayed
            inner_ready inner_scaled ret_ready ret_out update_ready state_ready
            r_squared r_summed r_mean r_rs_ready r_scaled r_exp r_plus r_silu r_gained r_ready
            scores_ready softmax_in p_ready p_turned p_out o_ready den_ready oa_ready
            oa_turned r_turned oa_out r_out gate_exp gate_plus gates_ready
            branch_ready gated merged m_turned m_out proj_ready x2_ready
            f_squared f_mean f_rs_ready h2_ready h2_turned h2_out
            k_stored v_stored x2_stored h2_stored state_stored""".split()
        (ident_in, bias_turned, w_in, bias_in, const_in, cache_in, za_in, zr_in, zg_in, x_in, state_in,
         bias_set, zeros_set, halves_set,
         qk_squared, qk_summed, qk_mean, qk_rs_ready, qk_scaled, qk_ready, v_ready,
         q_turned, k_turned, q_padded, keys_ready, cache_turned,
         rot_part, rotated, rq_turned, rk_turned, rq_ready, rqd_ready, rk_ready, k_decayed,
         inner_ready, inner_scaled, ret_ready, ret_out, update_ready, state_ready,
         r_squared, r_summed, r_mean, r_rs_ready, r_scaled, r_exp, r_plus, r_silu, r_gained, r_ready,
         scores_ready, softmax_in, p_ready, p_turned, p_out, o_ready, den_ready, oa_ready,
         oa_turned, r_turned, oa_out, r_out, gate_exp, gate_plus, gates_ready,
         branch_ready, gated, merged, m_turned, m_out, proj_ready, x2_ready,
         f_squared, f_mean, f_rs_ready, h2_ready, h2_turned, h2_out,
         k_stored, v_stored, x2_stored, h2_stored, state_stored) = [s.sem(n) for n in names]
        block = s.block()

        def tiles(eng, body):
            for i in range(BT):
                body(i, i)
            with eng.Fori(BT, NP) as i:
                body(i, BT)
            body(NP, 1)

        @block.sync
        def _(sp):
            sp.sem_inc(k_stored, 16)
            sp.dma_start(ident[:, :], d["ident"]).then_inc(ident_in, 16)
            sp.dma_start(flip[:, :], d["flip"]).then_inc(ident_in, 16)
            rel = d["rel"]
            sp.dma_start(bias_rev, bass.AP(rel.tensor, rel.offset, [[1, P], [rel.shape[1], AH], [1, BW]])).then_inc(bias_in, 16)
            for out, src in ((g_qk[:, 0, :], across(d["q_g"])), (g_qk[:, 1, :], across(d["k_g"])),
                             (g_r[:, :], across(d["r_g"])), (g_f[:, :], across(d["f_g"])),
                             (decay[:, :, :], d["decay"]), (q_dec[:, :, :], d["q_dec"]), (k_dec[:, :, :], d["k_dec"])):
                sp.dma_start(out, src).then_inc(const_in, 16)
            sp.dma_start(state[:, 1, :, :], d["state"].rearrange("h d e -> d h e")).then_inc(state_in, 16)

            def body(i, past):
                row = i * P if isinstance(i, int) else sp.snap((i - BT) * P)
                after(sp, qk_scaled, i)
                after(sp, v_ready, i)
                after(sp, qk_squared, i)
                sp.dma_start(za[:, :], d["z"][at(i * P, P), O_A:O_R]).then_inc(za_in, 16)
                after(sp, rotated, i)
                after(sp, update_ready, i)
                after(sp, r_ready, i)
                sp.dma_start(zr[:, :], d["z"][at(i * P, P), O_R:O_G]).then_inc(zr_in, 16)
                sp.dma_start(cs[:, :, :], d["cs"][at(i * P, P), :, :]).then_inc(zr_in, 16)
                after(sp, h2_turned, 2 * i)
                after(sp, merged, i)
                sp.dma_start(zg[:, :], d["z"][at(i * P, P), O_G:ZW]).then_inc(zg_in, 16)
                after(sp, x2_stored, 16 * i)
                after(sp, f_squared, i)
                after(sp, h2_ready, i)
                sp.dma_start(x[:, :], d["x"][at(i * P, P), :]).then_inc(x_in, 16)
                if isinstance(i, int) and i == 0:
                        for k in range(2):
                            sp.dma_start(w_a[:, 2 * k:2 * k + 2, :], d["w_a"].rearrange("(k p) n -> p k n", p=P)[:, 2 * k:2 * k + 2, :]).then_inc(w_in, 16)
                            sp.dma_start(w_r[:, 2 * k:2 * k + 2, :], d["w_r"].rearrange("(k p) n -> p k n", p=P)[:, 2 * k:2 * k + 2, :]).then_inc(w_in, 16)
                        sp.wait_ge(bias_set, AH)
                        sp.dma_start(w_o[:, :, :], d["w_o"].rearrange("(k p) n -> p k n", p=P)).then_inc(w_in, 16)
                if not isinstance(i, int) or i == NP:
                    kd, vd, n = ((d["nks"], d["nvs"], DEC) if isinstance(i, int) else
                                 (d["nkp"][at(row, P), :], d["nvp"][at(row, P), :], P))
                    slot = 1 if isinstance(i, int) else i
                    sp.wait_ge(qk_ready, i + 1)
                    sp.dma_start(kd, qk[0:n, AW:2 * AW]).then_inc(k_stored, 16)
                    sp.wait_ge(v_ready, i + 1)
                    sp.dma_start(vd, vals[0:n, slot, :]).then_inc(v_stored, 16)

            for i in range(BT):
                body(i, i)
            with sp.Fori(BT, NP) as i:
                body(i, BT)
            sp.wait_ge(o_ready, AH * NP)
            sp.wait_ge(k_turned, NP)
            sp.wait_ge(k_stored, 16 * (NP - BT) + 16)
            sp.dma_start(qk[:, AW:2 * AW], d["ck"]).then_inc(cache_in, 16)
            sp.dma_start(vals[:, 0, :], d["cv"]).then_inc(cache_in, 16)
            body(NP, 1)
            sp.wait_ge(state_ready, RH * NP)
            sp.dma_start(d["nsp"].rearrange("h d e -> d h e"), state[:, 0, :, :]).then_inc(state_stored, 16)
            sp.wait_ge(state_ready, RH * NT)
            sp.dma_start(d["nss"].rearrange("h d e -> d h e"), state[:, 1, :, :]).then_inc(state_stored, 16)
            sp.wait_ge(state_stored, 32)
            sp.wait_ge(k_stored, 16 * (NP - BT + 1) + 16)
            sp.wait_ge(v_stored, 16 * (NP - BT + 1))

        @block.gpsimd
        def _(pool):
            nc.gpsimd.memset(half[:, :], -0.5).then_inc(halves_set, 1)
            pool.wait_ge(halves_set, 1)
            nc.gpsimd.memset(qpad[:, :, :], 0.0).then_inc(zeros_set, 1)
            nc.gpsimd.memset(state[:, 0, :, :], 0.0).then_inc(zeros_set, 1)
            pool.wait_ge(const_in, 7 * 16)

            def body(i, past):
                sample = isinstance(i, int) and i == NP
                slot = 1 if sample else i
                pool.wait_ge(za_in, 16 * i + 16)
                after(pool, f_squared, i)
                nc.gpsimd.tensor_tensor(sq[:, :], za[:, 0:2 * AW], za[:, 0:2 * AW], ALU.mult).then_inc(qk_squared, 1)
                nc.gpsimd.tensor_copy(vals[:, slot, :], za[:, 2 * AW:3 * AW]).then_inc(v_ready, 1)
                pool.wait_ge(zr_in, 32 * i + 32)
                after(pool, rq_turned, i)
                after(pool, update_ready, i)
                zqk = zr[:, 0:2 * RW].rearrange("p (h c e) -> p h c e", h=2 * RH, c=2)
                x1, x2_ = zqk[:, :, 0, :], zqk[:, :, 1, :]
                cos = cs[:, 0:1, :].broadcast_to([P, 2 * RH, RD // 2])
                sin = cs[:, 1:2, :].broadcast_to([P, 2 * RH, RD // 2])
                for n, (a, ta, b, tb, op, out) in enumerate(((x1, cos, x2_, sin, ALU.subtract, rot[:, :, 0:RD // 2]),
                                                             (x1, sin, x2_, cos, ALU.add, rot[:, :, RD // 2:RD]))):
                    nc.gpsimd.tensor_tensor(part[:, 0, :, :], a, ta, ALU.mult).then_inc(rot_part, 1)
                    nc.gpsimd.tensor_tensor(part[:, 1, :, :], b, tb, ALU.mult).then_inc(rot_part, 1)
                    pool.wait_ge(rot_part, 5 * i + 3 * n + 2)
                    nc.gpsimd.tensor_tensor(out, part[:, 0, :, :], part[:, 1, :, :], op).then_inc(
                        rot_part if n == 0 else rotated, 1)
                    if n == 0:
                        pool.wait_ge(rot_part, 5 * i + 3)
                pool.wait_ge(qk_mean, i + 1)
                nc.gpsimd.tensor_tensor(qk_rs[:, :], qk_ms[:, :], half[:, :], ALU.pow).then_inc(qk_rs_ready, 1)
                pool.wait_ge(rotated, i + 1)
                pool.wait_ge(rk_turned, i + 1)
                kdec = k_dec[:, 1 if sample else 0, :].rearrange("p (h o) -> p h o", o=1).broadcast_to([P, RH, RD])
                nc.gpsimd.tensor_tensor(rot[:, RH:, :], rot[:, RH:, :], kdec, ALU.mult).then_inc(k_decayed, 1)
                pool.wait_ge(ret_out, i + 1)
                pool.wait_ge(qk_summed, i + 1)
                nc.gpsimd.tensor_tensor(sq[:, 0:RW], ro[:, :], ro[:, :], ALU.mult).then_inc(r_squared, 1)
                pool.wait_ge(r_mean, i + 1)
                nc.gpsimd.tensor_tensor(r_rs[:, :], r_ms[:, :], half[:, 0:RH], ALU.pow).then_inc(r_rs_ready, 1)
                pool.wait_ge(f_mean, i + 1)
                nc.gpsimd.tensor_tensor(f_rs[:, :], f_ms[:, :], half[:, 0:1], ALU.pow).then_inc(f_rs_ready, 1)

            tiles(pool, body)

        @block.scalar
        def _(act):
            def body(i, past):
                sample = isinstance(i, int) and i == NP
                slot = 1 if sample else i
                if sample:
                    act.wait_ge(cache_turned, 1)
                    nc.scalar.copy(keysT[:, :, 0:P], T[:, 1, :].rearrange("p (k t) -> p k t", k=4)).then_inc(keys_ready, 1)
                act.wait_ge(zr_in, 32 * i + 32)
                after(act, r_ready, i)
                nc.scalar.activation(r_gate[:, :], zr[:, 3 * RW:4 * RW], ACT.Exp, scale=-1.0).then_inc(r_exp, 1)
                act.wait_ge(q_turned, i + 1)
                act.wait_ge(zeros_set, 2)
                for odd in range(2):
                    rows = slice(64 * odd, 64 * odd + 64)
                    nc.scalar.copy(qpad[rows, odd:AH:2, :],
                                   T[rows, 0, :].rearrange("p (k t) -> p k t", k=4)).then_inc(q_padded, 1)
                act.wait_ge(k_turned, i + 1)
                nc.scalar.copy(keysT[:, :, at(slot * P, P)],
                               T[:, 1, :].rearrange("p (k t) -> p k t", k=4)).then_inc(keys_ready, 1)
                act.wait_ge(rq_turned, i + 1)
                nc.scalar.copy(rqT[:, :, :], heads4(O)).then_inc(rq_ready, 1)
                act.wait_ge(rk_turned, i + 1)
                nc.scalar.activation(rkT[:, :, :], heads4(M), ACT.Copy, scale=KSCALE).then_inc(rk_ready, 1)
                act.wait_ge(zg_in, 16 * i + 16)
                nc.scalar.activation(zg[:, :], zg[:, :], ACT.Exp, scale=-1.0).then_inc(gate_exp, 1)
                act.wait_ge(ret_ready, i + 1)
                after(act, r_turned, i)
                nc.scalar.copy(ro[:, :], O).then_inc(ret_out, 1)
                for h in range(AH):
                    W = (past + 1) * P if not sample else P + DEC
                    act.wait_ge(softmax_in, AH * i + h + 1)
                    nc.scalar.activation(sc[:, h % 2, 0:W], sc[:, h % 2, 0:W], ACT.Exp, scale=-1.0,
                                         bias=neg_max[:, h:h + 1], accum_out=den[:, h:h + 1]).then_inc(p_ready, 1)
                    act.wait_ge(p_turned, AH * i + h + 1)
                    after(act, o_ready, AH * i + h - 1)
                    if sample:
                        nc.scalar.copy(pT[:, h % 2, 0, :], T[:, 0, 0:P])
                        nc.scalar.copy(pT[0:DEC, h % 2, 1, :], T[0:DEC, 0, P:2 * P]).then_inc(p_out, 1)
                    else:
                        nc.scalar.copy(pT[:, h % 2, 0:past + 1, :].rearrange("p k t -> p (k t)"),
                                       T[:, :, :].rearrange("p b n -> p (b n)")[:, 0:W]).then_inc(p_out, 1)
                act.wait_ge(r_turned, i + 1)
                after(act, h2_stored, 16 * i)
                nc.scalar.copy(tT[:, 4:8, :], T[:, 0, :].rearrange("p (k t) -> p k t", k=4)).then_inc(r_out, 1)
                act.wait_ge(oa_turned, i + 1)
                nc.scalar.copy(tT[:, 0:4, :], T[:, 1, :].rearrange("p (k t) -> p k t", k=4)).then_inc(oa_out, 1)
                for b in range(2):
                    act.wait_ge(m_turned, 2 * i + b + 1)
                    nc.scalar.copy(tT[:, 4 * b:4 * b + 4, :], T[:, b, :].rearrange("p (k t) -> p k t", k=4)).then_inc(m_out, 1)
                act.wait_ge(x2_ready, i + 1)
                act.dma_start(d["x2"][at(i * P, P), :], x[:, :]).then_inc(x2_stored, 16)
                for b in range(2):
                    act.wait_ge(h2_turned, 2 * i + b + 1)
                    nc.scalar.copy(tT[:, 4 * b:4 * b + 4, :], T[:, b, :].rearrange("p (k t) -> p k t", k=4)).then_inc(h2_out, 1)
                act.wait_ge(h2_out, 2 * i + 2)
                act.dma_start(d["h2T"].rearrange("(k p) t -> p k t", p=P)[:, :, at(i * P, P)], tT[:, :, :]).then_inc(h2_stored, 16)

            tiles(act, body)
            act.wait_ge(x2_stored, 16 * NT)
            act.wait_ge(h2_stored, 16 * NT)

        @block.vector
        def _(dve):
            V = nc.vector
            for h in range(AH):
                dve.wait_ge(bias_turned, h + 1)
                V.tensor_scalar(bias8[:, h, :], S[:, h % 2, 0:BW], float(AD) ** 0.5, None, ALU.mult).then_inc(bias_set, 1)
            dve.wait_ge(bias_set, AH)
            V.memset(bias8[0:64, :, BAND + CHUNK:BAND + P], 8 * MASK).then_inc(bias_set, 1)
            V.memset(bias8[64:128, :, 0:CHUNK], 8 * MASK).then_inc(bias_set, 1)
            dve.wait_ge(bias_set, AH + 2)
            dve.wait_ge(const_in, 7 * 16)
            dve.wait_ge(state_in, 16)
            dve.wait_ge(zeros_set, 2)

            def body(i, past):
                sample = isinstance(i, int) and i == NP
                st = 1 if sample else 0
                W = (past + 1) * P if not sample else P + DEC
                b0 = (BT - past) * P
                dve.wait_ge(qk_squared, i + 1)
                V.tensor_reduce(qk_ms[:, :], sq[:, :].rearrange("p (h e) -> p h e", e=AD), AX.X, ALU.add).then_inc(qk_summed, 1)
                dve.wait_ge(qk_summed, i + 1)
                V.tensor_scalar(qk_ms[:, :], qk_ms[:, :], 1.0 / AD, EPS, ALU.mult, ALU.add).then_inc(qk_mean, 1)
                dve.wait_ge(qk_rs_ready, i + 1)
                if sample:
                    dve.wait_ge(cache_turned, 1)
                if not isinstance(i, int) or sample:
                    dve.wait_ge(k_stored, 16 * (i - BT) + 16)
                after(dve, k_turned, i)
                V.tensor_tensor(qk[:, :].rearrange("p (h e) -> p h e", e=AD), za[:, 0:2 * AW].rearrange("p (h e) -> p h e", e=AD),
                                qk_rs[:, :].rearrange("p (h o) -> p h o", o=1).broadcast_to([P, 2 * AH, AD]), ALU.mult
                                ).then_inc(qk_scaled, 1)
                dve.wait_ge(qk_scaled, i + 1)
                qk4 = qk[:, :].rearrange("p (c h e) -> p c h e", c=2, e=AD)
                gq = g_qk[:, :, :].rearrange("p c (o e) -> p c o e", o=1).broadcast_to([P, 2, AH, AD])
                V.tensor_tensor(qk4, qk4, gq, ALU.mult).then_inc(qk_ready, 1)
                dve.wait_ge(rq_ready, i + 1)
                V.tensor_tensor(rqdT[:, :, :], rqT[:, :, :], q_dec[:, :, :], ALU.mult).then_inc(rqd_ready, 1)
                dve.wait_ge(inner_ready, i + 1)
                V.tensor_tensor(inner[:, :, :], heads4(M), decay[:, :, :], ALU.mult).then_inc(inner_scaled, 1)
                dve.wait_ge(update_ready, i + 1)
                for h in range(RH):
                    g_l = gammas()[h] ** (DEC if sample else P)
                    V.scalar_tensor_tensor(out=state[:, st, h, :], in0=state[:, st, h, :], scalar=g_l,
                                           in1=M[:, h * RD:(h + 1) * RD], op0=ALU.mult, op1=ALU.add).then_inc(state_ready, 1)

                def softmax_head(h):
                    dve.wait_ge(scores_ready, AH * i + h + 1)
                    after(dve, p_turned, AH * i + h - 1)
                    V.memset(mark[:, h:h + 1], 0.0)
                    V.tensor_tensor_reduce(out=sc[:, h % 2, 0:W], in0=S[:, h % 2, 0:W], in1=bias8[:, h, b0:b0 + W],
                                           scale=-float(AD) ** -0.5, scalar=-LOWEST, op0=ALU.add, op1=ALU.min,
                                           accum_out=neg_max[:, h:h + 1]).then_inc(softmax_in, 1)

                softmax_head(0)
                softmax_head(1)
                dve.wait_ge(r_squared, i + 1)
                V.tensor_reduce(r_ms[:, :], heads4(sq[:, 0:RW]), AX.X, ALU.add).then_inc(r_summed, 1)
                dve.wait_ge(r_summed, i + 1)
                V.tensor_scalar(r_ms[:, :], r_ms[:, :], 1.0 / RD, EPS, ALU.mult, ALU.add).then_inc(r_mean, 1)
                softmax_head(2)
                dve.wait_ge(r_exp, i + 1)
                V.tensor_scalar(r_gate[:, :], r_gate[:, :], 1.0, None, ALU.add).then_inc(r_plus, 1)
                softmax_head(3)
                dve.wait_ge(r_plus, 2 * i + 1)
                V.reciprocal(r_gate[:, :], r_gate[:, :]).then_inc(r_plus, 1)
                dve.wait_ge(r_plus, 2 * i + 2)
                V.tensor_tensor(r_gate[:, :], r_gate[:, :], zr[:, 3 * RW:4 * RW], ALU.mult).then_inc(r_silu, 1)
                softmax_head(4)
                dve.wait_ge(r_rs_ready, i + 1)
                dve.wait_ge(ret_out, i + 1)
                V.tensor_tensor(heads4(ro[:, :]), heads4(ro[:, :]),
                                r_rs[:, :].rearrange("p (h o) -> p h o", o=1).broadcast_to([P, RH, RD]), ALU.mult).then_inc(r_scaled, 1)
                dve.wait_ge(r_scaled, i + 1)
                V.tensor_tensor(ro[:, :], ro[:, :], g_r[:, :], ALU.mult).then_inc(r_gained, 1)
                softmax_head(5)
                dve.wait_ge(r_gained, i + 1)
                dve.wait_ge(r_silu, i + 1)
                V.tensor_tensor(ro[:, :], ro[:, :], r_gate[:, :], ALU.mult).then_inc(r_ready, 1)
                dve.wait_ge(gate_exp, i + 1)
                V.tensor_scalar(zg[:, :], zg[:, :], 1.0, None, ALU.add).then_inc(gate_plus, 1)
                softmax_head(6)
                softmax_head(7)
                dve.wait_ge(gate_plus, i + 1)
                V.reciprocal(zg[:, :], zg[:, :]).then_inc(gates_ready, 1)
                dve.wait_ge(p_ready, AH * i + AH)
                V.reciprocal(rden[:, :], den[:, :]).then_inc(den_ready, 1)
                dve.wait_ge(den_ready, i + 1)
                dve.wait_ge(o_ready, AH * i + AH)
                after(dve, oa_turned, i)
                V.tensor_tensor(oa[:, :].rearrange("p (h e) -> p h e", e=AD), M.rearrange("p (h e) -> p h e", e=AD),
                                rden[:, :].rearrange("p (h o) -> p h o", o=1).broadcast_to([P, AH, AD]), ALU.mult
                                ).then_inc(oa_ready, 1)
                dve.wait_ge(gates_ready, i + 1)
                for c in range(2):
                    dve.wait_ge(branch_ready, 2 * i + c + 1)
                    V.tensor_tensor(zg[:, c * D:(c + 1) * D], zg[:, c * D:(c + 1) * D], S[:, c, :], ALU.mult).then_inc(gated, 1)
                dve.wait_ge(gated, 2 * i + 2)
                V.tensor_tensor(zg[:, 0:D], zg[:, 0:D], zg[:, D:2 * D], ALU.add).then_inc(merged, 1)
                dve.wait_ge(proj_ready, i + 1)
                dve.wait_ge(x_in, 16 * i + 16)
                V.tensor_tensor(x[:, :], x[:, :], OM[:, :, :].rearrange("p b n -> p (b n)"), ALU.add).then_inc(x2_ready, 1)
                dve.wait_ge(x2_ready, i + 1)
                dve.wait_ge(r_summed, i + 1)
                V.tensor_tensor_reduce(out=sq[:, :], in0=x[:, :], in1=x[:, :], scale=1.0, scalar=0.0, op0=ALU.mult, op1=ALU.add,
                                       accum_out=f_ms[:, 0:1]).then_inc(f_squared, 1)
                dve.wait_ge(f_squared, i + 1)
                V.tensor_scalar(f_ms[:, :], f_ms[:, :], 1.0 / D, EPS, ALU.mult, ALU.add).then_inc(f_mean, 1)
                dve.wait_ge(f_rs_ready, i + 1)
                dve.wait_ge(m_turned, 2 * i + 2)
                V.scalar_tensor_tensor(out=zg[:, 0:D], in0=x[:, :], scalar=f_rs[:, 0:1], in1=g_f[:, :],
                                       op0=ALU.mult, op1=ALU.mult).then_inc(h2_ready, 1)

            tiles(dve, body)

        @block.tensor
        def _(pe):
            def mm(out, a, b, start=True, stop=True):
                return nc.tensor.matmul(out, a, b, start=start, stop=stop)

            def turn(out_bank, src, n=4, width=P):
                for k in range(n):
                    last = nc.tensor.transpose(out_bank[:, k * P:(k + 1) * P], src(k), ident[:, :])
                return last

            pe.wait_ge(ident_in, 32)
            pe.wait_ge(bias_in, 16)
            for h in range(AH):
                after(pe, bias_set, h - 1)
                mm(S[:, h % 2, 0:512], flip[:, :], bias_rev[:, h, 0:512])
                mm(S[:, h % 2, 512:BW], flip[:, :], bias_rev[:, h, 512:BW]).then_inc(bias_turned, 1)

            def body(i, past):
                sample = isinstance(i, int) and i == NP
                st = 1 if sample else 0
                first = 0 if sample or isinstance(i, int) else (i - BT) * P
                after(pe, h2_out, 2 * i)
                if sample:
                    pe.wait_ge(cache_in, 32)
                    turn(T[:, 1, :], lambda k: qk[:, AW + k * P:AW + (k + 1) * P]).then_inc(cache_turned, 1)
                    pe.wait_ge(keys_ready, NP + 1)
                pe.wait_ge(qk_ready, i + 1)
                turn(T[:, 0, :], lambda k: qk[:, k * P:(k + 1) * P]).then_inc(q_turned, 1)
                turn(T[:, 1, :], lambda k: qk[:, AW + k * P:AW + (k + 1) * P]).then_inc(k_turned, 1)
                after(pe, x2_ready, i)
                pe.wait_ge(rotated, i + 1)
                turn(O, lambda k: rot[:, k, :]).then_inc(rq_turned, 1)
                turn(M, lambda k: rot[:, RH + k, :]).then_inc(rk_turned, 1)
                pe.wait_ge(rq_ready, i + 1)
                pe.wait_ge(rk_ready, i + 1)
                for h in range(RH):
                    last = mm(M[:, h * P:(h + 1) * P], rkT[:, h, :], rqT[:, h, :])
                last.then_inc(inner_ready, 1)
                pe.wait_ge(inner_scaled, i + 1)
                pe.wait_ge(rqd_ready, i + 1)
                after(pe, state_ready, RH * i)
                for h in range(RH):
                    v = zr[:, 2 * RW + h * RD:2 * RW + (h + 1) * RD]
                    mm(O[:, h * RD:(h + 1) * RD], inner[:, h, :], v, stop=False)
                    last = mm(O[:, h * RD:(h + 1) * RD], rqdT[:, h, :], state[:, st, h, :], start=False)
                last.then_inc(ret_ready, 1)
                pe.wait_ge(k_decayed, i + 1)
                for h in range(RH):
                    last = mm(M[:, h * RD:(h + 1) * RD], rot[:, RH + h, :], zr[:, 2 * RW + h * RD:2 * RW + (h + 1) * RD])
                last.then_inc(update_ready, 1)

                def scores(h):
                    W = (past + 1) * P if not sample else P + DEC
                    after(pe, softmax_in, AH * i + h - 1)
                    if h < 2:
                        after(pe, gated, 2 * i)
                        pe.wait_ge(bias_set, AH)
                    last = mm(S[:, h % 2, 0:min(W, 512)], qpad[:, h, :], keysT[:, h // 2, at(first, min(W, 512))])
                    if W > 512:
                        last = mm(S[:, h % 2, 512:W], qpad[:, h, :], keysT[:, h // 2, at(first + 512, W - 512)])
                    last.then_inc(scores_ready, 1)

                def values(h):
                    pe.wait_ge(p_ready, AH * i + h + 1)
                    after(pe, p_out, AH * i + h)
                    n = past + 1
                    for k in range(n):
                        w_ = DEC if sample and k == 1 else P
                        last = nc.tensor.transpose(T[0:w_, k // 4, (k % 4) * P:(k % 4 + 1) * P],
                                                   sc[:, h % 2, k * P:k * P + w_], ident[:, :])
                    last.then_inc(p_turned, 1)
                    pe.wait_ge(p_out, AH * i + h + 1)
                    if h == 0:
                        pe.wait_ge(state_ready, RH * i + RH)
                        pe.wait_ge(v_ready, i + 1)
                    for k in range(n):
                        w_ = DEC if sample and k == 1 else P
                        vt = k if sample or isinstance(i, int) else i - BT + k
                        last = mm(M[:, h * AD:(h + 1) * AD], pT[0:w_, h % 2, k, :], vals[0:w_, vt, h * AD:(h + 1) * AD],
                                  start=(k == 0), stop=(k == n - 1))
                    last.then_inc(o_ready, 1)

                pe.wait_ge(q_padded, 2 * i + 2)
                pe.wait_ge(keys_ready, i + 1 + (1 if sample else 0))
                scores(0)
                scores(1)
                for h in range(AH):
                    values(h)
                    if h + 2 < AH:
                        scores(h + 2)
                pe.wait_ge(r_ready, i + 1)
                turn(T[:, 0, :], lambda k: ro[:, k * P:(k + 1) * P]).then_inc(r_turned, 1)
                pe.wait_ge(oa_ready, i + 1)
                turn(T[:, 1, :], lambda k: oa[:, k * P:(k + 1) * P]).then_inc(oa_turned, 1)
                if isinstance(i, int) and i == 0:
                    pe.wait_ge(w_in, 5 * 16)
                pe.wait_ge(oa_out, i + 1)
                pe.wait_ge(softmax_in, AH * i + AH)
                for c in range(2):
                    if c == 1:
                        pe.wait_ge(r_out, i + 1)
                    for n in range(2):
                        for k in range(4):
                            last = mm(S[:, c, n * 512:(n + 1) * 512], tT[:, 4 * c + k, :],
                                      (w_a, w_r)[c][:, k, n * 512:(n + 1) * 512], start=(k == 0), stop=(k == 3))
                    last.then_inc(branch_ready, 1)
                pe.wait_ge(merged, i + 1)
                for b in range(2):
                    turn(T[:, b, :], lambda k: zg[:, (4 * b + k) * P:(4 * b + k + 1) * P]).then_inc(m_turned, 1)
                pe.wait_ge(m_out, 2 * i + 2)
                pe.wait_ge(ret_out, i + 1)
                for n in range(2):
                    for k in range(KD):
                        last = mm(OM[:, n, :], tT[:, k, :], w_o[:, k, n * 512:(n + 1) * 512], start=(k == 0), stop=(k == KD - 1))
                last.then_inc(proj_ready, 1)
                pe.wait_ge(h2_ready, i + 1)
                for b in range(2):
                    turn(T[:, b, :], lambda k: zg[:, (4 * b + k) * P:(4 * b + k + 1) * P]).then_inc(h2_turned, 1)

            tiles(pe, body)


def route(nc, d):
    G, GT = 3, 3
    GW = GT * P
    PARTS = (range(0, 5), range(5, 10), range(10, HC))
    with Stage(nc, "rt") as s:
        wq = s.sb("wq", [P, KD, 2 * PH * PK])
        keys = s.sb("keys", [P, HC, PK])
        h2T = s.sb("h2T", [P, 2, KD, GW])
        qT = s.sb("qT", [P, 2, HC, GW])
        sc = s.sb("sc", [P, GT, HC, PK])
        ident = s.sb("ident", [P, P])
        iota16 = s.sb("iota16", [P, TOPK])
        tv = s.sb("tv", [P, PH, 2, TOPK])
        ti = s.sb("ti", [P, PH, 2, TOPK], U32)
        tf = s.sb("tf", [P, PH, 2, TOPK])
        cand = s.sb("cand", [P, PH, TOPK, TOPK])
        bv = s.sb("bv", [P, PH, TOPK])
        bi = s.sb("bi", [P, PH, TOPK], U32)
        ab = s.sb("ab", [P, 2, SLOTS], U32)
        abf = s.sb("abf", [P, 2, SLOTS])
        hit = s.sb("hit", [P, 2, SLOTS, TOPK])
        out = s.sb("out", [P, 3, SLOTS])
        den = s.sb("den", [P, 2, PH])
        outT = s.sb("outT", [P, 3, P])
        mark = s.sb("mark", [P, 1])
        qp = s.pb("qp", [P, 3, 512])
        sp_ = s.pb("sp", [P, 4, 512])
        tp = s.pb("tp", [P, 512])
        names = """const_in w_in h2_in0 h2_in1 iota_set q_ready q_out s_ready s_out
            top8 found8 cut8 top16 found16 keyed cand_ready best8 bfound8 bcut8 best16 bfound16
            split ab_ready hit_ready picked shifted expd summed recip out_ready out_turned outT_ready stored""".split()
        (const_in, w_in, h2_in0, h2_in1, iota_set, q_ready, q_out, s_ready, s_out,
         top8, found8, cut8, top16, found16, keyed, cand_ready, best8, bfound8, bcut8, best16, bfound16,
         split, ab_ready, hit_ready, picked, shifted, expd, summed, recip, out_ready, out_turned, outT_ready, stored
         ) = [s.sem(n) for n in names]
        h2_in = (h2_in0, h2_in1)
        block = s.block()

        @block.sync
        def _(sp):
            sp.dma_start(ident[:, :], d["ident"]).then_inc(const_in, 16)
            h2_v = d["h2T"].rearrange("(k p) t -> p k t", p=P)
            for g in range(G):
                after(sp, q_ready, HC * (g - 1))
                sp.dma_start(h2T[:, g % 2, :, :], h2_v[:, :, g * GW:(g + 1) * GW]).then_inc(h2_in[g % 2], 16)
                if g == 0:
                    w_v = d["w_q"].rearrange("(k p) n -> p k n", p=P)
                    for c in range(4):
                        sp.dma_start(wq[:, :, c * 512:(c + 1) * 512], w_v[:, :, c * 512:(c + 1) * 512]).then_inc(w_in, 16)
                        sp.wait_ge(w_in, 16 * c + 16)
                    sp.dma_start(keys[:, :, :], d["keys"]).then_inc(const_in, 16)

        @block.gpsimd
        def _(pool):
            nc.gpsimd.iota(iota16[:, :], [[1, TOPK]], base=0, channel_multiplier=0,
                           allow_small_or_imprecise_dtypes=True).then_inc(iota_set, 1)
            pool.wait_ge(iota_set, 1)
            with pool.Fori(0, NT) as t:
                for c in range(2):
                    pool.wait_ge(hit_ready, 2 * t + c + 1)
                    h4 = hit[:, c, :, :].rearrange("p (h k) a -> p h k a", h=PH)
                    keyv = tf[:, :, c, :].rearrange("p h (o a) -> p h o a", o=1).broadcast_to([P, PH, TOPK, TOPK])
                    nc.gpsimd.tensor_tensor(h4, h4, keyv, ALU.mult).then_inc(picked, 1)

        @block.scalar
        def _(act):
            act.sem_inc(stored, 16)

            def queries_out(g, part):
                for hc in part:
                    act.wait_ge(q_ready, HC * g + hc + 1)
                    nc.scalar.copy(qT[:, g % 2, hc, :], qp[:, hc % 3, 0:GW]).then_inc(q_out, 1)

            def softmax_and_store(t):
                act.wait_ge(shifted, t + 1)
                nc.scalar.activation(bv[:, :, :], bv[:, :, :], ACT.Exp).then_inc(expd, 1)
                act.wait_ge(out_turned, t + 2)
                act.wait_ge(stored, 16 * t + 16)
                nc.scalar.copy(outT[:, :, :], tp[:, 0:3 * P].rearrange("p (c t) -> p c t", c=3)).then_inc(outT_ready, 1)
                act.wait_ge(outT_ready, t + 1)
                act.dma_start(d["route"][:, :, t * P:(t + 1) * P], outT[:, :, :]).then_inc(stored, 16)

            queries_out(0, range(HC))
            for t in range(NT):
                for b in range(4):
                    act.wait_ge(s_ready, 4 * t + b + 1)
                    act.wait_ge(found16, HC * t + HC)
                    nc.scalar.copy(sc[:, t % GT, 4 * b:4 * b + 4, :].rearrange("p h k -> p (h k)"), sp_[:, b, :]).then_inc(s_out, 1)
                if t:
                    softmax_and_store(t - 1)
                if t // GT + 1 < G:
                    queries_out(t // GT + 1, PARTS[t % GT])
            softmax_and_store(NT - 1)
            act.wait_ge(stored, 16 * NT + 16)

        @block.vector
        def _(dve):
            V = nc.vector
            dve.sem_inc(found16, GT * HC)
            dve.wait_ge(iota_set, 1)

            def take_wait():
                V.memset(mark[:, :], 0.0)

            def tile(t, u):
                dve.wait_ge(s_out, 4 * t + 4)
                take_wait()
                for h in range(HC):
                    V.max(tv[:, h // 2, h % 2, 0:8], sc[:, u, h, :]).then_inc(top8, 1)
                dve.wait_ge(top8, HC * t + HC)
                take_wait()
                for h in range(HC):
                    V.max_index(ti[:, h // 2, h % 2, 0:8], tv[:, h // 2, h % 2, 0:8], sc[:, u, h, :]).then_inc(found8, 1)
                dve.wait_ge(found8, HC * t + HC)
                take_wait()
                for h in range(HC):
                    V.match_replace(sc[:, u, h, :], tv[:, h // 2, h % 2, 0:8], sc[:, u, h, :], LOWEST).then_inc(cut8, 1)
                dve.wait_ge(cut8, HC * t + HC)
                take_wait()
                for h in range(HC):
                    V.max(tv[:, h // 2, h % 2, 8:16], sc[:, u, h, :]).then_inc(top16, 1)
                dve.wait_ge(top16, HC * t + HC)
                take_wait()
                for h in range(HC):
                    V.max_index(ti[:, h // 2, h % 2, 8:16], tv[:, h // 2, h % 2, 8:16], sc[:, u, h, :]).then_inc(found16, 1)
                V.tensor_tensor(cand[:, :, :, :],
                                tv[:, :, 0, :].rearrange("p h (a o) -> p h a o", o=1).broadcast_to([P, PH, TOPK, TOPK]),
                                tv[:, :, 1, :].rearrange("p h (o b) -> p h o b", o=1).broadcast_to([P, PH, TOPK, TOPK]),
                                ALU.add).then_inc(cand_ready, 1)
                dve.wait_ge(found16, HC * t + HC + GT * HC)
                V.tensor_copy(tf[:, :, :, :], ti[:, :, :, :]).then_inc(keyed, 1)
                dve.wait_ge(cand_ready, t + 1)
                take_wait()
                flat = lambda h: cand[:, h, :, :].rearrange("p a b -> p (a b)")
                for h in range(PH):
                    V.max(bv[:, h, 0:8], flat(h)).then_inc(best8, 1)
                dve.wait_ge(best8, PH * t + PH)
                take_wait()
                for h in range(PH):
                    V.max_index(bi[:, h, 0:8], bv[:, h, 0:8], flat(h)).then_inc(bfound8, 1)
                dve.wait_ge(bfound8, PH * t + PH)
                take_wait()
                for h in range(PH):
                    V.match_replace(flat(h), bv[:, h, 0:8], flat(h), LOWEST).then_inc(bcut8, 1)
                dve.wait_ge(bcut8, PH * t + PH)
                take_wait()
                for h in range(PH):
                    V.max(bv[:, h, 8:16], flat(h)).then_inc(best16, 1)
                dve.wait_ge(best16, PH * t + PH)
                take_wait()
                for h in range(PH):
                    V.max_index(bi[:, h, 8:16], bv[:, h, 8:16], flat(h)).then_inc(bfound16, 1)
                dve.wait_ge(bfound16, PH * t + PH)
                V.tensor_tensor(cand[:, :, 0, :], bv[:, :, :], bv[:, :, 0:1].broadcast_to([P, PH, TOPK]),
                                ALU.subtract).then_inc(split, 1)
                bi2 = bi[:, :, :].rearrange("p h k -> p (h k)")
                V.tensor_single_scalar(ab[:, 0, :], bi2, 4, ALU.logical_shift_right).then_inc(split, 1)
                V.tensor_single_scalar(ab[:, 1, :], bi2, 15, ALU.bitwise_and).then_inc(split, 1)
                dve.wait_ge(split, 3 * t + 3)
                V.tensor_copy(bv[:, :, :], cand[:, :, 0, :]).then_inc(shifted, 1)
                V.tensor_copy(abf[:, :, :], ab[:, :, :]).then_inc(ab_ready, 1)
                dve.wait_ge(ab_ready, t + 1)
                for c in range(2):
                    V.tensor_tensor(hit[:, c, :, :], abf[:, c, :].rearrange("p (s o) -> p s o", o=1).broadcast_to([P, SLOTS, TOPK]),
                                    iota16[:, :].rearrange("p (o a) -> p o a", o=1).broadcast_to([P, SLOTS, TOPK]),
                                    ALU.is_equal).then_inc(hit_ready, 1)
                dve.wait_ge(expd, t + 1)
                V.tensor_reduce(den[:, 0, :], bv[:, :, :], AX.X, ALU.add).then_inc(summed, 1)
                dve.wait_ge(summed, t + 1)
                V.reciprocal(den[:, 1, :], den[:, 0, :]).then_inc(recip, 1)
                dve.wait_ge(recip, t + 1)
                dve.wait_ge(out_turned, t + 1)
                V.tensor_tensor(out[:, 2, :].rearrange("p (h k) -> p h k", h=PH), bv[:, :, :],
                                den[:, 1, :].rearrange("p (h o) -> p h o", o=1).broadcast_to([P, PH, TOPK]), ALU.mult).then_inc(out_ready, 1)
                for c in range(2):
                    dve.wait_ge(picked, 2 * t + c + 1)
                    V.tensor_reduce(out[:, c, :], hit[:, c, :, :], AX.X, ALU.add).then_inc(out_ready, 1)

            with dve.Fori(0, G) as g:
                for u in range(GT):
                    tile(GT * g + u, u)

        @block.tensor
        def _(pe):
            pe.sem_inc(out_turned, 1)
            pe.wait_ge(const_in, 32)

            def queries(g, part):
                for hc in part:
                    if hc == 0:
                        pe.wait_ge(h2_in[g % 2], 16 * (g // 2) + 16)
                    if g == 0 and hc % 4 == 0:
                        pe.wait_ge(w_in, 4 * hc + 16)
                    after(pe, q_out, HC * g + hc - (2 if hc else 0))
                    for k in range(KD):
                        last = nc.tensor.matmul(qp[:, hc % 3, 0:GW], wq[:, k, hc * PK:(hc + 1) * PK], h2T[:, g % 2, k, :],
                                                start=(k == 0), stop=(k == KD - 1))
                    last.then_inc(q_ready, 1)

            def scores(t, u):
                for hc in range(HC):
                    if u == 0:
                        pe.wait_ge(q_out, HC * (t // GT) + hc + 1)
                    if hc % 4 == 0:
                        after(pe, s_out, 4 * t + hc // 4 - 3)
                    last = nc.tensor.matmul(sp_[:, hc // 4, (hc % 4) * PK:(hc % 4 + 1) * PK], qT[:, t // GT % 2, hc, u * P:(u + 1) * P],
                                            keys[:, hc, :], start=True, stop=True)
                    if hc % 4 == 3:
                        last.then_inc(s_ready, 1)

            def turn(t):
                pe.wait_ge(out_ready, 3 * t + 3)
                after(pe, outT_ready, t)
                for c in range(3):
                    last = nc.tensor.transpose(tp[:, c * P:(c + 1) * P], out[:, c, :], ident[:, :])
                last.then_inc(out_turned, 1)

            queries(0, range(HC))
            for t in range(NT):
                scores(t, t % GT)
                if t:
                    turn(t - 1)
                if t // GT + 1 < G:
                    queries(t // GT + 1, PARTS[t % GT])
            turn(NT - 1)


def spread(nc, d):
    B = 4
    S4 = 4
    with Stage(nc, "spr") as s:
        rt = s.sb("rt", [P, 3, TPAD])
        iota = s.sb("iota", [P, P])
        rows = s.sb("rows", [P, S4, B, P])
        cols = s.sb("cols", [P, S4, B, P])
        g = s.sb("g", [P, 2, PK, P])
        gp = s.pb("gp", [P, S4, B * P])
        rt_in, iota_set = s.sem("rt_in"), s.sem("iota_set")
        hot_ready, spread_ready, g_out = s.sem("hot_ready"), s.sem("spread_ready"), s.sem("g_out")
        g_stored = [s.sem("g_stored0"), s.sem("g_stored1")]
        FREE = S4
        steps = P // (B * S4)
        block = s.block()

        def tiles(eng, body):
            with eng.Fori(0, NP // 2) as pair:
                body(2 * pair, 0, pair, P)
                body(2 * pair + 1, 1, pair, P)
            body(NP, 0, NP // 2, DEC)

        @block.sync
        def _(sp):
            sp.dma_start(rt[:, :, :], d["route"]).then_inc(rt_in, 16)
            sp.sem_inc(g_stored[0], 16)
            sp.sem_inc(g_stored[1], 16)

            def body(t, slot, pair, n):
                sp.wait_ge(g_out, t * (P // B) + n // B + FREE)
                sp.dma_start(d["gates"].rearrange("j i t -> i j t")[:, :, at(t * P, n)],
                             g[:, slot, :, 0:n]).then_inc(g_stored[slot], 16)

            tiles(sp, body)
            sp.wait_ge(g_stored[0], 16 * (NP // 2 + 1) + 16)
            sp.wait_ge(g_stored[1], 16 * (NP // 2) + 16)

        @block.gpsimd
        def _(pool):
            nc.gpsimd.iota(iota[:, :], [[1, P]], base=0, channel_multiplier=0,
                           allow_small_or_imprecise_dtypes=True).then_inc(iota_set, 1)

        @block.vector
        def _(dve):
            dve.wait_ge(iota_set, 1)
            dve.wait_ge(rt_in, 16)

            def body(t, slot, pair, n):
                with dve.Fori(0, n // (B * S4)) as m:
                    for q in range(S4):
                        dve.wait_ge(spread_ready, t * (P // B) + m * S4 + q + 1)
                        for b in range(B):
                            tok = t * P + m * (B * S4) + q * B + b
                            nc.vector.tensor_scalar(rows[:, q, b, :], iota[:, :], rt[:, 0, at(tok, 1)], None, ALU.is_equal)
                            last = nc.vector.tensor_scalar(cols[:, q, b, :], iota[:, :], rt[:, 1, at(tok, 1)], rt[:, 2, at(tok, 1)],
                                                           ALU.is_equal, ALU.mult)
                        last.then_inc(hot_ready, 1)

            tiles(dve, body)

        @block.tensor
        def _(pe):
            pe.sem_inc(spread_ready, FREE)

            def body(t, slot, pair, n):
                with pe.Fori(0, n // (B * S4)) as m:
                    for q in range(S4):
                        pe.wait_ge(hot_ready, t * (P // B) + m * S4 + q + 1)
                        pe.wait_ge(g_out, t * (P // B) + m * S4 + q + 1)
                        for b in range(B):
                            last = nc.tensor.matmul(gp[:, q, b * P:(b + 1) * P], rows[:, q, b, :], cols[:, q, b, :],
                                                    start=True, stop=True)
                        last.then_inc(spread_ready, 1)

            tiles(pe, body)

        @block.scalar
        def _(act):
            act.sem_inc(g_out, FREE)

            def body(t, slot, pair, n):
                act.wait_ge(g_stored[slot], 16 * pair + 16)
                with act.Fori(0, n // (B * S4)) as m:
                    for q in range(S4):
                        act.wait_ge(spread_ready, t * (P // B) + m * S4 + q + 1 + FREE)
                        nc.scalar.copy(g[:, slot, :, at(m * (B * S4) + q * B, B)],
                                       gp[:, q, :].rearrange("p (t j) -> p j t", t=B)).then_inc(g_out, 1)

            tiles(act, body)


TG = [(0, 384), (384, 384), (768, 320)]
F32R = mybir.dt.float32r


def experts(nc, d):
    NG = len(TG)
    NV = KD * NG
    NJ = PK
    with Stage(nc, "exp") as s:
        h2 = [s.sb("h2_hi", [P, KD, TOK], F32R), s.sb("h2_lo", [P, KD, TOK], F32R)]
        acc = s.sb("acc", [P, KD, TOK])
        u_raw = s.sb("u_raw", [P, 2, KD * P])
        v_raw = s.sb("v_raw", [P, 2, D])
        u = [s.sb("u_hi", [P, 2, KD * P], F32R), s.sb("u_lo", [P, 2, KD * P], F32R)]
        v = [s.sb("v_hi", [P, 2, D], F32R), s.sb("v_lo", [P, 2, D], F32R)]
        gt = s.sb("gt", [P, 2, TOK])
        ge = s.sb("ge", [P, NG, 384])
        pr = s.sb("pr", [P, NG, 384])
        am = [s.sb("am_hi", [P, TOK], F32R), s.sb("am_lo", [P, TOK], F32R)]
        ident = s.sb("ident", [P, P])
        y = u_raw
        up = s.pb("up", [P, NG, 512])
        vp = s.pb("vp", [P, 4, 512])
        names = """h2_in h2_hi_ready h2_lo_ready zeroed ident_in u_in0 u_in1 v_in0 v_in1 g_in0 g_in1
            u_hi_ready u_lo_ready v_hi_ready v_lo_ready up_ready gelu_ready prod_ready am_hi_ready am_lo_ready
            down_ready added x2_in0 x2_in1 y_stored0 y_stored1 y_turned y_ready""".split()
        (h2_in, h2_hi_ready, h2_lo_ready, zeroed, ident_in, u_in0, u_in1, v_in0, v_in1, g_in0, g_in1,
         u_hi_ready, u_lo_ready, v_hi_ready, v_lo_ready, up_ready, gelu_ready, prod_ready, am_hi_ready, am_lo_ready,
         down_ready, added, x2_in0, x2_in1, y_stored0, y_stored1, y_turned, y_ready) = [s.sem(n) for n in names]
        u_in, v_in, g_in = (u_in0, u_in1), (v_in0, v_in1), (g_in0, g_in1)
        x2_in, y_stored = (x2_in0, x2_in1), (y_stored0, y_stored1)
        LO0, PROD0, GELU0, AMH0, DOWN0, ADD0 = 2, 2 * NG, NG, NG, NV, 4
        block = s.block()

        @block.sync
        def _(sp):
            sp.dma_start(ident[:, :], d["ident"]).then_inc(ident_in, 16)
            h2_v = d["h2T"].rearrange("(k p) t -> p k t", p=P)
            for k in range(0, KD, 2):
                sp.dma_start(acc[:, k:k + 2, :], h2_v[:, k:k + 2, 0:TOK]).then_inc(h2_in, 16)
                sp.wait_ge(h2_in, 8 * k + 16)

            def load(j, slot):
                sp.wait_ge(u_lo_ready, j + 1)
                sp.dma_start(u_raw[:, slot, :], d["u"][at(j, 1), :, :].rearrange("o p n -> p (o n)")).then_inc(u_in[slot], 16)
                sp.wait_ge(v_lo_ready, j + 1)
                sp.dma_start(v_raw[:, slot, :], d["v"].rearrange("(i j) e -> j i e", j=PK)[at(j, 1), :, :]
                             .rearrange("o i e -> i (o e)")).then_inc(v_in[slot], 16)
                sp.wait_ge(prod_ready, NG * j + NG)
                sp.dma_start(gt[:, slot, :], d["gates"][at(j, 1), :, :].rearrange("o i t -> i (o t)")).then_inc(g_in[slot], 16)

            with sp.Fori(0, NJ // 2) as pair:
                load(2 * pair, 0)
                load(2 * pair + 1, 1)
            sp.wait_ge(u_lo_ready, NJ + LO0)
            for t in range(NT + 2):
                if t >= 2:
                    r, n = t - 2, min(P, TOK - (t - 2) * P)
                    sp.wait_ge(y_ready, 2 * r + 2)
                    sp.dma_start(d["yp"][r * P:r * P + n, :] if r < NP else d["ys"][:, :], y[0:n, r % 2, :]
                                 ).then_inc(y_stored[r % 2], 16)
                if t < NT:
                    n = min(P, TOK - t * P)
                    after(sp, y_stored[t % 2], 16 * (t // 2))
                    sp.dma_start(y[0:n, t % 2, :], d["x2"][t * P:t * P + n, :]).then_inc(x2_in[t % 2], 16)
            sp.wait_ge(y_stored[0], 16 * (NT - NT // 2))
            sp.wait_ge(y_stored[1], 16 * (NT // 2))

        @block.gpsimd
        def _(pool):
            pool.sem_inc(u_lo_ready, LO0)
            pool.sem_inc(v_lo_ready, LO0)

            def split_u(j, slot):
                pool.wait_ge(u_hi_ready, j + 1)
                nc.gpsimd.tensor_tensor(u[1][:, slot, :], u_raw[:, slot, :], u[0][:, slot, :].bitcast(F32),
                                        ALU.subtract).then_inc(u_lo_ready, 1)

            def split_v(j, slot):
                pool.wait_ge(v_hi_ready, j + 1)
                nc.gpsimd.tensor_tensor(v[1][:, slot, :], v_raw[:, slot, :], v[0][:, slot, :].bitcast(F32),
                                        ALU.subtract).then_inc(v_lo_ready, 1)

            with pool.Fori(0, NJ // 2) as pair:
                for o in range(2):
                    split_u(2 * pair + o, o)
                    split_v(2 * pair + o, o)

        @block.scalar
        def _(act):
            act.sem_inc(gelu_ready, GELU0)
            act.sem_inc(am_hi_ready, AMH0)
            for k in range(KD):
                act.wait_ge(h2_in, 16 * (k // 2) + 16)
                nc.scalar.copy(h2[0][:, k, :], acc[:, k, :]).then_inc(h2_hi_ready, 1)

            def high_u(j, slot, half):
                act.wait_ge(u_in[slot], 16 * half + 16)
                after(act, up_ready, NG * j - NG)
                nc.scalar.copy(u[0][:, slot, :], u_raw[:, slot, :]).then_inc(u_hi_ready, 1)

            def high_v(j, slot, half):
                act.wait_ge(v_in[slot], 16 * half + 16)
                after(act, down_ready, NV * j)
                nc.scalar.copy(v[0][:, slot, :], v_raw[:, slot, :]).then_inc(v_hi_ready, 1)

            def gelu(j, g):
                w = TG[g][1]
                act.wait_ge(up_ready, NG * j + g + 1)
                after(act, prod_ready, NG * j + g + 1 + PROD0 - NG)
                nc.scalar.activation(ge[:, g, 0:w], up[:, g, 0:w], ACT.Gelu).then_inc(gelu_ready, 1)

            def high_am(j, g):
                t0, w = TG[g]
                act.wait_ge(prod_ready, NG * j + g + 1 + PROD0)
                act.wait_ge(down_ready, NV * j + KD * (g + 1))
                nc.scalar.copy(am[0][:, t0:t0 + w], pr[:, g, 0:w]).then_inc(am_hi_ready, 1)

            def step(j, slot, half, next_u=True):
                gelu(j - 1, 2)
                high_am(j - 1, 2)
                if next_u:
                    high_u(j + 1, 1 - slot, half + slot)
                gelu(j, 0)
                high_am(j, 0)
                high_v(j, slot, half)
                gelu(j, 1)
                high_am(j, 1)

            high_u(0, 0, 0)
            high_u(1, 1, 0)
            gelu(0, 0)
            high_am(0, 0)
            high_v(0, 0, 0)
            gelu(0, 1)
            high_am(0, 1)
            with act.Fori(0, NJ // 2 - 1) as pair:
                step(2 * pair + 1, 1, pair)
                step(2 * pair + 2, 0, pair + 1)
            step(NJ - 1, 1, NJ // 2 - 1, next_u=False)
            gelu(NJ - 1, 2)
            high_am(NJ - 1, 2)

        @block.vector
        def _(dve):
            V = nc.vector
            dve.sem_inc(added, ADD0)
            dve.sem_inc(prod_ready, PROD0)
            for k in range(KD):
                dve.wait_ge(h2_hi_ready, k + 1)
                V.tensor_tensor(h2[1][:, k, :], acc[:, k, :], h2[0][:, k, :].bitcast(F32), ALU.subtract).then_inc(h2_lo_ready, 1)
            dve.wait_ge(h2_lo_ready, KD)
            V.memset(acc[:, :, :], 0.0).then_inc(zeroed, 1)
            dve.wait_ge(zeroed, 1)

            def product(j, g, slot, half):
                t0, w = TG[g]
                if g == 0:
                    dve.wait_ge(g_in[slot], 16 * half + 16)
                dve.wait_ge(gelu_ready, NG * j + g + 1 + GELU0)
                dve.wait_ge(am_hi_ready, NG * j + g + 1)
                V.tensor_tensor(pr[:, g, 0:w], ge[:, g, 0:w], gt[:, slot, t0:t0 + w], ALU.mult).then_inc(prod_ready, 1)

            def low_am(j, g):
                t0, w = TG[g]
                dve.wait_ge(am_hi_ready, NG * j + g + 1 + AMH0)
                V.tensor_tensor(am[1][:, t0:t0 + w], pr[:, g, 0:w], am[0][:, t0:t0 + w].bitcast(F32), ALU.subtract
                                ).then_inc(am_lo_ready, 1)

            def add(j, g, chunks):
                t0, w = TG[g]
                for k in chunks:
                    m = KD * g + k
                    dve.wait_ge(down_ready, NV * j + m + 1)
                    V.tensor_tensor(acc[:, k, t0:t0 + w], acc[:, k, t0:t0 + w], vp[:, m % 4, 0:w], ALU.add).then_inc(added, 1)

            def step(j, slot, half, half_before, up=True):
                for g in range(NG):
                    add(j, g, (0, 1))
                    if g == 0:
                        product(j - 1, 2, 1 - slot, half_before)
                    elif up:
                        product(j, g - 1, slot, half)
                    add(j, g, (2, 3))
                    if g == 0:
                        low_am(j - 1, 2)
                    elif up:
                        low_am(j, g - 1)
                    add(j, g, (4, 5, 6, 7))

            for g in range(2):
                product(0, g, 0, 0)
                low_am(0, g)
            with dve.Fori(0, NJ // 2 - 1) as pair:
                step(2 * pair + 1, 1, pair, pair)
                step(2 * pair + 2, 0, pair + 1, pair)
            step(NJ - 1, 1, NJ // 2 - 1, NJ // 2 - 1)
            step(NJ, 0, 0, NJ // 2 - 1, up=False)
            for t in range(NT):
                n = min(P, TOK - t * P)
                dve.wait_ge(x2_in[t % 2], 16 * (t // 2) + 16)
                for c in range(2):
                    dve.wait_ge(y_turned, 2 * t + c + 1)
                    V.tensor_tensor(y[0:n, t % 2, c * 512:(c + 1) * 512], y[0:n, t % 2, c * 512:(c + 1) * 512],
                                    vp[0:n, 2 * (t % 2) + c, :], ALU.add).then_inc(y_ready, 1)

        @block.tensor
        def _(pe):
            pe.sem_inc(down_ready, DOWN0)
            pe.wait_ge(ident_in, 16)
            passes = ((0, 0), (0, 1), (1, 0))

            def step(j, slot, up_=True, down=True):
                if up_:
                    pe.wait_ge(u_lo_ready, j + 1 + LO0)
                if down:
                    pe.wait_ge(v_lo_ready, j + LO0)
                for g, (t0, w) in enumerate(TG):
                    if up_:
                        pe.wait_ge(gelu_ready, NG * j + g + 1)
                    if down:
                        pe.wait_ge(am_lo_ready, NG * (j - 1) + g + 1)
                    for k in range(KD):
                        if up_:
                            if isinstance(j, int) and j == 0 and g == 0:
                                pe.wait_ge(h2_lo_ready, k + 1)
                            for n, (a, b) in enumerate(passes):
                                last = nc.tensor.matmul(up[:, g, 0:w], u[a][:, slot, k * P:(k + 1) * P], h2[b][:, k, t0:t0 + w],
                                                        start=(k == 0 and n == 0), stop=(k == KD - 1 and n == 2))
                            if k == KD - 1:
                                last.then_inc(up_ready, 1)
                        if down:
                            m = KD * g + k
                            pe.wait_ge(added, NV * (j - 1) + m + 1)
                            for n, (a, b) in enumerate(passes):
                                last = nc.tensor.matmul(vp[:, m % 4, 0:w], v[a][:, 1 - slot, k * P:(k + 1) * P],
                                                        am[b][:, t0:t0 + w], start=(n == 0), stop=(n == 2))
                            last.then_inc(down_ready, 1)

            step(0, 0, down=False)
            with pe.Fori(0, NJ // 2 - 1) as pair:
                step(2 * pair + 1, 1)
                step(2 * pair + 2, 0)
            step(NJ - 1, 1)
            step(NJ, 0, up_=False)
            pe.wait_ge(added, NV * NJ + ADD0)
            for t in range(NT):
                n = min(P, TOK - t * P)
                after(pe, y_ready, 2 * (t - 2) + 2)
                for c in range(2):
                    for k in range(4):
                        last = nc.tensor.transpose(vp[0:n, 2 * (t % 2) + c, k * P:(k + 1) * P],
                                                   acc[:, 4 * c + k, t * P:t * P + n], ident[:, :])
                    last.then_inc(y_turned, 1)


def consts():
    f = np.float32
    half = RD // 2
    pos = np.concatenate([np.arange(SEQ), PAST + np.arange(DEC), np.zeros(TPAD - TOK)]).astype(f)
    inv = f(10000.0) ** (-np.arange(half, dtype=f) / f(half))
    ang = pos[:, None] * inv[None, :]
    g = np.array([1.0 - 2.0 ** (-5.0 - h) for h in range(RH)])
    m, l = np.arange(P)[:, None], np.arange(P)[None, :]
    decay = np.where((l >= m)[:, None, :], g[None, :, None] ** np.maximum(l - m, 0)[:, None, :], 0.0)
    q_dec = np.broadcast_to(g[None, :, None] ** (np.arange(P) + 1.0)[None, None, :], (P, RH, P))
    j = np.arange(P)[:, None]
    k_dec = np.stack([g ** (P - 1.0 - j) * KSCALE,
                      np.where(j < DEC, g ** np.maximum(DEC - 1.0 - j, 0), 0.0) * KSCALE], axis=1)
    return {"ident": np.eye(P, dtype=f), "flip": np.eye(P, dtype=f)[::-1], "cs": np.stack([np.cos(ang), np.sin(ang)], axis=1),
            "decay": decay.astype(f), "q_dec": q_dec.astype(f), "k_dec": k_dec.astype(f)}


def layout(a):
    rel = np.pad(a["attn_rel_bias"][0], ((0, 0), (BAND + P - 1 - CLIP, BAND + P - 1 - CLIP)), mode="edge")[:, ::-1]
    rel = rel[:, :P - 1 + BAND + P]
    u = a["peer_expert_u"][0].reshape(PK, PK, KD, P)
    return {
        "x": np.concatenate([a["x_prompt"][0], a["x_sample"][0], np.zeros((TPAD - TOK, D), np.float32)]),
        "ck": a["cache_attn_k"][0, 0].reshape(P, AW), "cv": a["cache_attn_v"][0, 0].reshape(P, AW),
        "state": a["state_retention"][0, 0], "mix_g": a["mix_norm_g"][0], "w_in": a["w_in"][0],
        "q_g": a["attn_q_norm_g"][0], "k_g": a["attn_k_norm_g"][0], "rel": rel,
        "r_g": a["ret_out_norm_g"][0].reshape(RW), "w_a": a["w_branch_attn"][0], "w_r": a["w_branch_ret"][0],
        "w_o": a["w_out"][0], "f_g": a["ffn_norm_g"][0], "w_q": a["peer_w_query"][0],
        "keys": a["peer_sub_keys"][0].reshape(HC, PK, P).transpose(2, 0, 1),
        "u": u.transpose(1, 3, 2, 0).reshape(PK, P, KD * PK),
        "v": a["peer_expert_v"][0],
    }


def program(nc, d):
    for name, shape in (("z", (TPAD, ZW)), ("x2", (TPAD, D)), ("h2T", (D, TPAD)), ("route", (P, 3, TPAD)),
                        ("gates", (PK, PK, TOK))):
        d[name] = nc.dram_tensor(f"scratch_{name}", shape, F32, kind="Internal").ap()
    project(nc, d)
    mix(nc, d)
    route(nc, d)
    spread(nc, d)
    experts(nc, d)


OUTPUTS = {"yp": ((SEQ, D), (1, SEQ, D)), "ys": ((DEC, D), (1, DEC, D)),
           "nkp": ((BAND, AW), (1, 1, BAND, AH, AD)), "nvp": ((BAND, AW), (1, 1, BAND, AH, AD)),
           "nsp": ((RH, RD, RD), (1, 1, RH, RD, RD)),
           "nks": ((DEC, AW), (1, 1, DEC, AH, AD)), "nvs": ((DEC, AW), (1, 1, DEC, AH, AD)),
           "nss": ((RH, RD, RD), (1, 1, RH, RD, RD))}


def kernel(**inputs):
    import concourse.bacc as bacc
    from concourse.bass_utils import run_bass_kernel_spmd

    nc = bacc.Bacc("TRN2", target_bir_lowering=False, num_devices=1)
    arrays, d = {}, {}
    for name, a in {**consts(), **layout({k: np.asarray(v) for k, v in inputs.items()})}.items():
        arrays[f"in_{name}"] = np.ascontiguousarray(a)
        d[name] = nc.dram_tensor(f"in_{name}", a.shape, mybir.dt.from_np(a.dtype), kind="ExternalInput").ap()
    for name, (shape, _) in OUTPUTS.items():
        d[name] = nc.dram_tensor(f"out_{name}", shape, F32, kind="ExternalOutput").ap()
    program(nc, d)
    r = run_bass_kernel_spmd(nc, [arrays], core_ids=[0])
    return tuple(r.results[0][f"out_{name}"].reshape(shape) for name, (_, shape) in OUTPUTS.items())
```

```python
import math
from contextlib import ExitStack

import numpy as np

import concourse.bass as bass
from concourse import mybir

F32 = mybir.dt.float32
BF16 = mybir.dt.bfloat16
F32R = mybir.dt.float32r
U32 = mybir.dt.uint32
ALU = mybir.AluOpType
ACT = mybir.ActivationFunctionType
AX = mybir.AxisListType

P = 128
D = 1024
KD = D // P
SEQ, DEC, PAST = 1024, 64, 128
NP = SEQ // P
NT = NP + 1
TOK = SEQ + DEC
TPAD = NT * P
EPS = 1e-6
AH, AD = 8, 64
AW = AH * AD
BAND = 512
BT = BAND // P
CLIP = 128
MASK = -1e30
RH, RD = 4, 128
RW = RH * RD
ZW = 3 * AW + 4 * RW + 2 * D
O_A, O_R, O_G = 0, 3 * AW, 3 * AW + 4 * RW
KSCALE = float(RD) ** -0.5
PH, PK, TOPK = 8, 128, 16
HC = 2 * PH
SLOTS = PH * TOPK
LOWEST = -3.0e38
CHUNK = 64


def at(start, size):
    return slice(start, start + size) if isinstance(start, int) else bass.ds(start, size)


def after(eng, sem, value):
    if not isinstance(value, int) or value > 0:
        eng.wait_ge(sem, value)


def across(row, parts=P):
    return bass.AP(row.tensor, row.offset, [[0, parts]] + [list(x) for x in row.ap])


class Stage:

    def __init__(self, nc, name):
        self.nc, self.name, self.ctx, self.sems = nc, name, ExitStack(), []

    def __enter__(self):
        self.ctx.__enter__()
        return self

    def __exit__(self, *e):
        self.ctx.__exit__(*e)
        self.nc.clear_and_free_semaphores(self.sems)
        self.nc.all_engine_barrier()

    def sb(self, name, shape, dt=F32):
        return self.ctx.enter_context(self.nc.sbuf_tensor(f"{self.name}_{name}", shape, dt))

    def pb(self, name, shape):
        return self.ctx.enter_context(self.nc.psum_tensor(f"{self.name}_{name}", shape, F32))

    def sem(self, name):
        self.sems.append(self.nc.alloc_semaphore(name=f"{self.name}_{name}"))
        return self.sems[-1]

    def block(self):
        return self.ctx.enter_context(self.nc.Block())


def project(nc, d):
    NB = ZW // 512
    GR = 3
    GN = NT // GR
    with Stage(nc, "prj") as s:
        x = s.sb("x", [P, 2, GN, D])
        gain = s.sb("gain", [P, D])
        ident = s.sb("ident", [P, P])
        half = s.sb("half", [P, GN])
        ms = s.sb("ms", [P, NT])
        rs = s.sb("rs", [P, NT])
        h = s.sb("h", [P, GN, D])
        hT = [s.sb("hT_hi", [P, KD, TPAD], F32R), s.sb("hT_lo", [P, KD, TPAD], F32R)]
        w_hi = s.sb("w_hi", [P, 2, KD, 512], F32R)
        w_lo = s.sb("w_lo", [P, 2, KD, 512], F32R)
        w_raw = s.sb("w_raw", [P, 2, 2, 512])
        zo = s.sb("zo", [P, NT, 512])
        sq = zo[:, NT - 2:NT, :].rearrange("p a b -> p (a b)")
        tp = s.pb("tp", [P, 3, 512])
        zp = s.pb("zp", [P, 5, 512])
        gain_in, ident_in = s.sem("gain_in"), s.sem("ident_in")
        x_in = [s.sem(f"x_in{g}") for g in range(GR)]
        w_in = [s.sem("w_in0"), s.sem("w_in1")]
        half_set, squared, mean_ready, rs_ready = s.sem("half_set"), s.sem("squared"), s.sem("mean_ready"), s.sem("rs_ready")
        h_ready, turned, hT_hi_ready, hT_lo_ready = s.sem("h_ready"), s.sem("turned"), s.sem("hT_hi_ready"), s.sem("hT_lo_ready")
        w_hi_ready, w_lo_ready = s.sem("w_hi_ready"), s.sem("w_lo_ready")
        z_ready, z_out = s.sem("z_ready"), s.sem("z_out")
        z_stored = [s.sem(f"z_stored{n}") for n in range(GR)]
        CH = KD // 2
        bank = lambda i: 4 if i == 8 else i % 4
        block = s.block()

        @block.sync
        def _(sp):
            w_v = d["w_in"].rearrange("(k p) n -> p k n", p=P)

            def load(b):
                for c in range(CH):
                    after(sp, w_lo_ready, CH * b + c - 1)
                    sp.dma_start(w_raw[:, c % 2, :, :], w_v[:, 2 * c:2 * c + 2, at(b * 512, 512)]).then_inc(w_in[c % 2], 16)

            def load_x(g):
                after(sp, h_ready, GN * (g - 1))
                sp.dma_start(x[:, g % 2, :, :], d["x"].rearrange("(n p) c -> p n c", p=P)[:, GN * g:GN * g + GN, :]
                             ).then_inc(x_in[g], 16)

            load_x(0)
            sp.dma_start(ident[:, :], d["ident"]).then_inc(ident_in, 16)
            sp.dma_start(gain[:, :], across(d["mix_g"])).then_inc(gain_in, 16)
            load(0)
            load_x(1)
            load_x(2)
            with sp.Fori(1, NB) as b:
                load(b)

        @block.gpsimd
        def _(pool):
            nc.gpsimd.memset(half[:, :], -0.5).then_inc(half_set, 1)
            pool.wait_ge(half_set, 1)
            for g in range(GR):
                pool.wait_ge(mean_ready, g + 1)
                nc.gpsimd.tensor_tensor(rs[:, GN * g:GN * g + GN], ms[:, GN * g:GN * g + GN], half[:, :], ALU.pow).then_inc(rs_ready, 1)

        @block.scalar
        def _(act):
            z_v = d["z"].rearrange("(n p) c -> p n c", p=P)

            def squares(g):
                act.wait_ge(x_in[g], 16)
                for i in range(GN * g, GN * g + GN):
                    after(act, squared, i)
                    nc.scalar.activation(sq, x[:, g % 2, i - GN * g, :], ACT.Square, accum_out=ms[:, i:i + 1]).then_inc(squared, 1)

            def high_h(g):
                for u in range(2 * GN):
                    i, c = GN * g + u // 2, u % 2
                    act.wait_ge(turned, 2 * i + c + 1)
                    nc.scalar.copy(hT[0][:, 4 * c:4 * c + 4, i * P:(i + 1) * P],
                                   tp[:, u % 3, :].rearrange("p (k t) -> p k t", k=4)).then_inc(hT_hi_ready, 1)

            def high_w(b, slot, chunks=range(CH)):
                for c in chunks:
                    act.wait_ge(w_in[c % 2], 32 * b + 16 * (c // 2) + 16)
                    after(act, z_ready, NT * (b - 1))
                    nc.scalar.copy(w_hi[:, slot, 2 * c:2 * c + 2, :], w_raw[:, c % 2, :, :]).then_inc(w_hi_ready, 1)

            def out(b, tiles):
                for i in tiles:
                    act.wait_ge(z_ready, NT * b + i + 1)
                    after(act, z_stored[i // GN], 16 * b)
                    nc.scalar.copy(zo[:, i, :], zp[:, bank(i), :]).then_inc(z_out, 1)
                    if i % GN == GN - 1:
                        act.wait_ge(z_out, NT * b + i + 1)
                        act.dma_start(z_v[:, i - GN + 1:i + 1, at(b * 512, 512)],
                                      zo[:, i - GN + 1:i + 1, :]).then_inc(z_stored[i // GN], 16)

            def step(b, slot, last=False):
                out(b, range(0, 3))
                if not last:
                    high_w(b + 1, 1 - slot, (0, 1))
                out(b, range(3, 5))
                if not last:
                    high_w(b + 1, 1 - slot, (2, 3))
                out(b, range(5, NT))

            squares(0)
            high_h(0)
            high_w(0, 0)
            squares(1)
            out(0, (0, 1))
            high_h(1)
            squares(2)
            out(0, (2, 3, 4))
            high_h(2)
            high_w(1, 1)
            out(0, (5, 6, 7, 8))
            with act.Fori(0, NB // 2 - 1) as pair:
                step(2 * pair + 1, 1)
                step(2 * pair + 2, 0)
            step(NB - 2, 1)
            step(NB - 1, 0, last=True)
            for g in range(GR):
                act.wait_ge(z_stored[g], 16 * NB)

        @block.vector
        def _(dve):
            V = nc.vector

            def norm(g):
                dve.wait_ge(squared, GN * g + GN)
                V.tensor_scalar(ms[:, GN * g:GN * g + GN], ms[:, GN * g:GN * g + GN], 1.0 / D, EPS, ALU.mult, ALU.add
                                ).then_inc(mean_ready, 1)
                dve.wait_ge(rs_ready, g + 1)
                for u in range(GN):
                    i = GN * g + u
                    after(dve, turned, 2 * (i - GN) + 2)
                    V.scalar_tensor_tensor(out=h[:, u, :], in0=x[:, g % 2, u, :], scalar=rs[:, i:i + 1], in1=gain[:, :],
                                           op0=ALU.mult, op1=ALU.mult).then_inc(h_ready, 1)

            def low_h(g):
                for u in range(2 * GN):
                    i, c = GN * g + u // 2, u % 2
                    dve.wait_ge(hT_hi_ready, 2 * i + c + 1)
                    V.tensor_tensor(hT[1][:, 4 * c:4 * c + 4, i * P:(i + 1) * P], tp[:, u % 3, :].rearrange("p (k t) -> p k t", k=4),
                                    hT[0][:, 4 * c:4 * c + 4, i * P:(i + 1) * P].bitcast(F32), ALU.subtract).then_inc(hT_lo_ready, 1)

            def low_w(b, slot):
                for c in range(CH):
                    dve.wait_ge(w_hi_ready, CH * b + c + 1)
                    V.tensor_tensor(w_lo[:, slot, 2 * c:2 * c + 2, :], w_raw[:, c % 2, :, :],
                                    w_hi[:, slot, 2 * c:2 * c + 2, :].bitcast(F32), ALU.subtract).then_inc(w_lo_ready, 1)

            dve.wait_ge(gain_in, 16)
            norm(0)
            low_h(0)
            low_w(0, 0)
            norm(1)
            low_h(1)
            norm(2)
            low_h(2)
            low_w(1, 1)
            with dve.Fori(1, NB // 2) as pair:
                low_w(2 * pair, 0)
                low_w(2 * pair + 1, 1)
            low_w(NB - 1, 0)

        @block.tensor
        def _(pe):
            pe.wait_ge(ident_in, 16)
            passes = ((0, 0), (0, 1), (1, 0))

            def turn(g):
                for u in range(2 * GN):
                    i, c = GN * g + u // 2, u % 2
                    pe.wait_ge(h_ready, i + 1)
                    after(pe, hT_lo_ready, 2 * i + c - 2)
                    for k in range(4):
                        last = nc.tensor.transpose(tp[:, u % 3, k * P:(k + 1) * P],
                                                   h[:, u // 2, (4 * c + k) * P:(4 * c + k + 1) * P], ident[:, :])
                    last.then_inc(turned, 1)

            def multiply(b, slot, tiles=range(NT)):
                for i in tiles:
                    if isinstance(b, int) and b == 0:
                        pe.wait_ge(hT_lo_ready, 2 * i + 2)
                    before = i + 4 - NT if i < 4 else i - 4 if i < 8 else -1
                    after(pe, z_out, NT * b + before + 1)
                    for k in range(KD):
                        if i == 0 and k % 2 == 0:
                            pe.wait_ge(w_lo_ready, CH * b + k // 2 + 1)
                        for n, (p, q) in enumerate(passes):
                            last = nc.tensor.matmul(zp[:, bank(i), :], hT[p][:, k, i * P:(i + 1) * P],
                                                    (w_hi, w_lo)[q][:, slot, k, :],
                                                    start=(k == 0 and n == 0), stop=(k == KD - 1 and n == 2))
                    last.then_inc(z_ready, 1)

            turn(0)
            multiply(0, 0, (0, 1))
            turn(1)
            multiply(0, 0, (2, 3, 4))
            turn(2)
            multiply(0, 0, (5, 6, 7, 8))
            with pe.Fori(0, NB // 2) as pair:
                multiply(2 * pair + 1, 1)
                multiply(2 * pair + 2, 0)


def gammas():
    return [1.0 - 2.0 ** (-5.0 - h) for h in range(RH)]


def mix(nc, d):
    with Stage(nc, "mix") as s:
        w_a = s.sb("w_a", [P, AW // P, D])
        w_r = s.sb("w_r", [P, RW // P, D])
        w_o = s.sb("w_o", [P, KD, D])
        ident = s.sb("ident", [P, P])
        bias8 = s.sb("bias8", [P, AH, (BT + 1) * P])
        keysT = s.sb("keysT", [P, AH // 2, NP * P])
        vals = s.sb("vals", [P, NP, AW])
        qpad = s.sb("qpad", [P, AH, P])
        za = s.sb("za", [P, 3 * AW])
        zqk = s.sb("zqk", [P, 2 * RW])
        zvg = s.sb("zvg", [P, 2 * RW])
        zg = s.sb("zg", [P, 2 * D])
        x = s.sb("x", [P, D])
        cs = s.sb("cs", [P, 2, RD // 2])
        sq = s.sb("sq", [P, D])
        qk = s.sb("qk", [P, 2 * AW])
        g_qk = s.sb("g_qk", [P, 2, AD])
        g_r = s.sb("g_r", [P, RW])
        g_f = s.sb("g_f", [P, D])
        part = s.sb("part", [P, KD, P])
        rot = s.sb("rot", [P, 2 * RH, RD])
        rqT = s.sb("rqT", [P, RH, P])
        rqdT = s.sb("rqdT", [P, RH, P])
        rkT = s.sb("rkT", [P, RH, P])
        inner = s.sb("inner", [P, RH, P])
        decay = s.sb("decay", [P, RH, P])
        q_dec = s.sb("q_dec", [P, RH, P])
        k_dec = s.sb("k_dec", [P, 2, RH])
        state = s.sb("state", [P, 2, RH, RD])
        ro = s.sb("ro", [P, RW])
        r_gate = s.sb("r_gate", [P, RW])
        sc = s.sb("sc", [P, 2, (BT + 1) * P])
        pT = s.sb("pT", [P, 2, BT + 1, P])
        oa = s.sb("oa", [P, AW])
        tT = s.sb("tT", [P, KD, P])
        half = s.sb("half", [P, 16])
        qk_ms, qk_rs = s.sb("qk_ms", [P, 16]), s.sb("qk_rs", [P, 16])
        r_ms, r_rs = s.sb("r_ms", [P, RH]), s.sb("r_rs", [P, RH])
        f_ms, f_rs = s.sb("f_ms", [P, 1]), s.sb("f_rs", [P, 1])
        neg_max, den, rden = s.sb("neg_max", [P, AH]), s.sb("den", [P, AH]), s.sb("rden", [P, AH])
        S = s.pb("S", [P, 2, 1024])
        X = s.pb("X", [P, 3, 512])
        M = s.pb("M", [P, 512])
        heads4 = lambda ap: ap.rearrange("p (h e) -> p h e", h=RH)
        four = lambda ap: ap.rearrange("p (k t) -> p k t", k=4)
        BW = (BT + 1) * P
        mark = s.sb("mark", [P, AH])
        flip = s.sb("flip", [P, P])
        bias_rev = w_o[:, :, :].rearrange("p k n -> p (k n)")[:, 0:AH * BW].rearrange("p (h n) -> p h n", h=AH)
        names = """ident_in w_a_in w_r_in w_o_in bias_in bias_turned const_in cache_in za_in zqk_in zvg_in zg_in x_in state_in
            bias_set zeros_set halves_set
            qk_squared qk_summed qk_mean qk_rs_ready qk_scaled qk_ready v_ready
            q_turned k_turned q_padded keys_ready cache_turned
            rot_part rotated rq_turned rk_turned rq_ready rqd_ready rk_ready k_decayed
            inner_ready inner_scaled ret_ready ret_out update_ready state_ready
            r_squared r_summed r_mean r_rs_ready r_scaled r_gate_in r_silu r_gained r_ready
            scores_ready softmax_in p_ready p_turned p_out o_ready den_ready oa_ready
            oa_turned r_turned oa_out r_out gates_ready
            branch_ready gated merged m_turned m_out proj_ready x2_ready
            f_squared f_mean f_rs_ready h2_ready h2_turned h2_out
            k_stored v_stored x2_stored h2_stored state_stored""".split()
        (ident_in, w_a_in, w_r_in, w_o_in, bias_in, bias_turned, const_in, cache_in, za_in, zqk_in, zvg_in, zg_in, x_in, state_in,
         bias_set, zeros_set, halves_set,
         qk_squared, qk_summed, qk_mean, qk_rs_ready, qk_scaled, qk_ready, v_ready,
         q_turned, k_turned, q_padded, keys_ready, cache_turned,
         rot_part, rotated, rq_turned, rk_turned, rq_ready, rqd_ready, rk_ready, k_decayed,
         inner_ready, inner_scaled, ret_ready, ret_out, update_ready, state_ready,
         r_squared, r_summed, r_mean, r_rs_ready, r_scaled, r_gate_in, r_silu, r_gained, r_ready,
         scores_ready, softmax_in, p_ready, p_turned, p_out, o_ready, den_ready, oa_ready,
         oa_turned, r_turned, oa_out, r_out, gates_ready,
         branch_ready, gated, merged, m_turned, m_out, proj_ready, x2_ready,
         f_squared, f_mean, f_rs_ready, h2_ready, h2_turned, h2_out,
         k_stored, v_stored, x2_stored, h2_stored, state_stored) = [s.sem(n) for n in names]
        block = s.block()

        def steps(eng, step):
            for i in range(BT):
                step(i, i)
            with eng.Fori(BT, NP - 1) as i:
                step(i, BT)
            step(NP - 1, BT)
            step(NP, 1)
            step(NP + 1, 0)
            step(NP + 2, 0)

        def has(i):
            return not isinstance(i, int) or 0 <= i < NT

        def sample(i):
            return isinstance(i, int) and i == NP

        def width(i, past):
            return P + DEC if sample(i) else (past + 1) * P

        @block.sync
        def _(sp):
            sp.sem_inc(k_stored, 16)
            sp.dma_start(ident[:, :], d["ident"]).then_inc(ident_in, 16)
            sp.dma_start(flip[:, :], d["flip"]).then_inc(ident_in, 16)

            def load_z(m):
                after(sp, qk_squared, m)
                after(sp, qk_scaled, m)
                after(sp, v_ready, m)
                sp.dma_start(za[:, :], d["z"][at(m * P, P), O_A:O_R]).then_inc(za_in, 16)
                after(sp, rotated, m)
                sp.dma_start(zqk[:, :], d["z"][at(m * P, P), O_R:O_R + 2 * RW]).then_inc(zqk_in, 16)
                sp.dma_start(cs[:, :, :], d["cs"][at(m * P, P), :, :]).then_inc(zqk_in, 16)

            def load_vg(m):
                after(sp, update_ready, m)
                after(sp, r_silu, m)
                sp.dma_start(zvg[:, :], d["z"][at(m * P, P), O_R + 2 * RW:O_G]).then_inc(zvg_in, 16)

            load_z(0)
            rel = d["rel"]
            sp.dma_start(bias_rev, bass.AP(rel.tensor, rel.offset, [[1, P], [rel.shape[1], AH], [1, BW]])).then_inc(bias_in, 16)
            for out, src in ((g_qk[:, 0, :], across(d["q_g"])), (g_qk[:, 1, :], across(d["k_g"])),
                             (g_r[:, :], across(d["r_g"])), (g_f[:, :], across(d["f_g"])),
                             (decay[:, :, :], d["decay"]), (q_dec[:, :, :], d["q_dec"]), (k_dec[:, :, :], d["k_dec"])):
                sp.dma_start(out, src).then_inc(const_in, 16)
            load_vg(0)
            sp.dma_start(state[:, 1, :, :], d["state"].rearrange("h d e -> d h e")).then_inc(state_in, 16)
            w_v = [d[n].rearrange("(k p) n -> p k n", p=P) for n in ("w_a", "w_r", "w_o")]
            sp.dma_start(w_a[:, :, :], w_v[0]).then_inc(w_a_in, 16)

            def step(i, past):
                m = i - 1
                row = i * P if isinstance(i, int) else sp.snap((i + 1 - BT) * P)
                if has(i - 2):
                    sp.wait_ge(x2_ready, 2 * (i - 2) + 2)
                    sp.dma_start(d["x2"][at((i - 2) * P, P), :], x[:, :]).then_inc(x2_stored, 16)
                if has(m):
                    after(sp, x2_stored, 16 * m)
                    after(sp, h2_ready, m)
                    sp.dma_start(x[:, :], d["x"][at(m * P, P), :]).then_inc(x_in, 16)
                if has(i + 1):
                    load_z(i + 1)
                    if not isinstance(i, int) or i + 1 >= BT:
                        if isinstance(i, int):
                            row = (i + 1 - BT) * P
                        kd, vd, n, slot = ((d["nks"], d["nvs"], DEC, 1) if sample(i + 1) else
                                           (d["nkp"][at(row, P), :], d["nvp"][at(row, P), :], P, i + 1))
                        sp.wait_ge(qk_ready, i + 2)
                        sp.dma_start(kd, qk[0:n, AW:2 * AW]).then_inc(k_stored, 16)
                        sp.wait_ge(v_ready, i + 2)
                        sp.dma_start(vd, vals[0:n, slot, :]).then_inc(v_stored, 16)
                if has(i):
                    after(sp, m_turned, 2 * i)
                    sp.dma_start(zg[:, :], d["z"][at(i * P, P), O_G:ZW]).then_inc(zg_in, 16)
                if isinstance(i, int) and i == 0:
                    sp.dma_start(w_r[:, :, :], w_v[1]).then_inc(w_r_in, 16)
                if has(i + 1):
                    load_vg(i + 1)
                if isinstance(i, int) and i == 0:
                    sp.wait_ge(bias_set, AH)
                    sp.dma_start(w_o[:, :, :], w_v[2]).then_inc(w_o_in, 16)
                if isinstance(i, int) and i == NP - 1:
                    sp.wait_ge(state_ready, RH * NP)
                    sp.dma_start(d["nsp"].rearrange("h d e -> d h e"), state[:, 0, :, :]).then_inc(state_stored, 16)
                if sample(i):
                    sp.wait_ge(state_ready, RH * NT)
                    sp.dma_start(d["nss"].rearrange("h d e -> d h e"), state[:, 1, :, :]).then_inc(state_stored, 16)

            for i in range(BT):
                step(i, i)
            with sp.Fori(BT, NP - 1) as i:
                step(i, BT)
            sp.wait_ge(o_ready, AH * (BT + 1))
            sp.dma_start(vals[:, 0, :], d["cv"]).then_inc(cache_in, 16)
            sp.wait_ge(k_turned, NP)
            sp.wait_ge(k_stored, 16 * (NP - BT) + 16)
            sp.dma_start(qk[:, AW:2 * AW], d["ck"]).then_inc(cache_in, 16)
            step(NP - 1, BT)
            step(NP, 1)
            step(NP + 1, 0)
            step(NP + 2, 0)
            sp.wait_ge(x2_stored, 16 * NT)
            sp.wait_ge(state_stored, 32)
            sp.wait_ge(k_stored, 16 * (NP - BT + 1) + 16)
            sp.wait_ge(v_stored, 16 * (NP - BT + 1))

        @block.gpsimd
        def _(pool):
            nc.gpsimd.memset(half[:, :], -0.5).then_inc(halves_set, 1)
            pool.wait_ge(halves_set, 1)

            def prepare(m):
                slot = 1 if sample(m) else m
                pool.wait_ge(za_in, 16 * m + 16)
                after(pool, h2_turned, 2 * (m - 2))
                nc.gpsimd.tensor_tensor(sq[:, :], za[:, 0:2 * AW], za[:, 0:2 * AW], ALU.mult).then_inc(qk_squared, 1)
                nc.gpsimd.tensor_copy(vals[:, slot, :], za[:, 2 * AW:3 * AW]).then_inc(v_ready, 1)
                pool.wait_ge(qk_mean, m + 1)
                nc.gpsimd.tensor_tensor(qk_rs[:, :], qk_ms[:, :], half[:, :], ALU.pow).then_inc(qk_rs_ready, 1)

            def rotary(m):
                pool.wait_ge(zqk_in, 32 * m + 32)
                after(pool, update_ready, m)
                after(pool, h2_stored, 16 * (m - 2))
                xv = zqk[:, :].rearrange("p (h c e) -> p h c e", h=2 * RH, c=2)
                x1, x2_ = xv[:, :, 0, :], xv[:, :, 1, :]
                pa, pb_ = [part[:, 4 * c:4 * c + 4, :].rearrange("p k (c e) -> p (k c) e", c=2) for c in range(2)]
                cos = cs[:, 0:1, :].broadcast_to([P, 2 * RH, RD // 2])
                sin = cs[:, 1:2, :].broadcast_to([P, 2 * RH, RD // 2])
                for n, (a, ta, b, tb, op, out) in enumerate(((x1, cos, x2_, sin, ALU.subtract, rot[:, :, 0:RD // 2]),
                                                             (x1, sin, x2_, cos, ALU.add, rot[:, :, RD // 2:RD]))):
                    nc.gpsimd.tensor_tensor(pa, a, ta, ALU.mult).then_inc(rot_part, 1)
                    nc.gpsimd.tensor_tensor(pb_, b, tb, ALU.mult).then_inc(rot_part, 1)
                    pool.wait_ge(rot_part, 5 * m + 3 * n + 2)
                    nc.gpsimd.tensor_tensor(out, pa, pb_, op).then_inc(rot_part if n == 0 else rotated, 1)
                    if n == 0:
                        pool.wait_ge(rot_part, 5 * m + 3)

            def step(i, past):
                if has(i):
                    pool.wait_ge(rotated, i + 1)
                    pool.wait_ge(rk_turned, i + 1)
                    kdec = k_dec[:, 1 if sample(i) else 0, :].rearrange("p (h o) -> p h o", o=1).broadcast_to([P, RH, RD])
                    nc.gpsimd.tensor_tensor(rot[:, RH:, :], rot[:, RH:, :], kdec, ALU.mult).then_inc(k_decayed, 1)
                if has(i + 1):
                    prepare(i + 1)
                if has(i):
                    pool.wait_ge(ret_out, i + 1)
                    if has(i + 1):
                        pool.wait_ge(qk_summed, i + 2)
                    else:
                        pool.wait_ge(h2_turned, 2 * (i - 1))
                    nc.gpsimd.tensor_tensor(sq[:, 0:RW], ro[:, :], ro[:, :], ALU.mult).then_inc(r_squared, 1)
                if has(i + 1):
                    rotary(i + 1)
                if has(i):
                    pool.wait_ge(r_mean, i + 1)
                    nc.gpsimd.tensor_tensor(r_rs[:, :], r_ms[:, :], half[:, 0:RH], ALU.pow).then_inc(r_rs_ready, 1)
                if has(i - 1):
                    pool.wait_ge(f_mean, i)
                    nc.gpsimd.tensor_tensor(f_rs[:, :], f_ms[:, :], half[:, 0:1], ALU.pow).then_inc(f_rs_ready, 1)

            nc.gpsimd.memset(qpad[:, :, :], 0.0).then_inc(zeros_set, 1)
            nc.gpsimd.memset(state[:, 0, :, :], 0.0).then_inc(zeros_set, 1)
            prepare(0)
            rotary(0)
            pool.wait_ge(const_in, 7 * 16)
            steps(pool, step)

        @block.scalar
        def _(act):
            def prepare(m):
                if sample(m):
                    act.wait_ge(cache_turned, 1)
                    nc.scalar.copy(keysT[:, :, 0:P], four(X[:, 1, :])).then_inc(keys_ready, 1)
                slot = 1 if sample(m) else m
                act.wait_ge(q_turned, m + 1)
                act.wait_ge(zeros_set, 2)
                for odd in range(2):
                    rows = slice(64 * odd, 64 * odd + 64)
                    nc.scalar.copy(qpad[rows, odd:AH:2, :], four(X[rows, 1, :])).then_inc(q_padded, 1)
                act.wait_ge(k_turned, m + 1)
                nc.scalar.copy(keysT[:, :, at(slot * P, P)], four(X[:, 1, :])).then_inc(keys_ready, 1)

            def swish_gate(m):
                act.wait_ge(zvg_in, 16 * m + 16)
                after(act, r_ready, m)
                nc.scalar.activation(r_gate[:, :], zvg[:, RW:2 * RW], ACT.Sigmoid).then_inc(r_gate_in, 1)

            def step(i, past):
                def exp(h):
                    if has(i) and h < AH:
                        W = width(i, past)
                        act.wait_ge(softmax_in, AH * i + h + 1)
                        if h == 0:
                            after(act, den_ready, i)
                        nc.scalar.activation(sc[:, h % 2, 0:W], sc[:, h % 2, 0:W], ACT.Exp, scale=-1.0,
                                             bias=neg_max[:, h:h + 1], accum_out=den[:, h:h + 1]).then_inc(p_ready, 1)

                def probs_out(h):
                    if has(i):
                        act.wait_ge(p_turned, AH * i + h + 1)
                        after(act, o_ready, AH * i + h - 1)
                        if sample(i):
                            nc.scalar.copy(pT[:, h % 2, 0, :], S[:, h % 2, 0:P])
                            nc.scalar.copy(pT[0:DEC, h % 2, 1, :], S[0:DEC, h % 2, P:2 * P]).then_inc(p_out, 1)
                        else:
                            nc.scalar.copy(pT[:, h % 2, 0:past + 1, :].rearrange("p k t -> p (k t)"),
                                           S[:, h % 2, 0:(past + 1) * P]).then_inc(p_out, 1)

                def h2_halves(b):
                    if has(i - 2):
                        if b == 0 and has(i):
                            act.wait_ge(rotated, i + 1)
                        elif b == 0:
                            act.wait_ge(h2_stored, 16 * (i - 2))
                        act.wait_ge(h2_turned, 2 * (i - 2) + b + 1)
                        nc.scalar.copy(part[:, 4 * b:4 * b + 4, :], four(X[:, (0, 1)[b], :])).then_inc(h2_out, 1)
                        if b == 1:
                            act.wait_ge(h2_out, 2 * (i - 2) + 2)
                            act.dma_start(d["h2T"].rearrange("(k p) t -> p k t", p=P)[:, :, at((i - 2) * P, P)], part[:, :, :]
                                          ).then_inc(h2_stored, 16)

                exp(0)
                if has(i):
                    act.wait_ge(rq_turned, i + 1)
                    after(act, ret_ready, i)
                    nc.scalar.copy(rqT[:, :, :], heads4(X[:, 2, :])).then_inc(rq_ready, 1)
                    act.wait_ge(rk_turned, i + 1)
                    nc.scalar.activation(rkT[:, :, :], heads4(X[:, 0, :]), ACT.Copy, scale=KSCALE).then_inc(rk_ready, 1)
                exp(1)
                if has(i - 1):
                    act.wait_ge(r_turned, i)
                    nc.scalar.copy(tT[:, 4:8, :], four(X[:, 1, :])).then_inc(r_out, 1)
                    act.wait_ge(oa_turned, i)
                    nc.scalar.copy(tT[:, 0:4, :], four(X[:, 2, :])).then_inc(oa_out, 1)
                probs_out(0)
                if has(i):
                    act.wait_ge(ret_ready, i + 1)
                    nc.scalar.copy(ro[:, :], X[:, 0, :]).then_inc(ret_out, 1)
                for h in range(1, 6):
                    exp(h + 1)
                    probs_out(h)
                    if h < 3:
                        h2_halves(h - 1)
                exp(7)
                probs_out(6)
                if has(i - 1):
                    for b in range(2):
                        act.wait_ge(m_turned, 2 * (i - 1) + b + 1)
                        nc.scalar.copy(tT[:, 4 * b:4 * b + 4, :], four(X[:, (0, 1)[b], :])).then_inc(m_out, 1)
                probs_out(7)
                if has(i + 1):
                    prepare(i + 1)
                if has(i):
                    act.wait_ge(zg_in, 16 * i + 16)
                    nc.scalar.activation(zg[:, :], zg[:, :], ACT.Sigmoid).then_inc(gates_ready, 1)
                if has(i + 1):
                    swish_gate(i + 1)

            swish_gate(0)
            prepare(0)
            steps(act, step)
            act.wait_ge(h2_stored, 16 * NT)

        @block.vector
        def _(dve):
            V = nc.vector

            def norms_mean(m):
                dve.wait_ge(qk_squared, m + 1)
                V.tensor_reduce(qk_ms[:, :], sq[:, :].rearrange("p (h e) -> p h e", e=AD), AX.X, ALU.add).then_inc(qk_summed, 1)
                dve.wait_ge(qk_summed, m + 1)
                V.tensor_scalar(qk_ms[:, :], qk_ms[:, :], 1.0 / AD, EPS, ALU.mult, ALU.add).then_inc(qk_mean, 1)

            def norms_scale(m):
                dve.wait_ge(qk_rs_ready, m + 1)
                if sample(m):
                    dve.wait_ge(cache_turned, 1)
                after(dve, k_turned, m)
                if not isinstance(m, int) or m > BT:
                    dve.wait_ge(k_stored, 16 * (m - BT) + 16)
                V.tensor_tensor(qk[:, :].rearrange("p (h e) -> p h e", e=AD), za[:, 0:2 * AW].rearrange("p (h e) -> p h e", e=AD),
                                qk_rs[:, :].rearrange("p (h o) -> p h o", o=1).broadcast_to([P, 2 * AH, AD]), ALU.mult
                                ).then_inc(qk_scaled, 1)
                dve.wait_ge(qk_scaled, m + 1)
                qk4 = qk[:, :].rearrange("p (c h e) -> p c h e", c=2, e=AD)
                gq = g_qk[:, :, :].rearrange("p c (o e) -> p c o e", o=1).broadcast_to([P, 2, AH, AD])
                V.tensor_tensor(qk4, qk4, gq, ALU.mult).then_inc(qk_ready, 1)

            def step(i, past):
                st = 1 if sample(i) else 0
                b0 = (BT - past) * P

                def softmax(h):
                    if has(i):
                        W = width(i, past)
                        dve.wait_ge(scores_ready, AH * i + h + 1)
                        after(dve, p_turned, AH * i + h - 1)
                        V.memset(mark[:, h:h + 1], 0.0)
                        V.tensor_tensor_reduce(out=sc[:, h % 2, 0:W], in0=S[:, h % 2, 0:W], in1=bias8[:, h, b0:b0 + W],
                                               scale=-float(AD) ** -0.5, scalar=-LOWEST, op0=ALU.add, op1=ALU.min,
                                               accum_out=neg_max[:, h:h + 1]).then_inc(softmax_in, 1)

                def gate(n):
                    if has(i - 1):
                        dve.wait_ge(gates_ready, i)
                        dve.wait_ge(branch_ready, 4 * (i - 1) + n + 1)
                        V.tensor_tensor(zg[:, n * 512:(n + 1) * 512], zg[:, n * 512:(n + 1) * 512], X[:, (2, 0, 1, 2)[n], :],
                                        ALU.mult).then_inc(gated, 1)

                softmax(0)
                softmax(1)
                if has(i - 2):
                    dve.wait_ge(f_rs_ready, i - 1)
                    V.scalar_tensor_tensor(out=sq[:, :], in0=x[:, :], scalar=f_rs[:, 0:1], in1=g_f[:, :],
                                           op0=ALU.mult, op1=ALU.mult).then_inc(h2_ready, 1)
                if has(i):
                    dve.wait_ge(rq_ready, i + 1)
                    V.tensor_tensor(rqdT[:, :, :], rqT[:, :, :], q_dec[:, :, :], ALU.mult).then_inc(rqd_ready, 1)
                    dve.wait_ge(inner_ready, i + 1)
                    V.tensor_tensor(inner[:, :, :], heads4(X[:, 0, :]), decay[:, :, :], ALU.mult).then_inc(inner_scaled, 1)
                    dve.wait_ge(r_gate_in, i + 1)
                    V.tensor_tensor(r_gate[:, :], r_gate[:, :], zvg[:, RW:2 * RW], ALU.mult).then_inc(r_silu, 1)
                softmax(2)
                if has(i):
                    dve.wait_ge(update_ready, i + 1)
                    for h in range(RH):
                        g_l = gammas()[h] ** (DEC if sample(i) else P)
                        V.scalar_tensor_tensor(out=state[:, st, h, :], in0=state[:, st, h, :], scalar=g_l,
                                               in1=X[:, 1, h * RD:(h + 1) * RD], op0=ALU.mult, op1=ALU.add).then_inc(state_ready, 1)
                softmax(3)
                gate(0)
                if has(i + 1):
                    norms_mean(i + 1)
                softmax(4)
                gate(1)
                softmax(5)
                gate(2)
                if has(i):
                    dve.wait_ge(r_squared, i + 1)
                    V.tensor_reduce(r_ms[:, :], heads4(sq[:, 0:RW]), AX.X, ALU.add).then_inc(r_summed, 1)
                    dve.wait_ge(r_summed, i + 1)
                    V.tensor_scalar(r_ms[:, :], r_ms[:, :], 1.0 / RD, EPS, ALU.mult, ALU.add).then_inc(r_mean, 1)
                softmax(6)
                gate(3)
                if has(i - 1):
                    dve.wait_ge(gated, 4 * i)
                    V.tensor_tensor(zg[:, 0:D], zg[:, 0:D], zg[:, D:2 * D], ALU.add).then_inc(merged, 1)
                softmax(7)
                if has(i + 1):
                    norms_scale(i + 1)
                if has(i):
                    dve.wait_ge(r_rs_ready, i + 1)
                    dve.wait_ge(ret_out, i + 1)
                    V.tensor_tensor(heads4(ro[:, :]), heads4(ro[:, :]),
                                    r_rs[:, :].rearrange("p (h o) -> p h o", o=1).broadcast_to([P, RH, RD]), ALU.mult).then_inc(r_scaled, 1)
                    dve.wait_ge(r_scaled, i + 1)
                    V.tensor_tensor(ro[:, :], ro[:, :], g_r[:, :], ALU.mult).then_inc(r_gained, 1)
                    dve.wait_ge(r_gained, i + 1)
                    dve.wait_ge(r_silu, i + 1)
                    V.tensor_tensor(ro[:, :], ro[:, :], r_gate[:, :], ALU.mult).then_inc(r_ready, 1)
                    dve.wait_ge(p_ready, AH * i + AH)
                    V.reciprocal(rden[:, :], den[:, :]).then_inc(den_ready, 1)
                    dve.wait_ge(den_ready, i + 1)
                    dve.wait_ge(o_ready, AH * i + AH)
                    V.tensor_tensor(oa[:, :].rearrange("p (h e) -> p h e", e=AD), M[:, :].rearrange("p (h e) -> p h e", e=AD),
                                    rden[:, :].rearrange("p (h o) -> p h o", o=1).broadcast_to([P, AH, AD]), ALU.mult
                                    ).then_inc(oa_ready, 1)
                if has(i - 1):
                    dve.wait_ge(x_in, 16 * i)
                    for n in range(2):
                        dve.wait_ge(proj_ready, 2 * (i - 1) + n + 1)
                        V.tensor_tensor(x[:, n * 512:(n + 1) * 512], x[:, n * 512:(n + 1) * 512], X[:, (2, 0)[n], :],
                                        ALU.add).then_inc(x2_ready, 1)
                    dve.wait_ge(x2_ready, 2 * i)
                    if has(i):
                        dve.wait_ge(r_summed, i + 1)
                    V.tensor_tensor_reduce(out=sq[:, :], in0=x[:, :], in1=x[:, :], scale=1.0, scalar=0.0, op0=ALU.mult, op1=ALU.add,
                                           accum_out=f_ms[:, 0:1]).then_inc(f_squared, 1)
                    dve.wait_ge(f_squared, i)
                    V.tensor_scalar(f_ms[:, :], f_ms[:, :], 1.0 / D, EPS, ALU.mult, ALU.add).then_inc(f_mean, 1)

            norms_mean(0)
            for h in range(AH):
                dve.wait_ge(bias_turned, h + 1)
                V.tensor_scalar(bias8[:, h, :], S[:, h % 2, 0:BW], float(AD) ** 0.5, None, ALU.mult).then_inc(bias_set, 1)
                if h == 2:
                    dve.wait_ge(const_in, 7 * 16)
                    norms_scale(0)
            dve.wait_ge(state_in, 16)
            dve.wait_ge(zeros_set, 2)
            dve.wait_ge(bias_set, AH)
            V.memset(bias8[0:64, :, BAND + CHUNK:BAND + P], 8 * MASK).then_inc(bias_set, 1)
            V.memset(bias8[64:128, :, 0:CHUNK], 8 * MASK).then_inc(bias_set, 1)
            dve.wait_ge(bias_set, AH + 2)
            steps(dve, step)

        @block.tensor
        def _(pe):
            def mm(out, a, b, start=True, stop=True):
                return nc.tensor.matmul(out, a, b, start=start, stop=stop)

            def turn(bank, src):
                for k in range(4):
                    last = nc.tensor.transpose(X[:, bank, k * P:(k + 1) * P], src(k), ident[:, :])
                return last

            def turn_q(m):
                if sample(m):
                    pe.wait_ge(m_out, 2 * (m - 1))
                    pe.wait_ge(cache_in, 32)
                    turn(1, lambda k: qk[:, AW + k * P:AW + (k + 1) * P]).then_inc(cache_turned, 1)
                    pe.wait_ge(keys_ready, m + 1)
                pe.wait_ge(qk_ready, m + 1)
                after(pe, m_out, 2 * (m - 1))
                turn(1, lambda k: qk[:, k * P:(k + 1) * P]).then_inc(q_turned, 1)

            def turn_k(m):
                pe.wait_ge(q_padded, 2 * m + 2)
                turn(1, lambda k: qk[:, AW + k * P:AW + (k + 1) * P]).then_inc(k_turned, 1)

            def turn_ret(m):
                pe.wait_ge(rotated, m + 1)
                after(pe, x2_ready, 2 * (m - 1) - 1)
                turn(2, lambda k: rot[:, k, :]).then_inc(rq_turned, 1)
                after(pe, x2_ready, 2 * (m - 1))
                turn(0, lambda k: rot[:, RH + k, :]).then_inc(rk_turned, 1)

            def step(i, past):
                st = 1 if sample(i) else 0
                first = 0 if isinstance(i, int) and i < BT or sample(i) else (i - BT) * P
                n_keys = past + 1

                def scores(h):
                    if has(i) and h < AH:
                        W = width(i, past)
                        after(pe, p_out, AH * i + h - 1)
                        last = mm(S[:, h % 2, 0:min(W, 512)], qpad[:, h, :], keysT[:, h // 2, at(first, min(W, 512))])
                        if W > 512:
                            last = mm(S[:, h % 2, 512:W], qpad[:, h, :], keysT[:, h // 2, at(first + 512, W - 512)])
                        last.then_inc(scores_ready, 1)

                def turn_probs(h):
                    if has(i):
                        pe.wait_ge(p_ready, AH * i + h + 1)
                        for k in range(n_keys):
                            w_ = DEC if sample(i) and k == 1 else P
                            last = nc.tensor.transpose(S[0:w_, h % 2, k * P:(k + 1) * P], sc[:, h % 2, k * P:k * P + w_], ident[:, :])
                        last.then_inc(p_turned, 1)

                def values(h):
                    if has(i):
                        pe.wait_ge(p_out, AH * i + h + 1)
                        if h == 0:
                            after(pe, oa_ready, i)
                            pe.wait_ge(v_ready, i + 1)
                        for k in range(n_keys):
                            w_ = DEC if sample(i) and k == 1 else P
                            vt = k if sample(i) or isinstance(i, int) and i < BT else i - BT + k
                            last = mm(M[:, h * AD:(h + 1) * AD], pT[0:w_, h % 2, k, :], vals[0:w_, vt, h * AD:(h + 1) * AD],
                                      start=(k == 0), stop=(k == n_keys - 1))
                        last.then_inc(o_ready, 1)

                def inner_products():
                    pe.wait_ge(rq_ready, i + 1)
                    pe.wait_ge(rk_ready, i + 1)
                    for h in range(RH):
                        last = mm(X[:, 0, h * P:(h + 1) * P], rkT[:, h, :], rqT[:, h, :])
                    last.then_inc(inner_ready, 1)

                def retention():
                    pe.wait_ge(inner_scaled, i + 1)
                    pe.wait_ge(rqd_ready, i + 1)
                    pe.wait_ge(zvg_in, 16 * i + 16)
                    after(pe, state_ready, RH * i)
                    for h in range(RH):
                        mm(X[:, 0, h * RD:(h + 1) * RD], inner[:, h, :], zvg[:, h * RD:(h + 1) * RD], stop=False)
                        last = mm(X[:, 0, h * RD:(h + 1) * RD], rqdT[:, h, :], state[:, st, h, :], start=False)
                    last.then_inc(ret_ready, 1)

                def update():
                    pe.wait_ge(k_decayed, i + 1)
                    if has(i - 1):
                        pe.wait_ge(r_out, i)
                    for h in range(RH):
                        last = mm(X[:, 1, h * RD:(h + 1) * RD], rot[:, RH + h, :], zvg[:, h * RD:(h + 1) * RD])
                    last.then_inc(update_ready, 1)

                def branch(n):
                    if not has(i - 1):
                        return
                    if isinstance(i, int) and i == 1 and n % 2 == 0:
                        pe.wait_ge((w_a_in, w_r_in)[n // 2], 16)
                    if n == 0:
                        pe.wait_ge(oa_out, i)
                    elif n == 1 and has(i - 2):
                        pe.wait_ge(h2_out, 2 * (i - 2) + 1)
                    elif n == 1 and has(i):
                        pe.wait_ge(ret_out, i + 1)
                    elif n == 2:
                        pe.wait_ge(r_out, i)
                        if has(i - 2):
                            pe.wait_ge(h2_out, 2 * (i - 2) + 2)
                        elif has(i):
                            pe.wait_ge(state_ready, RH * i + RH)
                    elif n == 3:
                        pe.wait_ge(gated, 4 * (i - 1) + 1)
                    w, c, half_ = (w_a, w_r)[n // 2], n // 2, n % 2
                    for k in range(4):
                        last = mm(X[:, (2, 0, 1, 2)[n], :], tT[:, 4 * c + k, :], w[:, k, half_ * 512:(half_ + 1) * 512],
                                  start=(k == 0), stop=(k == 3))
                    last.then_inc(branch_ready, 1)

                def turn_h2(b):
                    if has(i - 2):
                        if b == 0:
                            pe.wait_ge(h2_ready, i - 1)
                            if has(i):
                                pe.wait_ge(ret_out, i + 1)
                        elif has(i):
                            pe.wait_ge(state_ready, RH * i + RH)
                        elif has(i - 1):
                            pe.wait_ge(r_out, i)
                        turn(b, lambda k: sq[:, (4 * b + k) * P:(4 * b + k + 1) * P]).then_inc(h2_turned, 1)

                def project_half(n):
                    if has(i - 1):
                        if isinstance(i, int) and i == 1 and n == 0:
                            pe.wait_ge(w_o_in, 16)
                        pe.wait_ge(m_out, 2 * (i - 1) + 2)
                        for k in range(KD):
                            last = mm(X[:, (2, 0)[n], :], tT[:, k, :], w_o[:, k, n * 512:(n + 1) * 512],
                                      start=(k == 0), stop=(k == KD - 1))
                        last.then_inc(proj_ready, 1)

                if has(i):
                    pe.wait_ge(keys_ready, i + 1 + (1 if sample(i) else 0))
                scores(0)
                scores(1)
                if has(i):
                    turn_ret(i)
                if has(i - 1):
                    pe.wait_ge(r_ready, i)
                    if has(i):
                        pe.wait_ge(q_padded, 2 * i + 2)
                    turn(1, lambda k: ro[:, k * P:(k + 1) * P]).then_inc(r_turned, 1)
                    pe.wait_ge(oa_ready, i)
                    if has(i):
                        pe.wait_ge(rq_ready, i + 1)
                    else:
                        pe.wait_ge(x2_ready, 2 * (i - 2) + 2)
                    turn(2, lambda k: oa[:, k * P:(k + 1) * P]).then_inc(oa_turned, 1)
                if has(i):
                    inner_products()
                turn_probs(0)
                if has(i):
                    retention()
                scores(2)
                turn_probs(1)
                if has(i):
                    update()
                turn_h2(0)
                branch(0)
                values(0)
                scores(3)
                for h in range(2, 5):
                    turn_probs(h)
                    if h == 2:
                        turn_h2(1)
                    branch(h - 1)
                    values(h - 1)
                    scores(h + 2)
                turn_probs(5)
                values(4)
                scores(7)
                turn_probs(6)
                values(5)
                if has(i - 1):
                    pe.wait_ge(merged, i)
                    for b in range(2):
                        turn(b, lambda k: zg[:, (4 * b + k) * P:(4 * b + k + 1) * P]).then_inc(m_turned, 1)
                turn_probs(7)
                values(6)
                project_half(0)
                if has(i + 1):
                    turn_q(i + 1)
                values(7)
                if has(i + 1):
                    turn_k(i + 1)
                project_half(1)

            pe.wait_ge(ident_in, 32)
            pe.wait_ge(bias_in, 16)
            for h in range(AH):
                after(pe, bias_set, h - 1)
                mm(S[:, h % 2, 0:512], flip[:, :], bias_rev[:, h, 0:512])
                mm(S[:, h % 2, 512:BW], flip[:, :], bias_rev[:, h, 512:BW]).then_inc(bias_turned, 1)
                if h == 5:
                    turn_q(0)
                    turn_k(0)
            pe.wait_ge(q_padded, 2)
            pe.wait_ge(bias_set, AH)
            steps(pe, step)


def route(nc, d):
    COVER = ((0, 0, 1, 16), (16, 1, 3, 8), (40, 4, 4, 4), (56, 8, 8, 1))
    assert all(any(a0 <= a < a0 + n and (a + 1) * (w + 1) > TOPK for _, a0, n, w in COVER) for a in range(TOPK))
    CANDS = 64
    GROUPS = ((0,), (1, 2), (3, 4), (5, 6), (7, 8))
    GT = 2
    GW = GT * P

    def beside(t):
        g = next(n for n, tiles in enumerate(GROUPS) if t in tiles)
        u, n = t - GROUPS[g][0], len(GROUPS[g])
        return g, u, range(HC * u // n, HC * (u + 1) // n) if g + 1 < len(GROUPS) else ()

    with Stage(nc, "rt") as s:
        wq = s.sb("wq", [P, KD, 2 * PH * PK])
        keys = s.sb("keys", [P, HC, PK])
        h2T = s.sb("h2T", [P, 2, KD, GW])
        qT = s.sb("qT", [P, 2, HC, GW])
        sc = s.sb("sc", [P, GT, HC, PK])
        ident = s.sb("ident", [P, P])
        iota16 = s.sb("iota16", [P, TOPK])
        places = s.sb("places", [P, TOPK, SLOTS], BF16)
        tv = s.sb("tv", [P, PH, 2, TOPK])
        ti = s.sb("ti", [P, PH, 2, TOPK], U32)
        tf = s.sb("tf", [P, 2, TOPK, PH], BF16)
        cand = s.sb("cand", [P, PH, CANDS])
        bv = s.sb("bv", [P, PH, TOPK])
        bi = s.sb("bi", [P, PH, TOPK], U32)
        part = s.sb("part", [P, 2, SLOTS], U32)
        place = s.sb("place", [P, 3, TOPK, PH], BF16)
        ab = s.sb("ab", [P, 2, TOPK, PH], BF16)
        row = s.sb("row", [P, 4, TOPK, PH], BF16)
        hit = s.sb("hit", [P, 2, TOPK, SLOTS], BF16)
        shift = s.sb("shift", [P, PH, TOPK])
        out = s.sb("out", [P, 3, SLOTS])
        den = s.sb("den", [P, 2, PH])
        outT = s.sb("outT", [P, 3, P])
        mark = s.sb("mark", [P, 1])
        qp = s.pb("qp", [P, 3, 512])
        sp_ = s.pb("sp", [P, 4, 512])
        tp = s.pb("tp", [P, 512])
        names = """const_in w_in0 w_in1 w_in2 w_in3 h2_in0 h2_in1 iota_set q_ready q_out s_ready s_out
            top8 found8 cut8 top16 found16 keyed cand_ready best8 bfound8 bcut8 best16 bfound16
            split placed a_done b_done hit_ready picked folded tables shifted expd summed recip out_ready out_turned outT_ready stored""".split()
        (const_in, w_in0, w_in1, w_in2, w_in3, h2_in0, h2_in1, iota_set, q_ready, q_out, s_ready, s_out,
         top8, found8, cut8, top16, found16, keyed, cand_ready, best8, bfound8, bcut8, best16, bfound16,
         split, placed, a_done, b_done, hit_ready, picked, folded, tables, shifted, expd, summed, recip, out_ready, out_turned, outT_ready, stored
         ) = [s.sem(n) for n in names]
        h2_in, w_in = (h2_in0, h2_in1), (w_in0, w_in1, w_in2, w_in3)
        block = s.block()

        @block.sync
        def _(sp):
            h2_v = d["h2T"].rearrange("(k p) t -> p k t", p=P)
            w_v = d["w_q"].rearrange("(k p) n -> p k n", p=P)
            for g, tiles in enumerate(GROUPS):
                after(sp, q_ready, HC * (g - 1))
                sp.dma_start(h2T[:, g % 2, :, 0:len(tiles) * P], h2_v[:, :, tiles[0] * P:(tiles[-1] + 1) * P]).then_inc(h2_in[g % 2], 16)
                if g == 0:
                    for c in range(4):
                        sp.dma_start(wq[:, :, c * 512:(c + 1) * 512], w_v[:, :, c * 512:(c + 1) * 512]).then_inc(w_in[c], 16)
                        if c == 0:
                            sp.dma_start(keys[:, :, :], d["keys"]).then_inc(const_in, 16)
                            sp.dma_start(ident[:, :], d["ident"]).then_inc(const_in, 16)

        @block.gpsimd
        def _(pool):
            nc.gpsimd.iota(iota16[:, :], [[1, TOPK]], base=0, channel_multiplier=0,
                           allow_small_or_imprecise_dtypes=True).then_inc(iota_set, 1)

        @block.scalar
        def _(act):
            act.sem_inc(stored, 16)

            def queries_out(g, part):
                for hc in part:
                    act.wait_ge(q_ready, HC * g + hc + 1)
                    n = len(GROUPS[g]) * P
                    nc.scalar.copy(qT[:, g % 2, hc, 0:n], qp[:, hc % 3, 0:n]).then_inc(q_out, 1)

            def exp(t):
                act.wait_ge(shifted, t + 1)
                nc.scalar.activation(shift[:, :, :], shift[:, :, :], ACT.Exp).then_inc(expd, 1)

            def store(t):
                act.wait_ge(out_turned, t + 2)
                act.wait_ge(stored, 16 * t + 16)
                nc.scalar.copy(outT[:, :, :], tp[:, 0:3 * P].rearrange("p (c t) -> p c t", c=3)).then_inc(outT_ready, 1)
                act.wait_ge(outT_ready, t + 1)
                act.dma_start(d["route"][:, :, t * P:(t + 1) * P], outT[:, :, :]).then_inc(stored, 16)

            queries_out(0, range(HC))
            for t in range(NT):
                for b in range(4):
                    act.wait_ge(s_ready, 4 * t + b + 1)
                    act.wait_ge(found16, HC * t + HC)
                    nc.scalar.copy(sc[:, t % GT, 4 * b:4 * b + 4, :].rearrange("p h k -> p (h k)"), sp_[:, b, :]).then_inc(s_out, 1)
                if t:
                    exp(t - 1)
                g, _, part = beside(t)
                queries_out(g + 1, part)
                if t:
                    store(t - 1)
            exp(NT - 1)
            store(NT - 1)
            act.wait_ge(stored, 16 * NT + 16)

        @block.vector
        def _(dve):
            V = nc.vector
            dve.sem_inc(found16, GT * HC)
            dve.wait_ge(iota_set, 1)
            V.tensor_copy(places[:, :, :], iota16[:, :].rearrange("p (a o) -> p a o", o=1).broadcast_to([P, TOPK, SLOTS])
                          ).then_inc(tables, 1)
            dve.wait_ge(tables, 1)

            def take_wait():
                V.memset(mark[:, :], 0.0)

            def tile(t, u, first=False):
                dve.wait_ge(s_out, 4 * t + 4)
                take_wait()
                for h in range(HC):
                    V.max(tv[:, h // 2, h % 2, 0:8], sc[:, u, h, :]).then_inc(top8, 1)
                if not first:
                    gates(t - 1)
                dve.wait_ge(top8, HC * t + HC)
                take_wait()
                for h in range(HC):
                    V.max_index(ti[:, h // 2, h % 2, 0:8], tv[:, h // 2, h % 2, 0:8], sc[:, u, h, :]).then_inc(found8, 1)
                dve.wait_ge(found8, HC * t + HC)
                take_wait()
                for h in range(HC):
                    V.match_replace(sc[:, u, h, :], tv[:, h // 2, h % 2, 0:8], sc[:, u, h, :], LOWEST).then_inc(cut8, 1)
                dve.wait_ge(cut8, HC * t + HC)
                take_wait()
                for h in range(HC):
                    V.max(tv[:, h // 2, h % 2, 8:16], sc[:, u, h, :]).then_inc(top16, 1)
                dve.wait_ge(top16, HC * t + HC)
                take_wait()
                for h in range(HC):
                    V.max_index(ti[:, h // 2, h % 2, 8:16], tv[:, h // 2, h % 2, 8:16], sc[:, u, h, :]).then_inc(found16, 1)
                for p0, a0, rows, w in COVER:
                    V.tensor_tensor(cand[:, :, p0:p0 + rows * w].rearrange("p h (a b) -> p h a b", a=rows),
                                    tv[:, :, 0, a0:a0 + rows].rearrange("p h (a o) -> p h a o", o=1).broadcast_to([P, PH, rows, w]),
                                    tv[:, :, 1, 0:w].rearrange("p h (o b) -> p h o b", o=1).broadcast_to([P, PH, rows, w]),
                                    ALU.add).then_inc(cand_ready, 1)
                dve.wait_ge(found16, HC * t + HC + GT * HC)
                for c in range(2):
                    V.tensor_copy(tf[:, c, :, :], ti[:, :, c, :].rearrange("p h a -> p a h")).then_inc(keyed, 1)
                dve.wait_ge(cand_ready, len(COVER) * (t + 1))
                take_wait()
                flat = lambda h: cand[:, h, :]
                for h in range(PH):
                    V.max(bv[:, h, 0:8], flat(h)).then_inc(best8, 1)
                dve.wait_ge(best8, PH * t + PH)
                take_wait()
                for h in range(PH):
                    V.max_index(bi[:, h, 0:8], bv[:, h, 0:8], flat(h)).then_inc(bfound8, 1)
                dve.wait_ge(bfound8, PH * t + PH)
                take_wait()
                for h in range(PH):
                    V.match_replace(flat(h), bv[:, h, 0:8], flat(h), LOWEST).then_inc(bcut8, 1)
                dve.wait_ge(bcut8, PH * t + PH)
                take_wait()
                for h in range(PH):
                    V.max(bv[:, h, 8:16], flat(h)).then_inc(best16, 1)
                dve.wait_ge(best16, PH * t + PH)
                take_wait()
                for h in range(PH):
                    V.max_index(bi[:, h, 8:16], bv[:, h, 8:16], flat(h)).then_inc(bfound16, 1)
                dve.wait_ge(bfound16, PH * t + PH)
                V.tensor_tensor(shift[:, :, :], bv[:, :, :], bv[:, :, 0:1].broadcast_to([P, PH, TOPK]),
                                ALU.subtract).then_inc(shifted, 1)
                bi2 = bi[:, :, :].rearrange("p h k -> p (h k)")
                V.tensor_single_scalar(part[:, 0, :], bi2, 3, ALU.logical_shift_right).then_inc(split, 1)
                V.tensor_single_scalar(part[:, 1, :], bi2, 2, ALU.logical_shift_right).then_inc(split, 1)
                V.tensor_copy(place[:, 2, :, :], bi2.rearrange("p (h k) -> p k h", h=PH)).then_inc(placed, 1)
                dve.wait_ge(split, 2 * t + 2)
                for c in range(2):
                    V.tensor_copy(place[:, c, :, :], part[:, c, :].rearrange("p (h k) -> p k h", h=PH)).then_inc(placed, 1)
                dve.wait_ge(placed, 3 * t + 3)
                V.tensor_scalar(row[:, 0, :, :], place[:, 0, :, :], -1.0, 0.0, ALU.add, ALU.max).then_inc(a_done, 1)
                dve.wait_ge(a_done, 3 * t + 1)
                V.scalar_tensor_tensor(out=row[:, 1, :, :], in0=place[:, 1, :, :], scalar=-6.0, in1=row[:, 0, :, :],
                                       op0=ALU.add, op1=ALU.max).then_inc(a_done, 1)
                dve.wait_ge(a_done, 3 * t + 2)
                V.scalar_tensor_tensor(out=ab[:, 0, :, :], in0=place[:, 2, :, :], scalar=-48.0, in1=row[:, 1, :, :],
                                       op0=ALU.add, op1=ALU.max).then_inc(a_done, 1)
                dve.wait_ge(a_done, 3 * t + 3)
                V.tensor_scalar(row[:, 2, :, :], ab[:, 0, :, :], 8.0, 8.0, ALU.mult, ALU.add).then_inc(b_done, 1)
                V.tensor_scalar(row[:, 3, :, :], ab[:, 0, :, :], 4.0, 24.0, ALU.mult, ALU.add).then_inc(b_done, 1)
                dve.wait_ge(b_done, 6 * t + 1)
                V.scalar_tensor_tensor(out=row[:, 0, :, :], in0=ab[:, 0, :, :], scalar=16.0, in1=row[:, 2, :, :],
                                       op0=ALU.mult, op1=ALU.min).then_inc(b_done, 1)
                dve.wait_ge(b_done, 6 * t + 2)
                V.scalar_tensor_tensor(out=row[:, 1, :, :], in0=ab[:, 0, :, :], scalar=48.0, in1=row[:, 3, :, :],
                                       op0=ALU.add, op1=ALU.min).then_inc(b_done, 1)
                dve.wait_ge(b_done, 6 * t + 4)
                V.tensor_tensor(row[:, 2, :, :], row[:, 0, :, :], row[:, 1, :, :], ALU.min).then_inc(b_done, 1)
                dve.wait_ge(b_done, 6 * t + 5)
                V.tensor_tensor(ab[:, 1, :, :], place[:, 2, :, :], row[:, 2, :, :], ALU.subtract).then_inc(b_done, 1)
                for c in range(2):
                    if c == 1:
                        dve.wait_ge(b_done, 6 * t + 6)
                    V.tensor_tensor(hit[:, c, :, :], places[:, :, :],
                                    ab[:, c, :, :].rearrange("p k h -> p (k h)").rearrange("p (o s) -> p o s", o=1)
                                    .broadcast_to([P, TOPK, SLOTS]), ALU.is_equal).then_inc(hit_ready, 1)
                for c in range(2):
                    dve.wait_ge(hit_ready, 2 * t + c + 1)
                    dve.wait_ge(keyed, 2 * t + c + 1)
                    h4 = hit[:, c, :, :].rearrange("p a (k h) -> p a k h", h=PH)
                    V.tensor_tensor(h4, h4, tf[:, c, :, :].rearrange("p a (o h) -> p a o h", o=1).broadcast_to([P, TOPK, TOPK, PH]),
                                    ALU.mult).then_inc(picked, 1)
                dve.wait_ge(picked, 2 * t + 2)
                V.tensor_tensor(hit[:, :, 0:8, :], hit[:, :, 0:8, :], hit[:, :, 8:16, :], ALU.add).then_inc(folded, 1)
                dve.wait_ge(folded, 3 * t + 1)
                V.tensor_tensor(hit[:, :, 0:4, :], hit[:, :, 0:4, :], hit[:, :, 4:8, :], ALU.add).then_inc(folded, 1)
                dve.wait_ge(folded, 3 * t + 2)
                V.tensor_tensor(hit[:, :, 0:2, :], hit[:, :, 0:2, :], hit[:, :, 2:4, :], ALU.add).then_inc(folded, 1)
                dve.wait_ge(out_turned, t + 1)
                dve.wait_ge(folded, 3 * t + 3)
                V.tensor_tensor(out[:, 0:2, :], hit[:, :, 0, :], hit[:, :, 1, :], ALU.add).then_inc(out_ready, 1)

            def gates(t):
                dve.wait_ge(expd, t + 1)
                V.tensor_reduce(den[:, 0, :], shift[:, :, :], AX.X, ALU.add).then_inc(summed, 1)
                dve.wait_ge(summed, t + 1)
                V.reciprocal(den[:, 1, :], den[:, 0, :]).then_inc(recip, 1)
                dve.wait_ge(recip, t + 1)
                V.tensor_tensor(out[:, 2, :].rearrange("p (k h) -> p h k", h=PH), shift[:, :, :],
                                den[:, 1, :].rearrange("p (h o) -> p h o", o=1).broadcast_to([P, PH, TOPK]), ALU.mult).then_inc(out_ready, 1)

            tile(0, 0, first=True)
            with dve.Fori(0, NT // 2) as pair:
                tile(2 * pair + 1, 1)
                tile(2 * pair + 2, 0)
            gates(NT - 1)

        @block.tensor
        def _(pe):
            pe.sem_inc(out_turned, 1)

            def queries(g, part):
                for hc in part:
                    if hc == 0:
                        pe.wait_ge(h2_in[g % 2], 16 * (g // 2) + 16)
                    if g == 0 and hc % 4 == 0:
                        pe.wait_ge(w_in[hc // 4], 16)
                    after(pe, q_out, HC * g + hc - (2 if hc else 0))
                    for k in range(KD):
                        n = len(GROUPS[g]) * P
                        last = nc.tensor.matmul(qp[:, hc % 3, 0:n], wq[:, k, hc * PK:(hc + 1) * PK], h2T[:, g % 2, k, 0:n],
                                                start=(k == 0), stop=(k == KD - 1))
                    last.then_inc(q_ready, 1)

            def scores(t):
                g, u, _ = beside(t)
                for hc in range(HC):
                    if u == 0:
                        pe.wait_ge(q_out, HC * g + hc + 1)
                    if hc % 4 == 0:
                        after(pe, s_out, 4 * t + hc // 4 - 3)
                    last = nc.tensor.matmul(sp_[:, hc // 4, (hc % 4) * PK:(hc % 4 + 1) * PK], qT[:, g % 2, hc, u * P:(u + 1) * P],
                                            keys[:, hc, :], start=True, stop=True)
                    if hc % 4 == 3:
                        last.then_inc(s_ready, 1)

            def turn(t):
                pe.wait_ge(out_ready, 2 * t + 2)
                after(pe, outT_ready, t)
                for c in range(3):
                    last = nc.tensor.transpose(tp[:, c * P:(c + 1) * P], out[:, c, :], ident[:, :])
                last.then_inc(out_turned, 1)

            queries(0, range(HC))
            pe.wait_ge(const_in, 32)
            for t in range(NT):
                scores(t)
                g, _, part = beside(t)
                queries(g + 1, part)
                if t:
                    turn(t - 1)
            turn(NT - 1)


def spread(nc, d):
    B = 8
    BANKS = 4
    with Stage(nc, "spr") as s:
        rt = s.sb("rt", [P, 3, TPAD])
        place = s.sb("place", [P, 2, TPAD], BF16)
        iota = s.sb("iota", [P, P])
        iotas = s.sb("iotas", [P, P, B], BF16)
        hot_i = s.sb("hot_i", [P, 2, P, B], BF16)
        hot_j = s.sb("hot_j", [P, 2, P, B], BF16)
        rows = s.sb("rows", [P, 2, B, P])
        cols = s.sb("cols", [P, 2, B, P])
        g = s.sb("g", [P, 2, PK, P])
        gp = s.pb("gp", [P, BANKS, B * P])
        rt_in, iota_set, tables = s.sem("rt_in"), s.sem("iota_set"), s.sem("tables")
        hot_i_ready, hot_j_ready = s.sem("hot_i_ready"), s.sem("hot_j_ready")
        rows_ready, cols_ready = s.sem("rows_ready"), s.sem("cols_ready")
        spread_ready, g_out = s.sem("spread_ready"), s.sem("g_out")
        g_stored = [s.sem("g_stored0"), s.sem("g_stored1")]
        FREE = 2
        block = s.block()

        def tiles(eng, body):
            with eng.Fori(0, NP // 2) as pair:
                body(2 * pair, 0, pair, P)
                body(2 * pair + 1, 1, pair, P)
            body(NP, 0, NP // 2, DEC)

        def steps(t, n):
            return enumerate([t * (P // B) + q for q in range(n // B)])

        @block.sync
        def _(sp):
            sp.dma_start(rt[:, :, :], d["route"]).then_inc(rt_in, 16)
            sp.sem_inc(g_stored[0], 16)
            sp.sem_inc(g_stored[1], 16)

            def body(t, slot, pair, n):
                sp.wait_ge(g_out, t * (P // B) + n // B + BANKS)
                sp.dma_start(d["gates"].rearrange("j i t -> i j t")[:, :, at(t * P, n)],
                             g[:, slot, :, 0:n]).then_inc(g_stored[slot], 16)

            tiles(sp, body)
            sp.wait_ge(g_stored[0], 16 * (NP // 2 + 1) + 16)
            sp.wait_ge(g_stored[1], 16 * (NP // 2) + 16)

        @block.gpsimd
        def _(pool):
            nc.gpsimd.iota(iota[:, :], [[1, P]], base=0, channel_multiplier=0,
                           allow_small_or_imprecise_dtypes=True).then_inc(iota_set, 1)

        @block.vector
        def _(dve):
            dve.wait_ge(iota_set, 1)
            nc.vector.tensor_copy(iotas[:, :, :], iota[:, :].rearrange("p (k o) -> p k o", o=1).broadcast_to([P, P, B])
                                  ).then_inc(tables, 1)
            dve.wait_ge(rt_in, 16)
            nc.vector.tensor_copy(place[:, :, :], rt[:, 0:2, :]).then_inc(tables, 1)
            dve.wait_ge(tables, 2)

            def body(t, slot, pair, n):
                for q, step in steps(t, n):
                    tok = t * P + q * B
                    number = lambda c: place[:, c, at(tok, B)].rearrange("p (o b) -> p o b", o=1).broadcast_to([P, P, B])
                    nc.vector.tensor_tensor(hot_j[:, q % 2, :, :], iotas[:, :, :], number(1), ALU.is_equal).then_inc(hot_j_ready, 1)
                    dve.wait_ge(rows_ready, step + 1)
                    nc.vector.tensor_tensor(hot_i[:, q % 2, :, :], iotas[:, :, :], number(0), ALU.is_equal).then_inc(hot_i_ready, 1)
                    dve.wait_ge(hot_j_ready, step + 1)
                    dve.wait_ge(spread_ready, step + 1)
                    nc.vector.tensor_tensor(cols[:, q % 2, :, :], hot_j[:, q % 2, :, :].rearrange("p k b -> p b k"),
                                            rt[:, 2, at(tok, B)].rearrange("p (b o) -> p b o", o=1).broadcast_to([P, B, P]),
                                            ALU.mult).then_inc(cols_ready, 1)

            tiles(dve, body)

        @block.tensor
        def _(pe):
            pe.sem_inc(spread_ready, FREE)

            def body(t, slot, pair, n):
                for q, step in steps(t, n):
                    pe.wait_ge(rows_ready, step + 1 + FREE)
                    pe.wait_ge(cols_ready, step + 1)
                    pe.wait_ge(g_out, step + 1)
                    for b in range(B):
                        last = nc.tensor.matmul(gp[:, q % BANKS, b * P:(b + 1) * P], rows[:, q % 2, b, :], cols[:, q % 2, b, :],
                                                start=True, stop=True)
                    last.then_inc(spread_ready, 1)

            tiles(pe, body)

        @block.scalar
        def _(act):
            act.sem_inc(rows_ready, FREE)
            act.sem_inc(g_out, BANKS)

            def body(t, slot, pair, n):
                act.wait_ge(g_stored[slot], 16 * pair + 16)
                def copy_rows(q, step):
                    act.wait_ge(hot_i_ready, step + 1)
                    act.wait_ge(spread_ready, step + 1)
                    nc.scalar.copy(rows[:, q % 2, :, :], hot_i[:, q % 2, :, :].rearrange("p k b -> p b k")).then_inc(rows_ready, 1)

                def gates_out(q, step):
                    act.wait_ge(spread_ready, step + 1 + FREE)
                    nc.scalar.copy(g[:, slot, :, at(q * B, B)],
                                   gp[:, q % BANKS, :].rearrange("p (t j) -> p j t", t=B)).then_inc(g_out, 1)

                for q, step in steps(t, n):
                    copy_rows(q, step)
                    if q:
                        gates_out(q - 1, step - 1)
                gates_out(q, step)

            tiles(act, body)


TG = [(0, 384), (384, 384), (768, 320)]


def experts(nc, d):
    NG = len(TG)
    NV = KD * NG
    NJ = PK
    with Stage(nc, "exp") as s:
        h2 = [s.sb("h2_hi", [P, KD, TOK], F32R), s.sb("h2_lo", [P, KD, TOK], F32R)]
        acc = s.sb("acc", [P, KD, TOK])
        u_raw = s.sb("u_raw", [P, 2, KD * P])
        v_raw = s.sb("v_raw", [P, 2, D])
        u = [s.sb("u_hi", [P, 2, KD * P], F32R), s.sb("u_lo", [P, 2, KD * P], F32R)]
        v = [s.sb("v_hi", [P, 2, D], F32R), s.sb("v_lo", [P, 2, D], F32R)]
        gt = s.sb("gt", [P, 2, TOK])
        ge = s.sb("ge", [P, NG, 384])
        pr = s.sb("pr", [P, NG, 384])
        am = [s.sb("am_hi", [P, TOK], F32R), s.sb("am_lo", [P, TOK], F32R)]
        ident = s.sb("ident", [P, P])
        y = lambda t: (u_raw, v_raw)[t % 4 // 2][:, t % 2, :]
        up = s.pb("up", [P, NG, 512])
        vp = s.pb("vp", [P, 4, 512])
        names = """h2_in0 h2_in1 h2_in2 h2_in3 h2_hi_ready h2_lo_ready zeroed ident_in u_in0 u_in1 v_in0 v_in1 g_in0 g_in1
            u_hi_ready u_lo_ready v_hi_ready v_lo_ready up_ready gelu_ready prod_ready am_hi_ready am_lo_ready
            down_ready added y_turned y_ready""".split()
        (h2_in0, h2_in1, h2_in2, h2_in3, h2_hi_ready, h2_lo_ready, zeroed, ident_in, u_in0, u_in1, v_in0, v_in1, g_in0, g_in1,
         u_hi_ready, u_lo_ready, v_hi_ready, v_lo_ready, up_ready, gelu_ready, prod_ready, am_hi_ready, am_lo_ready,
         down_ready, added, y_turned, y_ready) = [s.sem(n) for n in names]
        u_in, v_in, g_in = (u_in0, u_in1), (v_in0, v_in1), (g_in0, g_in1)
        h2_in = (h2_in0, h2_in1, h2_in2, h2_in3)
        x2_in, y_stored = [[s.sem(f"{n}{slot}") for slot in range(4)] for n in ("x2_in", "y_stored")]
        LO0, PROD0, GELU0, AMH0, DOWN0, ADD0 = 2, 2 * NG, NG, NG, NV, 4
        block = s.block()

        @block.sync
        def _(sp):
            sp.dma_start(ident[:, :], d["ident"]).then_inc(ident_in, 16)

            def load(j, slot):
                sp.wait_ge(u_lo_ready, j + 1)
                sp.dma_start(u_raw[:, slot, :], d["u"][at(j, 1), :, :].rearrange("o p n -> p (o n)")).then_inc(u_in[slot], 16)
                sp.wait_ge(v_lo_ready, j + 1)
                sp.dma_start(v_raw[:, slot, :], d["v"].rearrange("(i j) e -> j i e", j=PK)[at(j, 1), :, :]
                             .rearrange("o i e -> i (o e)")).then_inc(v_in[slot], 16)
                sp.wait_ge(prod_ready, NG * j + NG)
                sp.dma_start(gt[:, slot, :], d["gates"][at(j, 1), :, :].rearrange("o i t -> i (o t)")).then_inc(g_in[slot], 16)

            with sp.Fori(0, NJ // 2) as pair:
                load(2 * pair, 0)
                load(2 * pair + 1, 1)
            sp.wait_ge(u_lo_ready, NJ + LO0)
            sp.wait_ge(v_lo_ready, NJ + LO0)
            rows = lambda t: min(P, TOK - t * P)

            def load_x2(t):
                after(sp, y_stored[t % 4], 16 * (t // 4))
                sp.dma_start(y(t)[0:rows(t), :], d["x2"][t * P:t * P + rows(t), :]).then_inc(x2_in[t % 4], 16)

            for t in range(4):
                load_x2(t)
            for t in range(NT):
                sp.wait_ge(y_ready, 2 * t + 2)
                sp.dma_start(d["yp"][t * P:(t + 1) * P, :] if t < NP else d["ys"][:, :], y(t)[0:rows(t), :]
                             ).then_inc(y_stored[t % 4], 16)
                if 4 <= t + 2 < NT:
                    load_x2(t + 2)
            for slot in range(4):
                sp.wait_ge(y_stored[slot], 16 * len(range(slot, NT, 4)))

        @block.gpsimd
        def _(pool):
            pool.sem_inc(u_lo_ready, LO0)
            pool.sem_inc(v_lo_ready, LO0)

            def split_u(j, slot):
                pool.wait_ge(u_hi_ready, j + 1)
                nc.gpsimd.tensor_tensor(u[1][:, slot, :], u_raw[:, slot, :], u[0][:, slot, :].bitcast(F32),
                                        ALU.subtract).then_inc(u_lo_ready, 1)

            def split_v(j, slot):
                pool.wait_ge(v_hi_ready, j + 1)
                nc.gpsimd.tensor_tensor(v[1][:, slot, :], v_raw[:, slot, :], v[0][:, slot, :].bitcast(F32),
                                        ALU.subtract).then_inc(v_lo_ready, 1)

            with pool.Fori(0, NJ // 2) as pair:
                for o in range(2):
                    split_u(2 * pair + o, o)
                    split_v(2 * pair + o, o)

        @block.scalar
        def _(act):
            act.sem_inc(gelu_ready, GELU0)
            act.sem_inc(am_hi_ready, AMH0)
            h2_v = d["h2T"].rearrange("(k p) t -> p k t", p=P)
            for k in range(0, KD, 2):
                act.dma_start(acc[:, k:k + 2, :], h2_v[:, k:k + 2, 0:TOK]).then_inc(h2_in[k // 2], 16)
            for k in range(KD):
                act.wait_ge(h2_in[k // 2], 16)
                nc.scalar.copy(h2[0][:, k, :], acc[:, k, :]).then_inc(h2_hi_ready, 1)

            def high_u(j, slot, half):
                act.wait_ge(u_in[slot], 16 * half + 16)
                after(act, up_ready, NG * j - NG)
                nc.scalar.copy(u[0][:, slot, :], u_raw[:, slot, :]).then_inc(u_hi_ready, 1)

            def high_v(j, slot, half):
                act.wait_ge(v_in[slot], 16 * half + 16)
                after(act, down_ready, NV * j)
                nc.scalar.copy(v[0][:, slot, :], v_raw[:, slot, :]).then_inc(v_hi_ready, 1)

            def gelu(j, g):
                w = TG[g][1]
                act.wait_ge(up_ready, NG * j + g + 1)
                after(act, prod_ready, NG * j + g + 1 + PROD0 - NG)
                nc.scalar.activation(ge[:, g, 0:w], up[:, g, 0:w], ACT.Gelu).then_inc(gelu_ready, 1)

            def high_am(j, g):
                t0, w = TG[g]
                act.wait_ge(prod_ready, NG * j + g + 1 + PROD0)
                act.wait_ge(down_ready, NV * j + KD * (g + 1))
                nc.scalar.copy(am[0][:, t0:t0 + w], pr[:, g, 0:w]).then_inc(am_hi_ready, 1)

            def step(j, slot, half, next_u=True):
                gelu(j - 1, 2)
                high_am(j - 1, 2)
                if next_u:
                    high_u(j + 1, 1 - slot, half + slot)
                gelu(j, 0)
                high_am(j, 0)
                high_v(j, slot, half)
                gelu(j, 1)
                high_am(j, 1)

            high_u(0, 0, 0)
            high_u(1, 1, 0)
            gelu(0, 0)
            high_am(0, 0)
            high_v(0, 0, 0)
            gelu(0, 1)
            high_am(0, 1)
            with act.Fori(0, NJ // 2 - 1) as pair:
                step(2 * pair + 1, 1, pair)
                step(2 * pair + 2, 0, pair + 1)
            step(NJ - 1, 1, NJ // 2 - 1, next_u=False)
            gelu(NJ - 1, 2)
            high_am(NJ - 1, 2)

        @block.vector
        def _(dve):
            V = nc.vector
            dve.sem_inc(added, ADD0)
            dve.sem_inc(prod_ready, PROD0)
            for k in range(KD):
                dve.wait_ge(h2_hi_ready, k + 1)
                V.tensor_tensor(h2[1][:, k, :], acc[:, k, :], h2[0][:, k, :].bitcast(F32), ALU.subtract).then_inc(h2_lo_ready, 1)
            dve.wait_ge(h2_lo_ready, KD)
            V.memset(acc[:, :, :], 0.0).then_inc(zeroed, 1)
            dve.wait_ge(zeroed, 1)

            def product(j, g, slot, half):
                t0, w = TG[g]
                if g == 0:
                    dve.wait_ge(g_in[slot], 16 * half + 16)
                dve.wait_ge(gelu_ready, NG * j + g + 1 + GELU0)
                dve.wait_ge(am_hi_ready, NG * j + g + 1)
                V.tensor_tensor(pr[:, g, 0:w], ge[:, g, 0:w], gt[:, slot, t0:t0 + w], ALU.mult).then_inc(prod_ready, 1)

            def low_am(j, g):
                t0, w = TG[g]
                dve.wait_ge(am_hi_ready, NG * j + g + 1 + AMH0)
                V.tensor_tensor(am[1][:, t0:t0 + w], pr[:, g, 0:w], am[0][:, t0:t0 + w].bitcast(F32), ALU.subtract
                                ).then_inc(am_lo_ready, 1)

            def add(j, g, chunks):
                t0, w = TG[g]
                for k in chunks:
                    m = KD * g + k
                    dve.wait_ge(down_ready, NV * j + m + 1)
                    V.tensor_tensor(acc[:, k, t0:t0 + w], acc[:, k, t0:t0 + w], vp[:, m % 4, 0:w], ALU.add).then_inc(added, 1)

            def step(j, slot, half, half_before, up=True):
                for g in range(NG):
                    add(j, g, (0, 1))
                    if g == 0:
                        product(j - 1, 2, 1 - slot, half_before)
                    elif up:
                        product(j, g - 1, slot, half)
                    add(j, g, (2, 3))
                    if g == 0:
                        low_am(j - 1, 2)
                    elif up:
                        low_am(j, g - 1)
                    add(j, g, (4, 5, 6, 7))

            for g in range(2):
                product(0, g, 0, 0)
                low_am(0, g)
            with dve.Fori(0, NJ // 2 - 1) as pair:
                step(2 * pair + 1, 1, pair, pair)
                step(2 * pair + 2, 0, pair + 1, pair)
            step(NJ - 1, 1, NJ // 2 - 1, NJ // 2 - 1)
            step(NJ, 0, 0, NJ // 2 - 1, up=False)
            for t in range(NT):
                n = min(P, TOK - t * P)
                dve.wait_ge(x2_in[t % 4], 16 * (t // 4) + 16)
                for c in range(2):
                    dve.wait_ge(y_turned, 2 * t + c + 1)
                    V.tensor_tensor(y(t)[0:n, c * 512:(c + 1) * 512], y(t)[0:n, c * 512:(c + 1) * 512],
                                    vp[0:n, 2 * (t % 2) + c, :], ALU.add).then_inc(y_ready, 1)

        @block.tensor
        def _(pe):
            pe.sem_inc(down_ready, DOWN0)
            pe.wait_ge(ident_in, 16)
            passes = ((0, 0), (0, 1), (1, 0))

            def step(j, slot, up_=True, down=True):
                if up_:
                    pe.wait_ge(u_lo_ready, j + 1 + LO0)
                if down:
                    pe.wait_ge(v_lo_ready, j + LO0)
                for g, (t0, w) in enumerate(TG):
                    if up_:
                        pe.wait_ge(gelu_ready, NG * j + g + 1)
                    if down:
                        pe.wait_ge(am_lo_ready, NG * (j - 1) + g + 1)
                    for k in range(KD):
                        if up_:
                            if isinstance(j, int) and j == 0 and g == 0:
                                pe.wait_ge(h2_lo_ready, k + 1)
                            for n, (a, b) in enumerate(passes):
                                last = nc.tensor.matmul(up[:, g, 0:w], u[a][:, slot, k * P:(k + 1) * P], h2[b][:, k, t0:t0 + w],
                                                        start=(k == 0 and n == 0), stop=(k == KD - 1 and n == 2))
                            if k == KD - 1:
                                last.then_inc(up_ready, 1)
                        if down:
                            m = KD * g + k
                            pe.wait_ge(added, NV * (j - 1) + m + 1)
                            for n, (a, b) in enumerate(passes):
                                last = nc.tensor.matmul(vp[:, m % 4, 0:w], v[a][:, 1 - slot, k * P:(k + 1) * P],
                                                        am[b][:, t0:t0 + w], start=(n == 0), stop=(n == 2))
                            last.then_inc(down_ready, 1)

            step(0, 0, down=False)
            with pe.Fori(0, NJ // 2 - 1) as pair:
                step(2 * pair + 1, 1)
                step(2 * pair + 2, 0)
            step(NJ - 1, 1)
            step(NJ, 0, up_=False)
            pe.wait_ge(added, NV * NJ + ADD0)
            for t in range(NT):
                n = min(P, TOK - t * P)
                after(pe, y_ready, 2 * (t - 2) + 2)
                for c in range(2):
                    for k in range(4):
                        last = nc.tensor.transpose(vp[0:n, 2 * (t % 2) + c, k * P:(k + 1) * P],
                                                   acc[:, 4 * c + k, t * P:t * P + n], ident[:, :])
                    last.then_inc(y_turned, 1)


def consts():
    f = np.float32
    half = RD // 2
    pos = np.concatenate([np.arange(SEQ), PAST + np.arange(DEC), np.zeros(TPAD - TOK)]).astype(f)
    inv = f(10000.0) ** (-np.arange(half, dtype=f) / f(half))
    ang = pos[:, None] * inv[None, :]
    g = np.array([1.0 - 2.0 ** (-5.0 - h) for h in range(RH)])
    m, l = np.arange(P)[:, None], np.arange(P)[None, :]
    decay = np.where((l >= m)[:, None, :], g[None, :, None] ** np.maximum(l - m, 0)[:, None, :], 0.0)
    q_dec = np.broadcast_to(g[None, :, None] ** (np.arange(P) + 1.0)[None, None, :], (P, RH, P))
    j = np.arange(P)[:, None]
    k_dec = np.stack([g ** (P - 1.0 - j) * KSCALE,
                      np.where(j < DEC, g ** np.maximum(DEC - 1.0 - j, 0), 0.0) * KSCALE], axis=1)
    return {"ident": np.eye(P, dtype=f), "flip": np.eye(P, dtype=f)[::-1], "cs": np.stack([np.cos(ang), np.sin(ang)], axis=1),
            "decay": decay.astype(f), "q_dec": q_dec.astype(f), "k_dec": k_dec.astype(f)}


def layout(a):
    rel = np.pad(a["attn_rel_bias"][0], ((0, 0), (BAND + P - 1 - CLIP, BAND + P - 1 - CLIP)), mode="edge")[:, ::-1]
    rel = rel[:, :P - 1 + BAND + P]
    u = a["peer_expert_u"][0].reshape(PK, PK, KD, P)
    return {
        "x": np.concatenate([a["x_prompt"][0], a["x_sample"][0], np.zeros((TPAD - TOK, D), np.float32)]),
        "ck": a["cache_attn_k"][0, 0].reshape(P, AW), "cv": a["cache_attn_v"][0, 0].reshape(P, AW),
        "state": a["state_retention"][0, 0], "mix_g": a["mix_norm_g"][0], "w_in": a["w_in"][0],
        "q_g": a["attn_q_norm_g"][0], "k_g": a["attn_k_norm_g"][0], "rel": rel,
        "r_g": a["ret_out_norm_g"][0].reshape(RW), "w_a": a["w_branch_attn"][0], "w_r": a["w_branch_ret"][0],
        "w_o": a["w_out"][0], "f_g": a["ffn_norm_g"][0], "w_q": a["peer_w_query"][0],
        "keys": a["peer_sub_keys"][0].reshape(HC, PK, P).transpose(2, 0, 1),
        "u": u.transpose(1, 3, 2, 0).reshape(PK, P, KD * PK),
        "v": a["peer_expert_v"][0],
    }


def program(nc, d):
    for name, shape in (("z", (TPAD, ZW)), ("x2", (TPAD, D)), ("h2T", (D, TPAD)), ("route", (P, 3, TPAD)),
                        ("gates", (PK, PK, TOK))):
        d[name] = nc.dram_tensor(f"scratch_{name}", shape, F32, kind="Internal").ap()
    project(nc, d)
    mix(nc, d)
    route(nc, d)
    spread(nc, d)
    experts(nc, d)


OUTPUTS = {"yp": ((SEQ, D), (1, SEQ, D)), "ys": ((DEC, D), (1, DEC, D)),
           "nkp": ((BAND, AW), (1, 1, BAND, AH, AD)), "nvp": ((BAND, AW), (1, 1, BAND, AH, AD)),
           "nsp": ((RH, RD, RD), (1, 1, RH, RD, RD)),
           "nks": ((DEC, AW), (1, 1, DEC, AH, AD)), "nvs": ((DEC, AW), (1, 1, DEC, AH, AD)),
           "nss": ((RH, RD, RD), (1, 1, RH, RD, RD))}


def kernel(**inputs):
    import concourse.bacc as bacc
    from concourse.bass_utils import run_bass_kernel_spmd

    nc = bacc.Bacc("TRN2", target_bir_lowering=False, num_devices=1)
    arrays, d = {}, {}
    for name, a in {**consts(), **layout({k: np.asarray(v) for k, v in inputs.items()})}.items():
        arrays[f"in_{name}"] = np.ascontiguousarray(a)
        d[name] = nc.dram_tensor(f"in_{name}", a.shape, mybir.dt.from_np(a.dtype), kind="ExternalInput").ap()
    for name, (shape, _) in OUTPUTS.items():
        d[name] = nc.dram_tensor(f"out_{name}", shape, F32, kind="ExternalOutput").ap()
    program(nc, d)
    r = run_bass_kernel_spmd(nc, [arrays], core_ids=[0])
    return tuple(r.results[0][f"out_{name}"].reshape(shape) for name, (_, shape) in OUTPUTS.items())
```
